# Optimizing a Trainium2 kernel written in Bass

```python
import math
import jax, jax.numpy as jnp
from jax import lax
import numpy as np

D_MODEL = 1024
BATCH = 1
SEQ = 256
DEPTH = 1

HEAD_DIM = 64
RWKV_HEADS = 8
RWKV_WIDTH = RWKV_HEADS * HEAD_DIM
ATT_HEADS = 8
ATT_WIDTH = ATT_HEADS * HEAD_DIM
IDX_HEADS = 8
IDX_DIM = 64
DECAY_RANK = 64
AAA_RANK = 64
GATE_RANK = 128
MAX_TOPK = 256
Q_BLOCK = 128
ROPE_THETA = 10000.0
D_FF = ((8 * D_MODEL // 3 + 255) // 256) * 256
NORM_EPS = 1e-6
LNX_EPS = 64e-5

RWKV_COLS = 3 * RWKV_WIDTH + DECAY_RANK + AAA_RANK + GATE_RANK
ATT_COLS = 3 * ATT_WIDTH
IDX_COLS = IDX_HEADS * IDX_DIM + IDX_DIM + IDX_HEADS
GATE_COLS = 2 * D_MODEL
IN_COLS = RWKV_COLS + ATT_COLS + IDX_COLS + GATE_COLS


def rmsnorm(x, g):
    xf = x.astype(jnp.float32)
    y = xf * lax.rsqrt(jnp.mean(xf * xf, axis=-1, keepdims=True) + NORM_EPS)
    return (y * g.astype(jnp.float32)).astype(x.dtype)

def rope(t):
    S, D = t.shape[1], t.shape[-1]
    half = D // 2
    inv = 1.0 / (ROPE_THETA ** (jnp.arange(half, dtype=jnp.float32) * 2.0 / D))
    ang = jnp.arange(S, dtype=jnp.float32)[:, None] * inv[None, :]
    cos = jnp.cos(ang)[None, :, None, :]
    sin = jnp.sin(ang)[None, :, None, :]
    tf = t.astype(jnp.float32)
    t1, t2 = tf[..., :half], tf[..., half:]
    return jnp.concatenate([t1 * cos - t2 * sin, t1 * sin + t2 * cos], axis=-1).astype(t.dtype)

def token_shift(p, mu):
    prev = jnp.pad(p, ((0, 0), (1, 0), (0, 0)))[:, :-1]
    return p + (prev - p) * mu

def rwkv7_mix(p, w_decay_up, w0, a_up, a0, g_up, k_k, k_a, r_k, lnx_g, lnx_b):
    B, S, _ = p.shape
    H, N = RWKV_HEADS, HEAD_DIM
    c = np.cumsum([RWKV_WIDTH, RWKV_WIDTH, RWKV_WIDTH, DECAY_RANK, AAA_RANK])
    r, k, v, wd, ad, gd = jnp.split(p, c, axis=-1)
    w = -jax.nn.softplus(-(w0 + jnp.tanh(wd) @ w_decay_up)) - 0.5
    a = jax.nn.sigmoid(a0 + ad @ a_up)
    g = jax.nn.sigmoid(gd) @ g_up
    kk = (k * k_k).reshape(B, S, H, N).astype(jnp.float32)
    kk = kk / jnp.maximum(jnp.linalg.norm(kk, axis=-1, keepdims=True), 1e-12)
    k = k * (1.0 + (a - 1.0) * k_a)
    heads = lambda t: t.reshape(B, S, H, N).astype(jnp.float32)
    r_h, k_h, v_h, a_h = heads(r), heads(k), heads(v), heads(a)
    decay = jnp.exp(-jnp.exp(heads(w)))
    tm = lambda t: jnp.moveaxis(t, 1, 0)

    def step(state, inp):
        r_t, d_t, k_t, v_t, kk_t, a_t = inp
        sa = jnp.einsum('bhij,bhj->bhi', state, -kk_t)
        state = (state * d_t[:, :, None, :]
                 + sa[..., None] * (kk_t * a_t)[:, :, None, :]
                 + v_t[..., None] * k_t[:, :, None, :])
        y_t = jnp.einsum('bhij,bhj->bhi', state, r_t)
        return state, y_t

    state0 = jnp.zeros((B, H, N, N), jnp.float32)
    _, y = lax.scan(step, state0, (tm(r_h), tm(decay), tm(k_h), tm(v_h), tm(kk), tm(a_h)))
    y = jnp.moveaxis(y, 0, 1)
    mean = jnp.mean(y, axis=-1, keepdims=True)
    var = jnp.mean(jnp.square(y - mean), axis=-1, keepdims=True)
    y = (y - mean) * lax.rsqrt(var + LNX_EPS)
    y = y * lnx_g.reshape(H, N) + lnx_b.reshape(H, N)
    bonus = jnp.sum(r_h * k_h * r_k.astype(jnp.float32), axis=-1, keepdims=True) * v_h
    y = (y + bonus).reshape(B, S, RWKV_WIDTH).astype(p.dtype)
    return y * g

def dsa_attention(q, k, v, q_idx, k_idx, w_idx):
    B, S, H, Dh = q.shape
    topk = min(MAX_TOPK, S // 4)
    nb = S // Q_BLOCK
    blk = lambda t: jnp.moveaxis(t.reshape((B, nb, Q_BLOCK) + t.shape[2:]), 1, 0)
    key_pos = jnp.arange(S)
    idx_scale = IDX_DIM ** -0.5 * IDX_HEADS ** -0.5

    def one_block(args):
        qb, qib, wib, bi = args
        t = bi * Q_BLOCK + jnp.arange(Q_BLOCK)
        sc = jax.nn.relu(jnp.einsum('bqhd,bsd->bqhs', qib, k_idx).astype(jnp.float32))
        score = jnp.einsum('bqhs,bqh->bqs', sc, wib.astype(jnp.float32)) * idx_scale
        causal = key_pos[None, None, :] <= t[None, :, None]
        score = jnp.where(causal, score, -jnp.inf)
        _, sel = lax.top_k(score, topk)
        valid = sel <= t[None, :, None]
        kg = jax.vmap(lambda kb, ib: kb[ib])(k, sel)
        vg = jax.vmap(lambda vb, ib: vb[ib])(v, sel)
        logits = jnp.einsum('bqhd,bqkhd->bqhk', qb, kg).astype(jnp.float32) * Dh ** -0.5
        logits = jnp.where(valid[:, :, None, :], logits, -jnp.inf)
        prob = jax.nn.softmax(logits, axis=-1).astype(vg.dtype)
        return jnp.einsum('bqhk,bqkhd->bqhd', prob, vg)

    out = lax.map(one_block, (blk(q), blk(q_idx), blk(w_idx), jnp.arange(nb)))
    return jnp.moveaxis(out, 0, 1).reshape(B, S, H * Dh)

def first_inputs(seed: int = 0) -> dict:
    key = jax.random.key(seed)
    ks = jax.random.split(key, 24)
    nrm = lambda k, shape, s: jax.random.normal(k, shape, jnp.float32) * s
    return {
        "x": jax.random.normal(ks[0], (BATCH, SEQ, D_MODEL), jnp.float32),
        "norm1_g": 1.0 + nrm(ks[1], (D_MODEL,), 0.05),
        "w_in": nrm(ks[2], (D_MODEL, IN_COLS), D_MODEL ** -0.5),
        "tshift_mu": jax.random.uniform(ks[3], (RWKV_COLS,), jnp.float32),
        "w_decay_up": nrm(ks[4], (DECAY_RANK, RWKV_WIDTH), 0.5 * DECAY_RANK ** -0.5),
        "w0": nrm(ks[5], (RWKV_WIDTH,), 0.5),
        "a_up": nrm(ks[6], (AAA_RANK, RWKV_WIDTH), 0.5 * AAA_RANK ** -0.5),
        "a0": nrm(ks[7], (RWKV_WIDTH,), 0.5),
        "g_up": nrm(ks[8], (GATE_RANK, RWKV_WIDTH), GATE_RANK ** -0.5),
        "k_k": 0.85 + nrm(ks[9], (RWKV_WIDTH,), 0.05),
        "k_a": 1.0 + nrm(ks[10], (RWKV_WIDTH,), 0.05),
        "r_k": nrm(ks[11], (RWKV_HEADS, HEAD_DIM), 0.1),
        "lnx_g": 1.0 + nrm(ks[12], (RWKV_WIDTH,), 0.05),
        "lnx_b": nrm(ks[13], (RWKV_WIDTH,), 0.01),
        "w_o_rwkv": nrm(ks[14], (RWKV_WIDTH, D_MODEL), RWKV_WIDTH ** -0.5),
        "w_o_att": nrm(ks[15], (ATT_WIDTH, D_MODEL), ATT_WIDTH ** -0.5),
        "w_out": nrm(ks[16], (D_MODEL, D_MODEL), D_MODEL ** -0.5),
        "norm2_g": 1.0 + nrm(ks[17], (D_MODEL,), 0.05),
        "w_ffn_in": nrm(ks[18], (D_MODEL, 2 * D_FF), D_MODEL ** -0.5),
        "w_ffn_out": nrm(ks[19], (D_FF, D_MODEL), D_FF ** -0.5),
        "normf_g": 1.0 + nrm(ks[20], (D_MODEL,), 0.05),
    }

def first_block(x, norm1_g, w_in, tshift_mu, w_decay_up, w0, a_up, a0, g_up, k_k, k_a, r_k,
              lnx_g, lnx_b, w_o_rwkv, w_o_att, w_out, norm2_g, w_ffn_in, w_ffn_out, normf_g):
    B, S, _ = x.shape
    h = x
    for _layer in range(DEPTH):
        u = rmsnorm(h, norm1_g)
        proj = u @ w_in
        c = np.cumsum([RWKV_COLS, ATT_COLS, IDX_COLS])
        p_rwkv, p_att, p_idx, p_gate = jnp.split(proj, c, axis=-1)

        y_a = rwkv7_mix(token_shift(p_rwkv, tshift_mu), w_decay_up, w0, a_up, a0, g_up,
                        k_k, k_a, r_k, lnx_g, lnx_b)

        q, k, v = jnp.split(p_att, 3, axis=-1)
        hv = lambda t: t.reshape(B, S, ATT_HEADS, HEAD_DIM)
        q, k, v = rope(hv(q)), rope(hv(k)), hv(v)
        ci = np.cumsum([IDX_HEADS * IDX_DIM, IDX_DIM])
        q_idx, k_idx, w_idx = jnp.split(p_idx, ci, axis=-1)
        q_idx = rope(q_idx.reshape(B, S, IDX_HEADS, IDX_DIM))
        k_idx = rope(k_idx[:, :, None, :])[:, :, 0, :]
        y_b = dsa_attention(q, k, v, q_idx, k_idx, w_idx)

        g_a, g_b = jnp.split(jax.nn.sigmoid(p_gate), 2, axis=-1)
        merged = g_a * (y_a @ w_o_rwkv) + g_b * (y_b @ w_o_att)
        h = h + merged @ w_out

        z = rmsnorm(h, norm2_g) @ w_ffn_in
        z_gate, z_up = jnp.split(z, 2, axis=-1)
        h = h + (jax.nn.silu(z_gate) * z_up) @ w_ffn_out
    return rmsnorm(h, normf_g)


GDN_HEADS = 8
GDN_DK = 128
GDN_DV = 128
GDN_CONV = 4
GDN_CHUNK = 64
DIL_PATTERN = ((128, 1), (512, 4), (2048, 16))
DIL_HEADS_PER_GROUP = 4
DIL_HD = 128
DIL_BLOCK = 128
N_EXPERTS = 64
TOP_K = 8
N_GROUPS = 8
TOPK_GROUPS = 4
D_EXPERT = 256
D_SHARED = 256
ROUTE_SCALE = 2.5
MOE_TOKEN_BLOCK = 512
EPS = 1e-6

GDN_QK_W = GDN_HEADS * GDN_DK
GDN_V_W = GDN_HEADS * GDN_DV
N_DIL_GROUPS = len(DIL_PATTERN)
DIL_HEADS = N_DIL_GROUPS * DIL_HEADS_PER_GROUP
DIL_W = DIL_HEADS * DIL_HD
DIL_OUT_W = DIL_HEADS_PER_GROUP * DIL_HD
SPLIT_WIDTHS = (GDN_QK_W, GDN_QK_W, GDN_V_W, GDN_V_W, GDN_HEADS, GDN_HEADS,
                DIL_W, DIL_W, DIL_W, D_MODEL, D_MODEL)
IN_W = sum(SPLIT_WIDTHS)
SPLIT_OFFSETS = tuple(sum(SPLIT_WIDTHS[:i + 1]) for i in range(len(SPLIT_WIDTHS) - 1))


def _rms(t, g):
    t32 = t.astype(jnp.float32)
    return t32 * lax.rsqrt(jnp.mean(t32 * t32, axis=-1, keepdims=True) + EPS) * g.astype(jnp.float32)

def _l2norm(t):
    return t * lax.rsqrt(jnp.sum(t * t, axis=-1, keepdims=True) + EPS)

def causal_depthwise_conv(x, w):
    K, C = w.shape
    return lax.conv_general_dilated(x, w[:, None, :], window_strides=(1,), padding=((K - 1, 0),),
                                    dimension_numbers=('NWC', 'WIO', 'NWC'), feature_group_count=C)

def chunk_gated_delta_rule(q, k, v, g, beta):
    B, H, S, dk = q.shape
    dv = v.shape[-1]
    C = GDN_CHUNK
    N = S // C
    q = q.reshape(B, H, N, C, dk)
    k = k.reshape(B, H, N, C, dk)
    v = v.reshape(B, H, N, C, dv)
    g = g.reshape(B, H, N, C)
    beta = beta.reshape(B, H, N, C)
    gc = jnp.cumsum(g, axis=-1)
    incl = jnp.tril(jnp.ones((C, C), bool))
    strict = jnp.tril(jnp.ones((C, C), bool), -1)
    decay = jnp.exp(jnp.where(incl, gc[..., :, None] - gc[..., None, :], -jnp.inf))
    k_beta = k * beta[..., None]
    a_mat = jnp.where(strict, jnp.einsum('bhnid,bhnjd->bhnij', k_beta, k) * decay, 0.0)
    lmat = a_mat + jnp.eye(C, dtype=a_mat.dtype)
    rhs = jnp.concatenate([v * beta[..., None], k_beta * jnp.exp(gc)[..., None]], axis=-1)
    sol = lax.linalg.triangular_solve(lmat, rhs, left_side=True, lower=True, unit_diagonal=True)
    u, w = sol[..., :dv], sol[..., dv:]
    qk = jnp.einsum('bhnid,bhnjd->bhnij', q, k) * decay
    q_dec = q * jnp.exp(gc)[..., None]
    k_dec = k * jnp.exp(gc[..., -1:] - gc)[..., None]
    g_tot = jnp.exp(gc[..., -1])

    def step(state, xs):
        u_n, w_n, qk_n, qd_n, kd_n, gt_n = xs
        v_new = u_n - jnp.einsum('bhck,bhkv->bhcv', w_n, state)
        o_n = jnp.einsum('bhck,bhkv->bhcv', qd_n, state) + jnp.einsum('bhij,bhjv->bhiv', qk_n, v_new)
        state = state * gt_n[..., None, None] + jnp.einsum('bhck,bhcv->bhkv', kd_n, v_new)
        return state, o_n

    xs = tuple(jnp.moveaxis(t, 2, 0) for t in (u, w, qk, q_dec, k_dec, g_tot))
    state0 = jnp.zeros((B, H, dk, dv), q.dtype)
    _, o = lax.scan(step, state0, xs)
    return jnp.moveaxis(o, 0, 2).reshape(B, H, S, dv)

def gated_deltanet(q, k, v, z, b, a, conv_w, a_log, dt_bias, norm_g):
    B, S, _ = q.shape
    f32 = jnp.float32
    qkv = jnp.concatenate([q, k, v], axis=-1).astype(f32)
    qkv = jax.nn.silu(causal_depthwise_conv(qkv, conv_w.astype(f32)))
    q, k, v = jnp.split(qkv, [GDN_QK_W, 2 * GDN_QK_W], axis=-1)

    def heads(t, d):
        return t.reshape(B, S, GDN_HEADS, d).transpose(0, 2, 1, 3)

    q = _l2norm(heads(q, GDN_DK)) * (GDN_DK ** -0.5)
    k = _l2norm(heads(k, GDN_DK))
    v = heads(v, GDN_DV)
    beta = jax.nn.sigmoid(b.astype(f32)).transpose(0, 2, 1)
    g = (-jnp.exp(a_log.astype(f32)) * jax.nn.softplus(a.astype(f32) + dt_bias.astype(f32))).transpose(0, 2, 1)
    o = chunk_gated_delta_rule(q, k, v, g, beta).transpose(0, 2, 1, 3)
    zg = jax.nn.silu(z.astype(f32).reshape(B, S, GDN_HEADS, GDN_DV))
    o = _rms(o, norm_g) * zg
    return o.reshape(B, S, GDN_V_W)

def dilated_window_attention(q, k, v, window, dilation):
    B, S, h, e = q.shape
    L = S // dilation
    W = window // dilation
    blk = math.gcd(L, DIL_BLOCK)
    nb = L // blk

    def sub(t):
        return t.reshape(B, L, dilation, h, e).transpose(0, 2, 3, 1, 4)

    qs = sub(q).reshape(B, dilation, h, nb, blk, e)
    key_idx = np.arange(nb)[:, None] * blk + np.arange(blk + W)[None, :]
    pad = ((0, 0), (0, 0), (0, 0), (W, 0), (0, 0))
    ks = jnp.pad(sub(k), pad)[:, :, :, key_idx]
    vs = jnp.pad(sub(v), pad)[:, :, :, key_idx]
    dist = np.arange(blk)[:, None] + W - np.arange(blk + W)[None, :]
    valid = (dist >= 0) & (dist <= W) & ((key_idx[:, None, :] - W) >= 0)
    s = jnp.einsum('bdhnqe,bdhnke->bdhnqk', qs, ks) * (e ** -0.5)
    s = jnp.where(valid, s, -jnp.inf)
    m = jnp.max(s, axis=-1, keepdims=True)
    p = jnp.exp(s - m)
    den = jnp.sum(p, axis=-1, keepdims=True)
    o = jnp.einsum('bdhnqk,bdhnke->bdhnqe', p, vs) / den
    lse = (m + jnp.log(den))[..., 0]
    o = o.reshape(B, dilation, h, L, e).transpose(0, 3, 1, 2, 4).reshape(B, S, h, e)
    lse = lse.reshape(B, dilation, h, L).transpose(0, 3, 1, 2).reshape(B, S, h)
    return o, lse

def dilated_mixture(q, k, v, q_norm_g, k_norm_g):
    B, S, _ = q.shape
    q = _rms(q.reshape(B, S, DIL_HEADS, DIL_HD), q_norm_g)
    k = _rms(k.reshape(B, S, DIL_HEADS, DIL_HD), k_norm_g)
    v = v.reshape(B, S, DIL_HEADS, DIL_HD).astype(jnp.float32)
    outs, lses = [], []
    for gi, (win, dil) in enumerate(DIL_PATTERN):
        hs = slice(gi * DIL_HEADS_PER_GROUP, (gi + 1) * DIL_HEADS_PER_GROUP)
        o, lse = dilated_window_attention(q[:, :, hs], k[:, :, hs], v[:, :, hs], win, dil)
        outs.append(o)
        lses.append(lse)
    wts = jax.nn.softmax(jnp.stack(lses), axis=0)
    y = jnp.einsum('gbsh,gbshe->bshe', wts, jnp.stack(outs))
    return y.reshape(B, S, DIL_OUT_W)

def moe_ffn(h, w_router, router_bias, w_gate, w_up, w_down, ws_gate, ws_up, ws_down):
    B, S, D = h.shape
    T = B * S
    f32 = jnp.float32
    ht = h.reshape(T, D)
    scores = jax.nn.sigmoid(ht.astype(f32) @ w_router.astype(f32))
    sel = scores + router_bias.astype(f32)
    grp = sel.reshape(T, N_GROUPS, N_EXPERTS // N_GROUPS)
    grp_score = jnp.sum(lax.top_k(grp, 2)[0], axis=-1)
    _, gidx = lax.top_k(grp_score, TOPK_GROUPS)
    gmask = jnp.sum(jax.nn.one_hot(gidx, N_GROUPS, dtype=f32), axis=1)
    emask = jnp.repeat(gmask, N_EXPERTS // N_GROUPS, axis=1) > 0
    _, eidx = lax.top_k(jnp.where(emask, sel, -jnp.inf), TOP_K)
    wk = jnp.take_along_axis(scores, eidx, axis=-1)
    wk = wk / jnp.sum(wk, axis=-1, keepdims=True) * ROUTE_SCALE
    combine = jnp.einsum('tk,tke->te', wk, jax.nn.one_hot(eidx, N_EXPERTS, dtype=f32)).astype(h.dtype)
    tb = math.gcd(T, MOE_TOKEN_BLOCK)

    def block(args):
        hb, cb = args
        a = jnp.einsum('td,edf->tef', hb, w_gate)
        u = jnp.einsum('td,edf->tef', hb, w_up)
        return jnp.einsum('tef,efd->td', jax.nn.silu(a) * u * cb[..., None], w_down)

    routed = lax.map(block, (ht.reshape(T // tb, tb, D), combine.reshape(T // tb, tb, N_EXPERTS))).reshape(T, D)
    shared = (jax.nn.silu(ht @ ws_gate) * (ht @ ws_up)) @ ws_down
    return (routed + shared).reshape(B, S, D)

def second_inputs(seed: int = 0) -> dict:
    key = jax.random.key(seed)
    ks = jax.random.split(key, 24)
    L, D, E = DEPTH, D_MODEL, N_EXPERTS
    nrm = lambda k, shape, scale: jax.random.normal(k, shape, jnp.float32) * scale
    dt = jnp.exp(jax.random.uniform(ks[7], (L, GDN_HEADS), jnp.float32, math.log(1e-3), math.log(1e-1)))
    return {
        "x": nrm(ks[0], (BATCH, SEQ, D), 1.0),
        "c": nrm(ks[1], (BATCH, D), 1.0),
        "w_ada": nrm(ks[2], (L, D, 6 * D), 0.5 * D ** -0.5),
        "b_ada": nrm(ks[3], (L, 6 * D), 0.02),
        "g_mix": 1.0 + nrm(ks[4], (L, D), 0.05),
        "w_in": nrm(ks[5], (L, D, IN_W), D ** -0.5),
        "gdn_conv_w": nrm(ks[6], (L, GDN_CONV, 2 * GDN_QK_W + GDN_V_W), 0.5),
        "gdn_a_log": jnp.log(jax.random.uniform(ks[8], (L, GDN_HEADS), jnp.float32, 1.0, 16.0)),
        "gdn_dt_bias": dt + jnp.log(-jnp.expm1(-dt)),
        "gdn_norm_g": 1.0 + nrm(ks[9], (L, GDN_DV), 0.05),
        "dil_q_norm_g": 1.0 + nrm(ks[10], (L, DIL_HD), 0.05),
        "dil_k_norm_g": 1.0 + nrm(ks[11], (L, DIL_HD), 0.05),
        "w_up_gdn": nrm(ks[12], (L, GDN_V_W, D), GDN_V_W ** -0.5),
        "w_up_dil": nrm(ks[13], (L, DIL_OUT_W, D), DIL_OUT_W ** -0.5),
        "w_out": nrm(ks[14], (L, D, D), D ** -0.5),
        "g_ffn": 1.0 + nrm(ks[15], (L, D), 0.05),
        "w_router": nrm(ks[16], (L, D, E), D ** -0.5),
        "router_bias": nrm(ks[17], (L, E), 0.01),
        "w_exp_gate": nrm(ks[18], (L, E, D, D_EXPERT), D ** -0.5),
        "w_exp_up": nrm(ks[19], (L, E, D, D_EXPERT), D ** -0.5),
        "w_exp_down": nrm(ks[20], (L, E, D_EXPERT, D), D_EXPERT ** -0.5),
        "w_sh_gate": nrm(ks[21], (L, D, D_SHARED), D ** -0.5),
        "w_sh_up": nrm(ks[22], (L, D, D_SHARED), D ** -0.5),
        "w_sh_down": nrm(ks[23], (L, D_SHARED, D), D_SHARED ** -0.5),
    }

def second_block(x, c, w_ada, b_ada, g_mix, w_in, gdn_conv_w, gdn_a_log, gdn_dt_bias, gdn_norm_g,
              dil_q_norm_g, dil_k_norm_g, w_up_gdn, w_up_dil, w_out, g_ffn, w_router, router_bias,
              w_exp_gate, w_exp_up, w_exp_down, w_sh_gate, w_sh_up, w_sh_down):
    cs = jax.nn.silu(c)
    for l in range(DEPTH):
        mod = (cs @ w_ada[l] + b_ada[l])[:, None, :]
        sh1, sc1, gt1, sh2, sc2, gt2 = jnp.split(mod, 6, axis=-1)
        h = _rms(x, g_mix[l]).astype(x.dtype) * (1.0 + sc1) + sh1
        proj = h @ w_in[l]
        (gq, gk, gv, gz, gb, ga, dil_q, dil_k, dil_v, gate_a, gate_b) = jnp.split(proj, SPLIT_OFFSETS, axis=-1)
        y_a = gated_deltanet(gq, gk, gv, gz, gb, ga, gdn_conv_w[l], gdn_a_log[l], gdn_dt_bias[l],
                             gdn_norm_g[l]).astype(x.dtype)
        y_b = dilated_mixture(dil_q, dil_k, dil_v, dil_q_norm_g[l], dil_k_norm_g[l]).astype(x.dtype)
        merged = jax.nn.sigmoid(gate_a) * (y_a @ w_up_gdn[l]) + jax.nn.sigmoid(gate_b) * (y_b @ w_up_dil[l])
        x = x + gt1 * (merged @ w_out[l])
        h2 = _rms(x, g_ffn[l]).astype(x.dtype) * (1.0 + sc2) + sh2
        x = x + gt2 * moe_ffn(h2, w_router[l], router_bias[l], w_exp_gate[l], w_exp_up[l], w_exp_down[l],
                              w_sh_gate[l], w_sh_up[l], w_sh_down[l])
    return x


def setup_inputs(seed=0):
    out = dict(first_inputs(seed))
    for name, value in second_inputs(seed + 1).items():
        if name != "x":
            out[name + "_2"] = value
    return out


def reference(
    x, norm1_g, w_in, tshift_mu, w_decay_up, w0, a_up, a0, g_up, k_k, k_a, r_k, lnx_g, lnx_b,
    w_o_rwkv, w_o_att, w_out, norm2_g, w_ffn_in, w_ffn_out, normf_g, c_2, w_ada_2, b_ada_2,
    g_mix_2, w_in_2, gdn_conv_w_2, gdn_a_log_2, gdn_dt_bias_2, gdn_norm_g_2, dil_q_norm_g_2,
    dil_k_norm_g_2, w_up_gdn_2, w_up_dil_2, w_out_2, g_ffn_2, w_router_2, router_bias_2,
    w_exp_gate_2, w_exp_up_2, w_exp_down_2, w_sh_gate_2, w_sh_up_2, w_sh_down_2,
):
    x = first_block(
        x, norm1_g, w_in, tshift_mu, w_decay_up, w0, a_up, a0, g_up, k_k, k_a, r_k, lnx_g,
        lnx_b, w_o_rwkv, w_o_att, w_out, norm2_g, w_ffn_in, w_ffn_out, normf_g,
    )
    return second_block(
        x, c_2, w_ada_2, b_ada_2, g_mix_2, w_in_2, gdn_conv_w_2, gdn_a_log_2, gdn_dt_bias_2,
        gdn_norm_g_2, dil_q_norm_g_2, dil_k_norm_g_2, w_up_gdn_2, w_up_dil_2, w_out_2, g_ffn_2,
        w_router_2, router_bias_2, w_exp_gate_2, w_exp_up_2, w_exp_down_2, w_sh_gate_2,
        w_sh_up_2, w_sh_down_2,
    )


_drawn_inputs = setup_inputs


def setup_inputs(seed=0):
    import zlib

    import numpy as np

    out = dict(_drawn_inputs(seed))
    spreads = {}
    factors = {'k_k': 4.288,
     'lnx_b': 3.96,
     'g_mix_2': 2.706,
     'gdn_norm_g_2': 3.918,
     'dil_q_norm_g_2': 5.75,
     'dil_k_norm_g_2': 4.901}
    for name, (base, spread) in spreads.items():
        noise = np.random.default_rng([zlib.crc32(name.encode()), seed]).standard_normal(out[name].shape)
        drawn = base * np.exp(spread * noise) if base else spread * noise
        out[name] = __import__('jax').numpy.asarray(drawn.astype(out[name].dtype))
    for name, factor in factors.items():
        out[name] = (out[name] * factor).astype(out[name].dtype)
    return out
```

```python
from contextlib import ExitStack

import numpy as np

import concourse.bass as bass
from concourse import mybir

F32 = mybir.dt.float32
ACT = mybir.ActivationFunctionType
ALU = mybir.AluOpType
AX = mybir.AxisListType

P = 128
D = 1024
S = 256
KD = D // P
TB = S // P
HEADS = 8
HD = 64
RW = HEADS * HD
RT = RW // P
DFF = 2816
TOPK = 64
NEG = -1.0e30

RWKV_COLS = 3 * RW + 64 + 64 + 128
ATT0 = RWKV_COLS
IDXQ0 = ATT0 + 3 * RW
IDXK0 = IDXQ0 + HEADS * HD
GATE0 = IDXK0 + HD + HEADS

T_R, T_K, T_V, T_WA, T_G = 0, 4, 8, 12, 13
T_Q, T_AK, T_AV, T_QI, T_GATE = 14, 18, 22, 26, 30

SLOTS = 6
SLOT = 2048
CH = 256

GH = 8
DH = 12
GDN_COLS = 4 * GH * P
DIL0 = GDN_COLS + 2 * GH
GATE0_2 = DIL0 + 3 * DH * P
T_GQ, T_GK, T_GV, T_GZ, T_DQ, T_DK, T_DV, T_GATE2 = 0, 8, 16, 24, 32, 44, 56, 68
EXPERTS = 64
DE = 256
TOP_E = 8
GROUPS = 8
TOP_G = 4
ROUTE_SCALE = 2.5

VROWS = {}
for _name, _rows in (("norm1_g", 8), ("tshift_mu", 14), ("w0", 4), ("a0", 4), ("k_k", 4), ("k_a", 4),
                     ("r_k", 4), ("lnx_g", 4), ("lnx_b", 4), ("norm2_g", 8), ("normf_g", 8),
                     ("g_mix_2", 8), ("g_ffn_2", 8), ("c_2", 8), ("gdn_norm_g_2", 1),
                     ("dil_q_norm_g_2", 1), ("dil_k_norm_g_2", 1)):
    VROWS[_name] = (sum(r for _, r in VROWS.values()), _rows)
VA = sum(r for _, r in VROWS.values())
VB = 6 * KD
VC = 4 * 3 * GH

CONST = {}


def constants():
    i = np.arange(P)
    s, t = i[:, None], i[None, :]
    parts = [("ident", s == t), ("ones", np.ones((P, P))),
             ("upper", np.concatenate([s < t, s <= t], 1))]
    for level in range(7):
        half = 1 << level
        pair = (s // (2 * half) == t // (2 * half)) & (s // half % 2 == 0) & (t // half % 2 == 1)
        parts.append((f"level{level}", pair))
    rot = np.zeros((P, P))
    for o in range(P):
        if o % HD < HD // 2:
            rot[o + HD // 2, o] = -1.0
        else:
            rot[o - HD // 2, o] = 1.0
    parts.append(("rot", rot))
    parts.append(("head_ones", s // HD == t // HD))
    inv = (np.float32(1.0) / (np.float32(10000.0) ** (np.arange(HD // 2, dtype=np.float32) * np.float32(2.0) / np.float32(HD)))).astype(np.float32)
    ang = np.arange(S, dtype=np.float32)[None, :] * inv[i % (HD // 2)][:, None]
    parts += [("cos", np.cos(ang)), ("sin", np.sin(ang))]
    parts.append(("before", np.tile((np.arange(8)[None, :] < np.arange(8)[:, None]).reshape(1, 64), (P, 1))))
    for g, (window, step) in enumerate(((128, 1), (512, 4), (2048, 16))):
        gap = s - np.arange(-P, P)[None, :]
        ok = (gap >= 0) & (gap <= window) & (gap % step == 0)
        parts.append((f"dil{g}", np.where(ok, 0.0, NEG)))
    parts.append(("pick", np.tile(np.arange(63)[None, :] == 31, (P, 1))))
    at = 0
    for name, a in parts:
        CONST[name] = (at, a.shape[1])
        at += a.shape[1]
    return np.concatenate([a.astype(np.float32) for _, a in parts], 1)


GROUPS_OF_SIGNALS = {
    "pe_turned": [("x_turned", 2), ("vectors_turned", 1), ("v_turned", 2), ("bk_turned", 2), ("y_turned", 2),
                  ("att_v_turned", 2), ("rows_turned", 1), ("gv_turned", 2), ("gk_turned", 1), ("d_v_turned", 1),
                  ("combine_turned", 1), ("out_turned", 2)],
    "pe_sums_of_squares": [("square_sum_0", 1), ("kk_summed", 1), ("square_sum_1", 1), ("square_sum_2", 1),
                           ("square_sum_3", 1), ("qk_row_sums", 1), ("o_row_sums", 1), ("d_row_sums", 1),
                           ("square_sum_4", 1)],
    "act_squares": [("squares_act_0", 1), ("kk_squared", 1), ("y_squared", 1), ("squares_act_1", 1),
                    ("squares_act_2", 1), ("squares_act_3", 1), ("qk_squared", 4), ("o_squared", 2),
                    ("d_squared", 6), ("squares_act_4", 1)],
    "act_roots": [("root_0", 1), ("kk_norm", 1), ("y_std", 1), ("root_1", 1), ("root_2", 1), ("root_3", 1),
                  ("qk_root", 1), ("o_root", 1), ("d_root", 1), ("root_4", 1)],
    "dve_variances": [("variance_0", 1), ("y_var", 1), ("variance_1", 1), ("variance_2", 1), ("variance_3", 1),
                      ("qk_var", 1), ("o_var", 1), ("d_var", 1), ("variance_4", 1)],
    "dve_inverses": [("o_inverse", 1), ("d_inverse", 1)],
    "dve_logs": [("soft_abs", 1), ("soft_one", 1), ("kd_log", 1)],
    "act_exps": [("rate_exp", 1), ("soft_exp", 1), ("soft_ln", 1), ("kd_ready", 1)],
    "products_made": [("prods_made", 16), ("g_prods_made", 4)],
    "carried_made": [("x_made", 4), ("g_carried", 2)],
    "solution_made": [("sa_made", 4), ("g_solved", 4)],
    "solution_copied": [("sa_copied", 4), ("g_new_copied", 4)],
    "output_made": [("y_made", 4), ("g_out_made", 4)],
    "output_copied": [("y_copied", 4), ("g_out_copied", 4)],
    "state_multiplied": [("state_made", 2), ("g_state_made", 2)],
    "state_written": [("state_ready", 4), ("g_state_ready", 2)],
    "logits_made": [("att_scored", 2), ("d_scored", 8)],
    "maximum_ready": [("row_max", 2), ("d_max_ready", 8)],
    "exps_made": [("probs_made", 16), ("d_probs_made", 8)],
    "exps_turned": [("probs_turned", 2), ("d_probs_turned", 8)],
    "exps_copied": [("probs_t_ready", 3), ("d_probs_t_ready", 8)],
    "mix_made": [("att_made", 2), ("d_mixed", 8)],
    "mix_normed": [("att_normed", 2), ("d_scaled", 2)],
    "mix_turned": [("att_turned", 2), ("d_turned", 2)],
    "mix_copied": [("y_att_copied", 2), ("y_dil_ready", 2)],
}
IN_GROUP = {name: (group, sum(n for _, n in names[:i]))
            for group, names in GROUPS_OF_SIGNALS.items() for i, (name, _) in enumerate(names)}


class Chain:

    def __init__(self, eng, sem):
        self.eng, self.sem, self.n = eng, sem, 0

    def __call__(self, ins):
        self.n += 1
        ins.then_inc(self.sem, 1)
        self.eng.wait_ge(self.sem, self.n)


def build(nc, ins, out, stages=99):
    fp = ins
    ctx = ExitStack()
    with ctx:
        def sb(name, shape):
            return ctx.enter_context(nc.sbuf_tensor(name, shape, F32))

        sems = {}

        def sig(name):
            name = IN_GROUP.get(name, (name, 0))[0]
            if name not in sems:
                sems[name] = ctx.enter_context(nc.semaphore(name))
            return sems[name]

        def reached(name, n):
            return sig(name), n + IN_GROUP.get(name, (name, 0))[1]

        ncst = fp["consts"].shape[1]
        cst = sb("cst", [P, ncst])
        ring = sb("ring", [P, SLOTS, SLOT])
        h = sb("h", [P, KD, S])
        u = sb("u", [P, KD, S])
        proj = sb("proj", [P, 84, S])
        work = sb("work", [P, 10, 1024])
        vec = sb("vec", [P, VA + VB + VC])
        rs = sb("rs", [P, S])
        small = sb("small", [P, 256])
        lora = work[:, 9, :].rearrange("p (s n) -> p s n", s=2)
        idxw = work[:, 3, 0:KD * (HD + HEADS)].rearrange("p (k n) -> p k n", k=KD)
        psum = ctx.enter_context(nc.psum_tensor("psum", [P, 8, 512], F32))
        bank = [psum[:, b, :] for b in range(8)]

        def const(name, rows=P):
            at, n = CONST[name]
            return cst[0:rows, at:at + n]

        ident = const("ident")

        def v(name, k=0):
            if name == "b_ada_2":
                at = VA
            elif name == "conv":
                at = VA + VB
            else:
                at = VROWS[name][0]
            return vec[:, at + k:at + k + 1]

        def unit(i):
            return proj[:, 46 + 4 * i:50 + 4 * i, :]

        def w4(i):
            return work[:, i, :].rearrange("p (m t) -> p m t", m=4)

        def halves(ap):
            flat = ap.rearrange("p m t -> p (m t)")
            return flat[:, 0:512], flat[:, 512:1024]

        fill = [sig(f"slot_filled_{j}") for j in range(SLOTS)]
        multiplied = sig("chunks_multiplied")
        evacuated = sig("chunks_evacuated")

        class Stream:

            def __init__(self):
                self.n = self.linear = 0

            def skip(self, count, linear=True):
                self.n += count
                self.linear += count * linear

        class Chunk:

            def __init__(self, place, c, j, it):
                self.c, self.j = c, j
                self.pair = c // 2 if it is None else it * (SLOTS // 2) + j // 2
                self.third = c // 3 if it is None else it * (SLOTS // 3) + j // 3
                self.slot = (place.n + j) % SLOTS
                self.filled = ((place.n + j) // SLOTS + 1) * 16 + (0 if it is None else it * 16)
                self.n = c + place.n
                self.linear = c + place.linear
                self.turn = it
                self.parity = (place.linear + j) % 2

        def sweep(eng, place, count, body, linear=True):
            turns = count // SLOTS
            done = 0
            if turns > 1:
                with eng.Fori(0, turns) as it:
                    for j in range(SLOTS):
                        body(Chunk(place, it * SLOTS + j, j, it))
                done = turns * SLOTS
            for j in range(done, count):
                body(Chunk(place, j, j, None))
            place.skip(count, linear)

        def columns(w, width, base=0):
            return lambda at: w[:, bass.ds(at.c * width + base, width)].rearrange("(k p) n -> p k n", p=P)

        def rows(w, tiles):
            return lambda at: w[bass.ds(at.c * (tiles * P), tiles * P), :].rearrange("(k p) n -> p k n", p=P)

        def columns_of_pair(w, base):
            return lambda at: w[:, bass.ds(at.pair * CH + base, CH)].rearrange("(k p) n -> p k n", p=P)

        def load(sp, place, count, source, linear=True):
            def body(at):
                if not isinstance(at.n, int) or at.n >= SLOTS:
                    sp.wait_ge(multiplied, at.n - (SLOTS - 1))
                src = source(at)
                sp.dma_start(ring[:, at.slot, :].rearrange("p (k n) -> p k n", k=src.shape[1]), src) \
                    .then_inc(fill[at.slot], 16)
            sweep(sp, place, count, body, linear)

        def pe_linear(pe, place, count, rhs, m_tiles=2, k_tiles=KD):
            width = m_tiles * P
            banks = m_tiles // 2

            def body(at):
                pe.wait_ge(fill[at.slot], at.filled)
                pe.wait_ge(evacuated, at.linear + 1)
                for m in range(m_tiles):
                    for k in range(k_tiles):
                        o = k * width + m * P
                        last = pe.matmul(bank[banks * at.parity + m // 2][:, m % 2 * S:(m % 2 + 1) * S],
                                         ring[:, at.slot, o:o + P], rhs[:, k, :],
                                         start=(k == 0), stop=(k == k_tiles - 1))
                last.then_inc(multiplied, 1)
            sweep(pe, place, count, body)

        def evacuate(eng, place, count, write, banks=1):
            def body(at):
                eng.wait_ge(multiplied, at.n + 1)
                src = psum[:, banks * at.parity:banks * (at.parity + 1), :].rearrange("p b (m t) -> p (b m) t", t=S)
                write(at.c, src).then_inc(evacuated, 1)
            sweep(eng, place, count, body)

        over = sig("stage_over")

        class Stages:
            def __init__(self, eng):
                self.eng, self.n = eng, 0

            def end(self):
                self.n += 1
                self.eng.drain().then_inc(over, 1)
                self.eng.wait_ge(over, 4 * self.n)

        class Norm:
            def __init__(self):
                self.n = 0
        squares = work[:, 0:2, :].rearrange("p a (k t) -> p (a k) t", t=S)

        def act_norm(act, r, shift=None):
            act.activation(squares[:, 0:4, :], h[:, 0:4, :], ACT.Square).then_inc(sig(f"squares_act_{r}"), 1)
            act.wait_ge(*reached(f"variance_{r}", 1))
            act.activation(rs[:, :], rs[:, :], ACT.Sqrt).then_inc(sig(f"root_{r}"), 1)

        def pe_norm(pe, r):
            pe.wait_ge(*reached(f"squares_act_{r}", 1))
            pe.wait_ge(*reached("squares_dve", r + 1))
            for k in range(KD):
                last = pe.matmul(bank[7][:, 0:S], const("ones"), squares[:, k, :], start=(k == 0), stop=(k == KD - 1))
            last.then_inc(sig(f"square_sum_{r}"), 1)

        def dve_norm(dve, link, r, gain, shift=None, dst=u):
            dve.tensor_tensor(squares[:, 4:8, :], h[:, 4:8, :], h[:, 4:8, :], ALU.mult).then_inc(sig("squares_dve"), 1)
            dve.wait_ge(*reached(f"square_sum_{r}", 1))
            dve.tensor_scalar(rs[:, :], bank[7][:, 0:S], 1.0 / D, 1e-6, ALU.mult, ALU.add).then_inc(sig(f"variance_{r}"), 1)
            dve.wait_ge(*reached(f"root_{r}", 1))
            link(dve.reciprocal(rs[:, :], rs[:, :]))
            for k in range(KD):
                ins = dve.scalar_tensor_tensor(out=dst[:, k, :], in0=h[:, k, :], scalar=gain(k), in1=rs[:, :],
                                               op0=ALU.mult, op1=ALU.mult)
                if shift is not None:
                    link(ins)
                    dve.tensor_scalar(dst[:, k, :], dst[:, k, :], shift(k), None, ALU.add)

        comb_dram = nc.dram_tensor("combine", (EXPERTS, S), F32, kind="Internal").ap()
        block = ctx.enter_context(nc.Block())

        decay_log, a_gate, g_gate, kk, k2, bonus, sq, cum = (unit(i) for i in range(8))
        tanh_wd, sig_gd, kidx = proj[:, 78, :], proj[:, 79, :], proj[:, 82, :]
        shifted = work[:, 0:4, :].rearrange("p a n -> p (a n)")[:, 0:14 * S].rearrange("p (m t) -> p m t", t=S)
        ar = work[:, 0:2, :].rearrange("p a (x c s t) -> p (a x) c s t", x=2, c=TB, s=2)
        b_til, k_til, e1, e2, e3, cum_prev = w4(2), w4(3), w4(4), w4(5), w4(6), w4(7)
        v_tok = work[:, 8, :].rearrange("p (c n) -> p c n", c=TB)
        bk_tok = work[:, 9, :].rearrange("p (s n) -> p s n", s=2)
        prods = work[:, 4:6, :].rearrange("p a (h n) -> p (a h) n", n=512)
        levels = [work[:, 6, 0:512], work[:, 6, 512:1024]]
        inv, inv_t = halves(cum)
        upd, xs_sa = halves(kk)
        xs, sa = xs_sa[:, 0:256], xs_sa[:, 256:512]
        state = halves(k2)[0].rearrange("p (m n) -> p m n", m=RT)
        y_tok = decay_log.rearrange("p m t -> p (m t)").rearrange("p (c n) -> p c n", c=TB)
        y_rwkv = unit(1)
        cend = small[:, 0:8].rearrange("p (m c) -> p m c", c=TB)
        mid = small[:, 8:16].rearrange("p (m c) -> p m c", c=TB)
        carry = small[:, 16:20]
        one_less_ka = small[:, 20:24]
        w_idx = small[:, 24:40].rearrange("p (b n) -> p b n", b=TB)
        stat = small[:, 48:64]
        stat2 = small[:, 64:80]

        def heads4(ap):
            return ap.rearrange("p (h t) -> p h t", t=P)

        def spread(ap, n):
            return ap.rearrange("p (o t) -> p o t", o=1).to_broadcast([P, n, ap.shape[1]])

        class Solver:

            def __init__(self, inv, inv_t, upd, levels, m_t):
                self.inv, self.inv_t, self.upd, self.levels, self.m_t = inv, inv_t, upd, levels, m_t

            def pe(self, pe, b):
                inv, inv_t, upd = self.inv, self.inv_t, self.upd
                pe.wait_ge(*reached("solve_start", b + 1))
                for i in range(4):
                    last = pe.transpose(bank[5][:, i * P:(i + 1) * P], inv_t[:, i * P:(i + 1) * P], ident)
                last.then_inc(sig("solve_turned"), 1)
                for lv in range(6):
                    n = 6 * b + lv
                    pe.wait_ge(*reached("level_masked", n + 1))
                    if lv == 0:
                        pe.wait_ge(*reached("solve_copied", b + 1))
                    else:
                        pe.wait_ge(*reached("inv_updated", 11 * b + 2 * lv))
                    for i in range(4):
                        last = pe.matmul(bank[4][:, i * P:(i + 1) * P], self.levels[n % 2][:, i * P:(i + 1) * P],
                                         inv[:, i * P:(i + 1) * P], start=True, stop=True)
                    last.then_inc(sig("upd_made"), 1)
                    pe.wait_ge(*reached("upd_copied", n + 1))
                    if lv < 5:
                        for i in range(4):
                            last = pe.matmul(bank[5][:, i * P:(i + 1) * P], inv_t[:, i * P:(i + 1) * P],
                                             upd[:, i * P:(i + 1) * P], start=True, stop=True)
                        last.then_inc(sig("inv_step"), 1)
                    for i in range(4):
                        last = pe.matmul(bank[6][:, i * P:(i + 1) * P], upd[:, i * P:(i + 1) * P],
                                         inv_t[:, i * P:(i + 1) * P], start=True, stop=True)
                    last.then_inc(sig("inv_step"), 1)

            def act(self, act, b):
                act.wait_ge(*reached("solve_turned", b + 1))
                act.activation(self.inv, bank[5], ACT.Copy).then_inc(sig("solve_copied"), 1)
                for lv in range(6):
                    act.wait_ge(*reached("upd_made", 6 * b + lv + 1))
                    act.activation(self.upd, bank[4], ACT.Copy).then_inc(sig("upd_copied"), 1)

            def dve(self, dve, link, b):
                inv, inv_t = self.inv, self.inv_t
                link(dve.tensor_tensor(heads4(inv_t), self.m_t, spread(const("level0"), 4), ALU.mult))
                dve.tensor_tensor(heads4(inv_t), spread(ident, 4), heads4(inv_t), ALU.subtract) \
                   .then_inc(sig("solve_start"), 1)
                dve.wait_ge(*reached("solve_start", b + 1))
                dve.wait_ge(*reached("solve_copied", b + 1))
                for lv in range(6):
                    done = 11 * b + 2 * lv
                    if lv < 5:
                        dve.wait_ge(*reached("inv_step", done + 1))
                        dve.tensor_tensor(inv, inv, bank[5], ALU.subtract).then_inc(sig("inv_updated"), 1)
                        done += 1
                    dve.wait_ge(*reached("inv_step", done + 1))
                    dve.tensor_tensor(inv_t, inv_t, bank[6], ALU.subtract).then_inc(sig("inv_updated"), 1)
                    dve.wait_ge(*reached("inv_updated", done + 1))

            def pool(self, pool, b):
                for lv in range(6):
                    n = 6 * b + lv
                    if n >= 2:
                        pool.wait_ge(*reached("upd_made", n - 1))
                    pool.tensor_tensor(heads4(self.levels[n % 2]), self.m_t, spread(const(f"level{lv + 1}"), 4), ALU.mult) \
                        .then_inc(sig("level_masked"), 1)

        def batch(b):
            return b // 2, 2 * (b % 2)

        rwkv_solver = Solver(inv, inv_t, upd, levels, prods[:, :, 0:P])

        conv_units = (0, 1, 2, 5, 6, 7)
        beta_rows, rate_rows, soft_rows, gc_rows = (work[0:GH, 4, i * S:(i + 1) * S] for i in range(4))
        norm_rows = rs[0:32, :]
        kq = work[:, 0:4, :].rearrange("p a (h c s t) -> p (a h) c s t", h=2, c=TB, s=2)
        vb_tok = work[:, 5:7, :].rearrange("p c (h n) -> p c h n", h=GH)
        kd_tok = work[:, 7, :].rearrange("p (h n) -> p h n", h=GH)
        egrow = work[:, 7, 0:512]
        g_prods = work[:, 8, :].rearrange("p (h s t) -> p h s t", h=4, s=2)
        g_levels = [work[:, 9, 0:512], work[:, 9, 512:1024]]
        late = proj[:, T_GV:T_GV + 8, :].rearrange("p (a m) t -> p a (m t)", a=4)
        g_inv, g_inv_t, g_upd, g_xs = (late[:, i, :] for i in range(4))
        g_solver = Solver(g_inv, g_inv_t, g_upd, g_levels, g_prods[:, :, 0, :])
        o_gdn = proj[:, T_GQ:T_GQ + GH, :]
        decays = u[:, 0:4, :].rearrange("p (h) (s t) -> p h s t", s=2)
        g_state = u[:, 4:8, :].rearrange("p a (h n) -> p (a h) n", h=2)
        y_gdn = proj[:, T_GZ:T_GZ + GH, :]
        gc_col = small[:, 200:216].rearrange("p (c n) -> p c n", c=TB)
        beta_col = small[:, 216:232].rearrange("p (c n) -> p c n", c=TB)
        kd_col = small[:, 232:240]
        rate_col, dt_col = small[0:GH, 240:241], small[0:GH, 241:242]
        d_logits = [work[:, i, 0:768].rearrange("p (g n) -> p g n", g=3) for i in range(2)]
        d_probs = [work[:, 2 + i, 0:768].rearrange("p (g n) -> p g n", g=3) for i in range(2)]
        d_probs_t = work[:, 4, 0:768].rearrange("p (g n) -> p g n", g=3)
        dv_tok = work[:, 5:8, :].rearrange("p a n -> p (a n)").rearrange("p (c h n) -> p c h n", c=TB, h=DH)
        d_tok = work[:, 8, 0:512]
        y_dil = w4(9)
        d_max, d_sum = small[:, 80:88], small[:, 96:104]
        router = proj[:, 32:34, :].rearrange("p a n -> p (a n)").rearrange("p (k n) -> p k n", k=KD)
        router_b = proj[:, 34, 0:EXPERTS]
        sc_e, sel_e, left_e, comb_e = (work[:, 3, (2 + 2 * i) * EXPERTS:(4 + 2 * i) * EXPERTS].rearrange("p (b n) -> p b n", b=TB) for i in range(4))
        best_e = work[:, 4, 0:128].rearrange("p (b g n) -> p b g n", b=TB, g=GROUPS)
        gs_e = work[:, 4, 128:144].rearrange("p (b g) -> p b g", b=TB)
        more_e, same_e = (work[:, 4, 256 + i * 64:320 + i * 64].rearrange("p (g j) -> p g j", g=GROUPS) for i in range(2))
        rank_e, sum_e, top_e = work[:, 4, 400:408], work[:, 4, 408:409], work[:, 4, 416:424]
        comb_t = work[0:EXPERTS, 4, 512:768]
        silu_e = [work[:, 5, i * 512:(i + 1) * 512] for i in range(2)]
        hid_e = [work[:, 6, i * 512:(i + 1) * 512] for i in range(2)]
        comb_row = [work[:, 7, i * S:(i + 1) * S] for i in range(2)]
        out_tok = work[:, 8:10, :]

        dil_items = [(b, i) for b in range(TB) for i in range(4)]
        dil_masks = cst[:, CONST["dil0"][0]:CONST["dil0"][0] + 6 * P].rearrange("p (g n) -> p g n", g=3)

        def add_gated(dve, place, gate):
            for c in range(2):
                lin = place.linear + c
                tl = slice(4 * c, 4 * c + 4)
                dve.wait_ge(multiplied, place.n + c + 1)
                src = psum[:, 2 * (lin % 2):2 * (lin % 2) + 2, :].rearrange("p b (m t) -> p (b m) t", t=S)
                dve.tensor_tensor(merge_tmp, src, proj[:, gate + 4 * c:gate + 4 * c + 4, :], ALU.mult).then_inc(evacuated, 1)
                dve.wait_ge(evacuated, lin + 3)
                dve.tensor_tensor(merged[:, tl, :], merged[:, tl, :], merge_tmp, ALU.add).then_inc(sig("merged_ready"), 1)
                dve.wait_ge(*reached("merged_ready", c + 1 + (2 if gate > T_GATE + KD else 0)))
            place.skip(2)

        def expert_steps(step):
            step(0, 0, None)
            step(1, 1, 0)
            step(2, 0, 0)

        def expert_loop(eng, step):
            with eng.Fori(0, EXPERTS // 2 - 1) as it:
                step(it * 2 + 3, 1, it + 1)
                step(it * 2 + 4, 0, it + 1)

        def act_experts(act, place):
            n0 = place.n

            def step(e, par, turn):
                act.wait_ge(multiplied, n0 + 1 if turn is None else e * 3 + n0)
                if turn is not None:
                    act.wait_ge(*reached("hid_ready", e))
                act.activation(silu_e[par], bank[4 + 2 * par], ACT.Silu).then_inc(sig("silu_done"), 1)
            expert_steps(step)
            expert_loop(act, step)

        def dve_experts(dve, place):
            n0 = place.n
            by_tile = lambda ap: ap.rearrange("p (f t) -> p f t", f=2)

            def step(e, par, turn):
                dve.wait_ge(multiplied, n0 + 2 if turn is None else e * 3 + (n0 + 1))
                dve.wait_ge(*reached("silu_done", e + 1))
                if turn is None:
                    dve.tensor_tensor(hid_e[par], silu_e[par], bank[5 + 2 * par], ALU.mult).then_inc(sig("au_free"), 1)
                    dve.drain().then_inc(sig("hid_ready"), 1)
                    return
                dve.tensor_tensor(silu_e[par], silu_e[par], bank[5 + 2 * par], ALU.mult).then_inc(sig("au_free"), 1)
                dve.wait_ge(*reached("au_free", e + 3))
                dve.wait_ge(*reached(f"comb_filled_{1 - par}", turn * 16 + 16))
                dve.tensor_tensor(by_tile(hid_e[par]), by_tile(silu_e[par]), spread(comb_row[1 - par], 2), ALU.mult).then_inc(sig("hid_ready"), 1)
            expert_steps(step)
            expert_loop(dve, step)

        def later(at):
            at.third = at.third + SLOTS // 3
            return at

        def row_to_all(pe, dst, rows_, i, k, first=True):
            return pe.matmul(dst, ident[0:k, i:i + 1].to_broadcast([k, P]), rows_, start=True, stop=True)

        def sum_to_row(pe, dst, src, i, n):
            return pe.matmul(dst, const("pick")[:, 31 - i:63 - i], src, start=(i == 0), stop=(i == n - 1))

        relu_s = work[:, 0:2, :].rearrange("p a (b n) -> p (a b) n", n=512)
        score, rest, sel_bias = (work[:, 2, i * S:(i + 1) * S] for i in range(3))
        logits = work[:, 3:5, :].rearrange("p a (b n) -> p (a b) n", n=512)
        probs = work[:, 5:7, :].rearrange("p a (b n) -> p (a b) n", n=512)
        probs_t = work[:, 7:9, :].rearrange("p a (i t) -> p a i t", t=P)
        att_v = unit(3).rearrange("p m t -> p (m t)").rearrange("p (c n) -> p c n", c=TB)
        att_tok = halves(unit(4))[0]
        y_att = unit(6)
        top8, row_max, row_sum = small[:, 80:88], small[:, 88:96], small[:, 96:104]
        rope_tmp = work[:, 0:4, :].rearrange("p a (b n) -> p (a b) n", n=512)
        rope_tiles = [proj[:, t:t + 2, :] for t in (T_Q, T_Q + 2, T_AK, T_AK + 2, T_QI, T_QI + 2)] + [proj[:, 82:83, :]]
        own_causal = const("dil0")[:, P:2 * P]
        merged = work[:, 0:2, :].rearrange("p a (k t) -> p (a k) t", t=S)
        merge_tmp = w4(2)
        hidden = proj[:, 0:DFF // P, :]
        mods = small[:, 128:176]
        gain1, gain2, c_act = small[:, 176:184], small[:, 184:192], small[:, 192:200]

        baw = work[:, 3, 0:KD * 16].rearrange("p (k n) -> p k n", k=KD)
        ba_rows = work[0:8, 4, 0:2 * S].rearrange("p (s t) -> p s t", s=2)

        def place_of(hd):
            return 2 * (hd // 4) + hd % 2, hd // 2 % 2

        def head_at(i):
            return i // 4 * 4 + i // 2 % 2 + 2 * (i % 2)

        def pe_scores(pe, base, q_tile, key, b, n):
            for hd in range(HEADS):
                bk, half = place_of(hd)
                part = slice(HD * (hd % 2), HD * (hd % 2) + HD)
                last = pe.matmul(bank[base + bk][:, half * S:half * S + n], proj[part, q_tile + hd // 2, b * P:(b + 1) * P],
                                 key(hd)[part, 0:n], start=True, stop=True)
            return last

        def pair_view(ap, n):
            return ap.rearrange("p (i n) -> p i n", i=2)[:, :, 0:n]

        @block.sync
        def _(sp):
            place = Stream()
            sp.dma_start(work[:, 0:2, :], fp["x"].rearrange("o (b p) d -> p (o b) d", p=P)).then_inc(sig("x_loaded"), 16)
            sp.dma_start(cst[:, :], fp["consts"]).then_inc(sig("consts_loaded"), 16)
            stage = work[:, 2, :]
            for name, (at, n) in VROWS.items():
                src = fp[name]
                if len(src.shape) == 2:
                    src = src.rearrange("a b -> (a b)")
                sp.dma_start(stage[at:at + n, 0:P], src.rearrange("(a p) -> a p", p=P)).then_inc(sig("vectors_loaded"), 16)
            sp.dma_start(stage[0:VB, P:2 * P], fp["b_ada_2"].rearrange("o (a p) -> (o a) p", p=P)).then_inc(sig("vectors_loaded"), 16)
            sp.dma_start(stage[0:VC, 2 * P:3 * P], fp["gdn_conv_w_2"].rearrange("o j (a p) -> (o j a) p", p=P)).then_inc(sig("vectors_loaded"), 16)
            sp.dma_start(lora[0:64, 0, :], fp["w_decay_up"]).then_inc(sig("lora_loaded"), 16)
            sp.dma_start(lora[64:128, 0, :], fp["a_up"]).then_inc(sig("lora_loaded"), 16)
            sp.dma_start(lora[:, 1, :], fp["g_up"]).then_inc(sig("lora_loaded"), 16)
            sp.dma_start(idxw[:, :, :], fp["w_in"][:, IDXK0:GATE0].rearrange("(k p) n -> p k n", p=P)).then_inc(sig("idxw_loaded"), 16)
            first = columns(fp["w_in"], CH)
            load(sp, place, SLOTS, first)
            load(sp, place, 15 - SLOTS, columns(fp["w_in"], CH, SLOTS * CH))
            load(sp, place, 8, columns(fp["w_in"], CH, GATE0))
            load(sp, place, 2, columns(fp["w_o_rwkv"], 512))
            load(sp, place, 2, columns(fp["w_o_att"], 512))
            load(sp, place, 4, columns(fp["w_out"], CH))
            pair_source = [columns_of_pair(fp["w_ffn_in"], 0), columns_of_pair(fp["w_ffn_in"], DFF)]
            load(sp, place, 2 * (DFF // CH), lambda at: pair_source[at.j % 2](at), linear=False)
            load(sp, place, DFF // (2 * P), rows(fp["w_ffn_out"], 2), linear=False)
            load(sp, place, 24, columns(fp["w_ada_2"][0], CH), linear=False)
            if stages < 7:
                return
            sp.wait_ge(over, 4 * 6)
            sp.dma_start(baw, fp["w_in_2"][0][:, GDN_COLS:DIL0].rearrange("(k p) n -> p k n", p=P)).then_inc(sig("ba_loaded"), 16)
            for first, count in ((0, 12), (12, 4)):
                load(sp, place, count, columns(fp["w_in_2"][0], CH, first * CH))
            for first, count in ((0, 18), (18, 8)):
                load(sp, place, count, columns(fp["w_in_2"][0], CH, DIL0 + first * CH))
            if stages < 8:
                return
            sp.dma_start(rate_col, fp["gdn_a_log_2"].rearrange("o h -> h o")).then_inc(sig("rates_loaded"), 16)
            sp.dma_start(dt_col, fp["gdn_dt_bias_2"].rearrange("o h -> h o")).then_inc(sig("rates_loaded"), 16)
            if stages < 10:
                return
            load(sp, place, 4, columns(fp["w_up_gdn_2"][0], CH))
            load(sp, place, 2, columns(fp["w_up_dil_2"][0], 512))
            load(sp, place, 4, columns(fp["w_out_2"][0], CH))
            if stages < 11:
                return
            tall = lambda w: w.rearrange("(k p) n -> p k n", p=P)
            load(sp, place, 2, lambda at: tall(fp[("w_sh_gate_2", "w_sh_up_2")[at.c]][0]), linear=False)
            sp.wait_ge(over, 4 * 16)
            sp.dma_start(router, fp["w_router_2"][0].rearrange("(k p) n -> p k n", p=P)).then_inc(sig("router_loaded"), 16)
            sp.dma_start(router_b, fp["router_bias_2"].to_broadcast([P, EXPERTS])).then_inc(sig("router_loaded"), 16)

            def expert_source(at):
                kind = at.j % 3
                if kind < 2:
                    w = fp[("w_exp_gate_2", "w_exp_up_2")[kind]][0]
                    return w[bass.ds(at.third, 1), :, :].rearrange("e (k p) n -> p (e k) n", p=P)
                w = fp["w_exp_down_2"][0]
                return w[bass.ds(at.third - 1, 1), :, :].rearrange("e (k p) n -> p (e k) n", p=P)
            first_sources = lambda at: tall(fp["w_sh_down_2"][0]) if at.c == 2 else expert_source(at)
            load(sp, place, SLOTS, first_sources, linear=False)
            load(sp, place, 3 * EXPERTS - SLOTS, lambda at: expert_source(later(at)), linear=False)
            load(sp, place, 1, lambda at: tall(fp["w_exp_down_2"][0][EXPERTS - 1]), linear=False)
            for b in range(TB):
                sp.wait_ge(*reached(f"out_ready_{b}", 1))
                sp.dma_start(out[0, b * P:(b + 1) * P, :], out_tok[:, b, :]).then_inc(sig("out_written"), 16)
            sp.wait_ge(*reached("out_written", 32))

        @block.gpsimd
        def _(pool):
            st = Stages(pool)
            st.end()
            st.end()
            link = Chain(pool, sig("pool_chain"))
            pool.wait_ge(*reached("token_shifted", 1))
            pool.wait_ge(*reached("a_gate_ready", 4))
            pool.wait_ge(*reached("one_less_ka_ready", 1))
            for m in range(RT):
                pool.tensor_scalar(k2[:, m, :], a_gate[:, m, :], v("k_a", m), one_less_ka[:, m:m + 1], ALU.mult, ALU.add) \
                    .then_inc(sig("pool_scaled"), 1)
            pool.wait_ge(*reached("pool_scaled", 4))
            pool.tensor_tensor(k2, k2, proj[:, T_K:T_K + RT, :], ALU.mult).then_inc(sig("k2_ready"), 1)
            pool.wait_ge(*reached("k2_ready", 1))
            link(pool.tensor_tensor(bonus, k2, proj[:, T_R:T_R + RT, :], ALU.mult))
            for m in range(RT):
                pool.tensor_scalar(bonus[:, m, :], bonus[:, m, :], v("r_k", m), None, ALU.mult).then_inc(sig("bonus_terms"), 1)
            st.end()
            if stages < 2:
                return
            for b in range(4):
                pool.wait_ge(*reached("prods_masked", 4 * (b + 1)))
                rwkv_solver.pool(pool, b)
            st.end()
            if stages < 3:
                return
            for i, t in enumerate(rope_tiles):
                n = t.shape[1]
                pool.tensor_tensor(rope_tmp[:, i, 0:n * S].rearrange("p (m t) -> p m t", t=S), t, spread(const("cos"), n), ALU.mult) \
                    .then_inc(sig("rope_cos"), 1)
            st.end()
            st.end()
            st.end()
            st.end()
            st.end()
            if stages < 7:
                return
            st.end()
            if stages < 8:
                return
            st.end()
            st.end()
            for b in range(4):
                pool.wait_ge(*reached("decay_exp", b + 1))
                if b:
                    pool.wait_ge(*reached("g_prods_ready", b))
                pool.tensor_tensor(decays, heads4(g_xs).rearrange("p h (o t) -> p h o t", o=1).to_broadcast([P, 4, 2, P]),
                                   const("upper").rearrange("p (o s t) -> p o s t", o=1, s=2).to_broadcast([P, 4, 2, P]), ALU.mult) \
                    .then_inc(sig("decay_masked"), 1)
                pool.wait_ge(*reached("g_prods_ready", b + 1))
                g_solver.pool(pool, 4 + b)
            st.end()
            st.end()
            if stages < 9:
                return
            st.end()
            st.end()
            if stages < 10:
                return
            st.end()
            if stages < 11:
                return
            pool.wait_ge(*reached("combine_written", 16))
            with pool.Fori(0, EXPERTS // 2) as it:
                for j in range(2):
                    pool.wait_ge(*reached("hid_ready", it * 2 + (j + 1)))
                    pool.dma_start(comb_row[j], comb_dram[bass.ds(it * 2 + j, 1), :].to_broadcast([P, S])).then_inc(sig(f"comb_filled_{j}"), 16)
            st.end()
            st.end()

        @block.scalar
        def _(act):
            st = Stages(act)
            place = Stream()
            act.drain().then_inc(evacuated, 2)
            act.wait_ge(*reached("x_turned", 2))
            act.activation(h[:, :, P:S], psum[:, 2:4, :].rearrange("p b (k t) -> p (b k) t", t=P), ACT.Copy)
            st.end()
            act_norm(act, 0)
            act.wait_ge(*reached("idx_multiplied", 2))
            act.activation(kidx, bank[4][:, 0:S], ACT.Copy)
            act.activation(w_idx, bank[5][:, 0:2 * HEADS].rearrange("p (b n) -> p b n", b=TB), ACT.Copy,
                           scale=float(HD) ** -0.5 * float(HEADS) ** -0.5)
            evacuate(act, place, 15, lambda c, src: act.activation(proj[:, bass.ds(c * 2, 2), :], src, ACT.Copy))
            evacuate(act, place, 8, lambda c, src: act.activation(proj[:, bass.ds(c * 2 + T_GATE, 2), :], src, ACT.Sigmoid))
            st.end()
            act.wait_ge(*reached("token_shifted", 1))
            act.activation(tanh_wd[0:64, :], proj[0:64, T_WA, :], ACT.Tanh).then_inc(sig("lora_in"), 1)
            act.activation(sig_gd, proj[:, T_G, :], ACT.Sigmoid).then_inc(sig("lora_in"), 1)
            for m in range(RT):
                act.wait_ge(*reached("lora_out", 1))
                act.activation(a_gate[:, m, :], bank[2 + m // 2][:, m % 2 * S:(m % 2 + 1) * S], ACT.Sigmoid, bias=v("a0", m)) \
                   .then_inc(sig("a_gate_ready"), 1)
            for m in range(RT):
                act.activation(decay_log[:, m, :], bank[m // 2][:, m % 2 * S:(m % 2 + 1) * S], ACT.Sigmoid, bias=v("w0", m)) \
                   .then_inc(sig("decay_sig"), 1)
            act.activation(g_gate, psum[:, 4:6, :].rearrange("p b (m t) -> p (b m) t", t=S), ACT.Copy).then_inc(sig("g_copied"), 1)
            act.wait_ge(*reached("kk_raw", 1))
            act.activation(sq, kk, ACT.Square).then_inc(sig("kk_squared"), 1)
            act.wait_ge(*reached("kk_summed", 1))
            act.activation(sq, psum[:, 6:8, :].rearrange("p b (m t) -> p (b m) t", t=S), ACT.Sqrt).then_inc(sig("kk_norm"), 1)
            act.wait_ge(*reached("cum_ready", 1))
            act.activation(e1, cum, ACT.Exp).then_inc(sig("exps"), 1)
            act.activation(e2, cum, ACT.Exp, scale=-1.0).then_inc(sig("exps"), 1)
            act.wait_ge(*reached("cum_ready", 2))
            act.activation(e3, cum_prev, ACT.Exp).then_inc(sig("exps"), 1)
            act.activation(carry, carry, ACT.Exp).then_inc(sig("exps"), 1)
            act.wait_ge(*reached("v_turned", 2))
            act.activation(v_tok, psum[:, 0:2, :], ACT.Copy)
            act.wait_ge(*reached("bk_turned", 2))
            act.activation(bk_tok, psum[:, 2:4, :], ACT.Copy)
            st.end()
            if stages < 2:
                return
            for b in range(4):
                ch, m0 = batch(b)
                rwkv_solver.act(act, b)
                act.wait_ge(*reached("x_made", b + 1))
                act.activation(xs, bank[7][:, 0:256], ACT.Copy, scale=-1.0).then_inc(sig("x_copied"), 1)
                act.wait_ge(*reached("sa_made", b + 1))
                act.activation(sa, bank[4][:, 0:256], ACT.Copy).then_inc(sig("sa_copied"), 1)
                act.wait_ge(*reached("y_made", b + 1))
                act.activation(y_tok[:, ch, m0 * P:m0 * P + 256], bank[5][:, 0:256], ACT.Copy).then_inc(sig("y_copied"), 1)
            yc = w4(0).rearrange("p m t -> p (m t)").rearrange("p (g n) -> p g n", n=HD)
            act.wait_ge(*reached("y_centred", 1))
            act.activation(w4(1).rearrange("p m t -> p (m t)").rearrange("p (g n) -> p g n", n=HD), yc, ACT.Square).then_inc(sig("y_squared"), 1)
            act.wait_ge(*reached("y_var", 1))
            act.activation(stat2, stat2, ACT.Sqrt).then_inc(sig("y_std"), 1)
            act.wait_ge(*reached("y_turned", 2))
            for m in range(RT):
                act.activation(w4(2)[:, m, :].rearrange("p (c t) -> p c t", c=TB),
                               psum[:, 0:2, m * P:(m + 1) * P], ACT.Identity, scale=v("lnx_g", m), bias=v("lnx_b", m)) \
                   .then_inc(sig("y_affine"), 1)
            st.end()
            if stages < 3:
                return
            for c in range(TB):
                act.wait_ge(*reached("att_v_turned", c + 1))
                act.activation(att_v[:, c, :], bank[7], ACT.Copy).then_inc(sig("att_v_copied"), 1)
            st.end()
            for b in range(TB):
                n = (b + 1) * P
                act.wait_ge(*reached("idx_scored", b + 1))
                if b:
                    act.wait_ge(*reached("idx_summed", b))
                for bk in range(4):
                    act.activation(pair_view(relu_s[:, bk, :], n), pair_view(bank[bk], n), ACT.Relu).then_inc(sig("idx_relu"), 1)
                act.wait_ge(*reached("row_max", b + 1))
                for i in range(HEADS):
                    hd = head_at(i)
                    act.activation(pair_view(probs[:, i // 2, :], n)[:, i % 2, :], pair_view(logits[:, i // 2, :], n)[:, i % 2, :], ACT.Exp,
                                   bias=row_max[:, i:i + 1], accum_out=row_sum[:, hd:hd + 1]).then_inc(sig("probs_made"), 1)
                act.wait_ge(*reached("probs_turned", b + 1))
                if b:
                    act.wait_ge(*reached("att_made", b))
                for kb in range(b + 1):
                    act.activation(probs_t[:, kb, :, :], psum[:, 2 * kb:2 * kb + 2, :].rearrange("p a (i t) -> p (a i) t", t=P), ACT.Copy) \
                       .then_inc(sig("probs_t_ready"), 1)
                act.wait_ge(*reached("att_turned", b + 1))
                act.activation(y_att[:, :, b * P:(b + 1) * P], bank[5].rearrange("p (m t) -> p m t", t=P), ACT.Copy).then_inc(sig("y_att_copied"), 1)
            st.end()
            st.end()
            place.skip(8)
            act_norm(act, 1)

            def silu_gate(at):
                if at.j % 2 == 0:
                    act.wait_ge(multiplied, at.n + 1)
                    src = bank[at.j // 2 % 3 * 2].rearrange("p (m t) -> p m t", t=S)
                    act.activation(hidden[:, bass.ds(at.pair * 2, 2), :], src, ACT.Silu).then_inc(sig("gate_silu"), 1)
            sweep(act, place, 2 * (DFF // CH), silu_gate, linear=False)
            place.skip(DFF // (2 * P), False)
            act.wait_ge(*reached("h_ready", 1))
            act_norm(act, 2)
            st.end()
            act.activation(c_act, vec[:, VROWS["c_2"][0]:VROWS["c_2"][0] + KD], ACT.Silu).then_inc(sig("c_ready"), 1)
            place.skip(24, False)
            st.end()
            if stages < 7:
                return
            act_norm(act, 3)
            act.wait_ge(*reached("ba_multiplied", 1))
            act.activation(ba_rows, bank[4][0:8, :].rearrange("p (s t) -> p s t", s=2), ACT.Copy)
            copy_to = lambda base, func: lambda c, src: act.activation(proj[:, bass.ds(c * 2 + base, 2), :], src, func)
            evacuate(act, place, 12, copy_to(0, ACT.Copy))
            evacuate(act, place, 4, copy_to(T_GZ, ACT.Silu))
            evacuate(act, place, 18, copy_to(T_DQ, ACT.Copy))
            evacuate(act, place, 8, copy_to(T_GATE2, ACT.Sigmoid))
            st.end()
            if stages < 8:
                return
            for i, un in enumerate(conv_units):
                act.wait_ge(*reached("conv_summed", i + 1))
                act.activation(proj[:, 4 * i:4 * i + 4, :], w4(un), ACT.Silu).then_inc(sig("conv_done"), 1)
            act.wait_ge(*reached("rates_loaded", 32))
            act.activation(rate_col, rate_col, ACT.Exp).then_inc(sig("rate_exp"), 1)
            act.activation(beta_rows, beta_rows, ACT.Sigmoid)
            act.wait_ge(*reached("soft_abs", 1))
            act.activation(soft_rows, soft_rows, ACT.Exp, scale=-1.0).then_inc(sig("soft_exp"), 1)
            act.wait_ge(*reached("soft_exp", 1))
            act.wait_ge(*reached("soft_one", 1))
            act.activation(soft_rows, soft_rows, ACT.Ln).then_inc(sig("soft_ln"), 1)
            act.wait_ge(*reached("conv_done", 6))
            for i in range(4):
                act.activation(w4((0, 1, 2, 5)[i]), proj[:, 4 * i:4 * i + 4, :], ACT.Square).then_inc(sig("qk_squared"), 1)
            act.wait_ge(*reached("qk_var", 1))
            act.activation(norm_rows[0:16, :], norm_rows[0:16, :], ACT.Sqrt).then_inc(sig("qk_root"), 1)
            st.end()
            act.wait_ge(*reached("rows_turned", 1))
            act.activation(gc_col, bank[0][:, 0:16].rearrange("p (c n) -> p c n", c=TB), ACT.Copy).then_inc(sig("cols_copied"), 1)
            act.activation(beta_col, bank[0][:, 16:32].rearrange("p (c n) -> p c n", c=TB), ACT.Copy).then_inc(sig("cols_copied"), 1)
            act.wait_ge(*reached("kd_log", 1))
            act.activation(kd_col, kd_col, ACT.Exp).then_inc(sig("kd_ready"), 1)
            st.end()
            for b in range(4):
                ch, h0 = b // 2, 4 * (b % 2)
                act.wait_ge(*reached("decay_log", b + 1))
                act.activation(g_xs, g_xs, ACT.Exp).then_inc(sig("decay_exp"), 1)
                if ch:
                    act.wait_ge(*reached("gc_spread", b + 1))
                    if b == 2:
                        act.wait_ge(*reached("g_state_made", 2))
                    act.activation(egrow, bank[7], ACT.Exp).then_inc(sig("eg_ready"), 1)
                g_solver.act(act, 4 + b)
                act.wait_ge(*reached("g_solved", b + 1))
                act.activation(g_upd, bank[4], ACT.Copy).then_inc(sig("g_new_copied"), 1)
                act.wait_ge(*reached("g_out_made", b + 1))
                act.activation(o_gdn[:, h0:h0 + 4, ch * P:(ch + 1) * P], heads4(bank[5]), ACT.Copy).then_inc(sig("g_out_copied"), 1)
            st.end()
            for i in range(2):
                act.activation(w4(i), o_gdn[:, 4 * i:4 * i + 4, :], ACT.Square).then_inc(sig("o_squared"), 1)
            act.wait_ge(*reached("o_var", 1))
            act.activation(norm_rows[0:8, :], norm_rows[0:8, :], ACT.Sqrt).then_inc(sig("o_root"), 1)
            st.end()
            if stages < 9:
                return
            for i in range(6):
                act.activation(w4(i), proj[:, T_DQ + 4 * i:T_DQ + 4 * i + 4, :], ACT.Square).then_inc(sig("d_squared"), 1)
            act.wait_ge(*reached("d_var", 1))
            act.activation(norm_rows[0:24, :], norm_rows[0:24, :], ACT.Sqrt).then_inc(sig("d_root"), 1)
            act.wait_ge(*reached("d_v_turned", 1))
            act.wait_ge(*reached("d_row_sums", 1))
            act.activation(dv_tok.rearrange("p c h n -> p (c h n)"), psum[:, 2:8, :].rearrange("p b n -> p (b n)"), ACT.Copy)
            st.end()
            for i, (b, slot_) in enumerate(dil_items):
                n = (b + 1) * P
                at = slot_ + 4 * b
                act.wait_ge(*reached("d_max_ready", i + 1))
                if i >= 2:
                    act.wait_ge(*reached("d_probs_turned", i - 1))
                act.activation(d_probs[i % 2][:, :, 0:n], d_logits[i % 2][:, :, 0:n], ACT.Exp, bias=d_max[:, at:at + 1],
                               accum_out=d_sum[:, at:at + 1]).then_inc(sig("d_probs_made"), 1)
                act.wait_ge(*reached("d_probs_turned", i + 1))
                if i:
                    act.wait_ge(*reached("d_mixed", i))
                act.activation(d_probs_t[:, :, 0:n], psum[:, 4:6, :].rearrange("p b n -> p (b n)")[:, 0:768].rearrange("p (g n) -> p g n", g=3)[:, :, 0:n],
                               ACT.Copy).then_inc(sig("d_probs_t_ready"), 1)
                if slot_ == 3:
                    act.wait_ge(*reached("d_turned", b + 1))
                    act.activation(y_dil[:, :, b * P:(b + 1) * P], heads4(bank[7]), ACT.Copy).then_inc(sig("y_dil_ready"), 1)
            st.end()
            if stages < 10:
                return
            place.skip(10)
            st.end()
            if stages < 11:
                return
            act_norm(act, 4)
            act.wait_ge(*reached("routed", 1))
            act.activation(sc_e, bank[0][:, 0:2 * EXPERTS].rearrange("p (b n) -> p b n", b=TB), ACT.Sigmoid).then_inc(sig("scores_ready"), 1)
            act.wait_ge(*reached("combine_turned", 1))
            act.activation(comb_t, bank[0][0:EXPERTS, 0:S], ACT.Copy).then_inc(sig("combine_copied"), 1)
            act.wait_ge(*reached("combine_copied", 1))
            act.dma_start(comb_dram, comb_t).then_inc(sig("combine_written"), 16)

            act_experts(act, place)
            st.end()
            act.wait_ge(*reached("out_turned", 1))
            act.activation(out_tok[:, 0, :], psum[:, 4:6, :].rearrange("p b n -> p (b n)"), ACT.Copy).then_inc(sig("out_ready_0"), 1)
            act.wait_ge(*reached("combine_written", 16))
            st.end()

        @block.vector
        def _(dve):
            st = Stages(dve)
            link = Chain(dve, sig("dve_chain"))
            dve.wait_ge(*reached("x_turned", 2))
            dve.tensor_copy(h[:, :, 0:P], psum[:, 0:2, :].rearrange("p b (k t) -> p (b k) t", t=P))
            dve.wait_ge(*reached("vectors_turned", 1))
            link(dve.tensor_copy(vec[:, :], bank[4][:, 0:VA + VB + VC]))
            dve.tensor_scalar(one_less_ka, vec[:, VROWS["k_a"][0]:VROWS["k_a"][0] + RT], -1.0, 1.0, ALU.mult, ALU.add) \
               .then_inc(sig("one_less_ka_ready"), 1)
            st.end()
            dve_norm(dve, link, 0, lambda k: v("norm1_g", k))
            dve.drain().then_inc(sig("u_ready"), 1)
            st.end()
            mix = proj[:, 0:14, :]
            dve.tensor_scalar(shifted[:, :, 0:1], mix[:, :, 0:1], -1.0, None, ALU.mult)
            link(dve.tensor_tensor(shifted[:, :, 1:S], mix[:, :, 0:S - 1], mix[:, :, 1:S], ALU.subtract))
            for m in (12, 13, *range(12)):
                ins = dve.scalar_tensor_tensor(out=mix[:, m, :], in0=shifted[:, m, :], scalar=v("tshift_mu", m), in1=mix[:, m, :],
                                               op0=ALU.mult, op1=ALU.add)
            ins.then_inc(sig("token_shifted"), 1)
            dve.wait_ge(*reached("token_shifted", 1))
            for m in range(RT):
                ins = dve.tensor_scalar(kk[:, m, :], proj[:, T_K + m, :], v("k_k", m), None, ALU.mult)
            ins.then_inc(sig("kk_raw"), 1)
            dve.wait_ge(*reached("decay_sig", 4))
            link(dve.tensor_scalar(decay_log, decay_log, -float(np.exp(-0.5)), None, ALU.mult))
            for m in range(RT):
                for c in range(TB):
                    ins = dve.tensor_tensor_scan(cum[:, m, c * P:(c + 1) * P], const("ones"), decay_log[:, m, c * P:(c + 1) * P],
                                                 0.0, ALU.mult, ALU.add)
            link(ins)
            cums = cum.rearrange("p m (c t) -> p m c t", c=TB)
            link(dve.tensor_copy(cend, cums[:, :, :, P - 1]))
            link(dve.tensor_scalar(mid, cend, 0.5, None, ALU.mult))
            dve.tensor_tensor(carry, mid[:, :, 0], mid[:, :, 1], ALU.add)
            flat = cum.rearrange("p m (c t) -> p (m c) t", c=TB)
            dve.tensor_tensor(flat, flat, small[:, 8:16].rearrange("p (n o) -> p n o", o=1).to_broadcast([P, 8, P]), ALU.subtract) \
               .then_inc(sig("cum_ready"), 1)
            dve.wait_ge(*reached("cum_ready", 1))
            dve.tensor_tensor(cum_prev, cum, decay_log, ALU.subtract).then_inc(sig("cum_ready"), 1)
            dve.wait_ge(*reached("kk_norm", 1))
            link(dve.tensor_scalar(sq, sq, 1e-12, None, ALU.max))
            link(dve.reciprocal(sq, sq))
            link(dve.tensor_tensor(kk, kk, sq, ALU.mult))
            dve.wait_ge(*reached("exps", 3))
            tiles = lambda ap: ap.rearrange("p m (c t) -> p m c t", c=TB)
            for m in range(RT):
                dve.tensor_tensor(ar[:, m, :, 0, :], tiles(kk)[:, m], tiles(e3)[:, m], ALU.mult)
                dve.tensor_tensor(ar[:, m, :, 1, :], proj[:, T_R + m, :].rearrange("p (c t) -> p c t", c=TB), tiles(e1)[:, m], ALU.mult)
            link(dve.tensor_tensor(b_til, kk, a_gate, ALU.mult))
            dve.tensor_tensor(b_til, b_til, e2, ALU.mult).then_inc(sig("bk_ready"), 1)
            dve.wait_ge(*reached("k2_ready", 1))
            dve.tensor_tensor(k_til, k2, e2, ALU.mult).then_inc(sig("bk_ready"), 1)
            dve.wait_ge(*reached("bonus_summed", 1))
            dve.tensor_tensor(bonus, psum[:, 4:6, :].rearrange("p b (m t) -> p (b m) t", t=S), proj[:, T_V:T_V + RT, :], ALU.mult)
            st.end()
            if stages < 2:
                return
            for b in range(4):
                ch, m0 = batch(b)
                if b:
                    dve.wait_ge(*reached("y_made", b))
                for i in range(4):
                    dve.wait_ge(*reached("prods_made", 4 * b + i + 1))
                    dve.tensor_tensor(prods[:, i, :].rearrange("p (s n) -> p s n", s=2), bank[i].rearrange("p (s n) -> p s n", s=2),
                                      spread(const("upper"), 2), ALU.mult).then_inc(sig("prods_masked"), 1)
                dve.wait_ge(*reached("prods_masked", 4 * (b + 1)))
                rwkv_solver.dve(dve, link, b)
                if ch == 0:
                    dve.wait_ge(*reached("state_made", b + 1))
                    for i in range(2):
                        dve.scalar_tensor_tensor(out=state[:, m0 + i, :], in0=bank[6][:, i * P:(i + 1) * P], scalar=carry[:, m0 + i:m0 + i + 1],
                                                 in1=const("head_ones"), op0=ALU.mult, op1=ALU.mult).then_inc(sig("state_ready"), 1)
            y3 = y_tok.rearrange("p c n -> p (c n)").rearrange("p (g n) -> p g n", n=HD)
            yc = w4(0).rearrange("p m t -> p (m t)").rearrange("p (g n) -> p g n", n=HD)
            y2 = w4(1).rearrange("p m t -> p (m t)").rearrange("p (g n) -> p g n", n=HD)
            wide = lambda ap: ap.rearrange("p (g o) -> p g o", o=1).to_broadcast([P, 16, HD])
            dve.wait_ge(*reached("y_copied", 4))
            link(dve.tensor_reduce(stat, y3, AX.X, ALU.add))
            link(dve.tensor_scalar(stat, stat, 1.0 / HD, None, ALU.mult))
            dve.tensor_tensor(yc, y3, wide(stat), ALU.subtract).then_inc(sig("y_centred"), 1)
            dve.wait_ge(*reached("y_squared", 1))
            link(dve.tensor_reduce(stat2, y2, AX.X, ALU.add))
            dve.tensor_scalar(stat2, stat2, 1.0 / HD, 64e-5, ALU.mult, ALU.add).then_inc(sig("y_var"), 1)
            dve.wait_ge(*reached("y_std", 1))
            link(dve.reciprocal(stat2, stat2))
            dve.tensor_tensor(yc, yc, wide(stat2), ALU.mult).then_inc(sig("y_normed"), 1)
            dve.wait_ge(*reached("y_affine", 4))
            link(dve.tensor_tensor(y_rwkv, w4(2), bonus, ALU.add))
            dve.tensor_tensor(y_rwkv, y_rwkv, g_gate, ALU.mult)
            st.end()
            if stages < 3:
                return
            for i, t in enumerate(rope_tiles):
                n = t.shape[1]
                dve.wait_ge(*reached("rotated", i + 1))
                dve.wait_ge(*reached("rope_cos", i + 1))
                link(dve.tensor_tensor(t, bank[i][:, 0:n * S].rearrange("p (m t) -> p m t", t=S), spread(const("sin"), n), ALU.mult))
                dve.tensor_tensor(t, t, rope_tmp[:, i, 0:n * S].rearrange("p (m t) -> p m t", t=S), ALU.add)
            st.end()
            for b in range(TB):
                n = (b + 1) * P
                dve.wait_ge(*reached("idx_relu", 4 * (b + 1)))
                for hd in range(HEADS):
                    bk, half = place_of(hd)
                    src, w = pair_view(relu_s[:, bk, :], n)[:, half, :], w_idx[:, b, hd:hd + 1]
                    if hd == 0:
                        link(dve.tensor_scalar(score[:, 0:n], src, w, None, ALU.mult))
                    else:
                        link(dve.scalar_tensor_tensor(out=score[:, 0:n], in0=src, scalar=w, in1=score[:, 0:n], op0=ALU.mult, op1=ALU.add))
                dve.tensor_tensor(score[:, n - P:n], score[:, n - P:n], own_causal, ALU.add).then_inc(sig("idx_summed"), 1)
                dve.wait_ge(*reached("idx_summed", b + 1))
                left = score
                for _ in range(TOPK // 8):
                    link(dve.max(top8, left[:, 0:n]))
                    link(dve.match_replace(out=rest[:, 0:n], in_to_replace=top8, in_values=left[:, 0:n], imm_value=-3.0e38))
                    left = rest
                link(dve.tensor_tensor(sel_bias[:, 0:n], rest[:, 0:n], score[:, 0:n], ALU.not_equal))
                link(dve.tensor_scalar(sel_bias[:, 0:n], sel_bias[:, 0:n], -1.0, -NEG, ALU.add, ALU.mult))
                link(dve.tensor_tensor(sel_bias[:, n - P:n], sel_bias[:, n - P:n], own_causal, ALU.add))
                dve.wait_ge(*reached("att_scored", b + 1))
                for bk in range(4):
                    ins = dve.scalar_tensor_tensor(out=pair_view(logits[:, bk, :], n), in0=pair_view(bank[4 + bk], n), scalar=float(HD) ** -0.5,
                                                   in1=spread(sel_bias[:, 0:n], 2), op0=ALU.mult, op1=ALU.add)
                link(ins)
                link(dve.tensor_reduce(row_max, logits.rearrange("p b (i n) -> p (b i) n", i=2)[:, :, 0:n], AX.X, ALU.max))
                dve.tensor_scalar(row_max, row_max, -1.0, None, ALU.mult).then_inc(sig("row_max"), 1)
                dve.wait_ge(*reached("probs_made", HEADS * (b + 1)))
                link(dve.reciprocal(row_sum, row_sum))
                dve.wait_ge(*reached("att_made", b + 1))
                dve.tensor_tensor(att_tok.rearrange("p (i d) -> p i d", d=HD), bank[4].rearrange("p (i d) -> p i d", d=HD),
                                  row_sum.rearrange("p (i o) -> p i o", o=1).to_broadcast([P, HEADS, HD]), ALU.mult).then_inc(sig("att_normed"), 1)
            st.end()
            def gated(c, src):
                return dve.tensor_tensor(merged[:, 4 * c:4 * c + 4, :], src, proj[:, T_GATE + 4 * c:T_GATE + 4 * c + 4, :], ALU.mult)

            place = Stream()
            place.skip(23)
            evacuate(dve, place, 2, gated, banks=2)
            dve.wait_ge(evacuated, place.linear + 2)
            add_gated(dve, place, T_GATE + KD)
            evacuate(dve, place, 4, lambda c, src: dve.tensor_tensor(h[:, 2 * c:2 * c + 2, :], src, h[:, 2 * c:2 * c + 2, :], ALU.add))
            st.end()
            dve.drain().then_inc(sig("pair_evacuated"), 3)
            dve_norm(dve, link, 1, lambda k: v("norm2_g", k))
            dve.drain().then_inc(sig("u_ready"), 1)

            def up_product(at):
                if at.j % 2 == 1:
                    dve.wait_ge(multiplied, at.n + 1)
                    dve.wait_ge(*reached("gate_silu", at.pair + 1))
                    dst = hidden[:, bass.ds(at.pair * 2, 2), :]
                    dve.tensor_tensor(dst, dst, bank[at.j // 2 % 3 * 2 + 1].rearrange("p (m t) -> p m t", t=S), ALU.mult) \
                       .then_inc(sig("pair_evacuated"), 1)
            sweep(dve, place, 2 * (DFF // CH), up_product, linear=False)
            place.skip(DFF // (2 * P), False)
            dve.wait_ge(multiplied, place.n)
            link(dve.tensor_tensor(h[:, :, :], h[:, :, :], psum[:, 0:4, :].rearrange("p b (m t) -> p (b m) t", t=S), ALU.add))
            dve.drain().then_inc(sig("h_ready"), 1)
            dve.wait_ge(*reached("h_ready", 1))
            dve_norm(dve, link, 2, lambda k: v("normf_g", k), dst=h)
            st.end()
            place.skip(24, False)
            dve.drain().then_inc(sig("ada_free"), 1)
            base = place.n - 24
            with dve.Fori(0, 24 // SLOTS) as it:
                dve.wait_ge(multiplied, it * SLOTS + base + SLOTS)
                dve.tensor_tensor(mods[:, bass.ds(it * 12, 12)], bank[0][:, 0:12], vec[:, bass.ds(it * 12 + VA, 12)], ALU.add) \
                   .then_inc(sig("ada_free"), 1)
            dve.wait_ge(*reached("ada_free", 1 + 24 // SLOTS))
            for gain, name, at in ((gain1, "g_mix_2", KD), (gain2, "g_ffn_2", 4 * KD)):
                link(dve.tensor_scalar(gain, mods[:, at:at + KD], 1.0, None, ALU.add))
                link(dve.tensor_tensor(gain, gain, vec[:, VROWS[name][0]:VROWS[name][0] + KD], ALU.mult))
            st.end()
            if stages < 7:
                return
            dve_norm(dve, link, 3, lambda k: gain1[:, k:k + 1], lambda k: mods[:, k:k + 1])
            dve.drain().then_inc(sig("u_ready"), 1)
            place.skip(42)
            st.end()
            if stages < 8:
                return
            def tap(j, tile):
                at = VA + VB + j * 3 * GH + tile
                return vec[:, at:at + 1]
            for i, un in enumerate(conv_units):
                acc = w4(un)
                for m in range(4):
                    tile = 4 * i + m
                    link(dve.tensor_scalar(acc[:, m, :], proj[:, tile, :], tap(3, tile), None, ALU.mult))
                    for back in range(1, 4):
                        ins = dve.scalar_tensor_tensor(out=acc[:, m, back:S], in0=proj[:, tile, 0:S - back], scalar=tap(3 - back, tile),
                                                       in1=acc[:, m, back:S], op0=ALU.mult, op1=ALU.add)
                        if back < 3 or m < 3:
                            link(ins)
                ins.then_inc(sig("conv_summed"), 1)
            dve.wait_ge(*reached("rates_loaded", 32))
            link(dve.tensor_scalar(rate_rows, rate_rows, dt_col, None, ALU.add))
            dve.scalar_tensor_tensor(out=soft_rows, in0=rate_rows, scalar=-1.0, in1=rate_rows, op0=ALU.mult, op1=ALU.max).then_inc(sig("soft_abs"), 1)
            link(dve.tensor_scalar(rate_rows, rate_rows, 0.0, None, ALU.max))
            dve.wait_ge(*reached("soft_exp", 1))
            dve.tensor_scalar(soft_rows, soft_rows, 1.0, None, ALU.add).then_inc(sig("soft_one"), 1)
            dve.wait_ge(*reached("soft_ln", 1))
            link(dve.tensor_tensor(rate_rows, rate_rows, soft_rows, ALU.add))
            dve.wait_ge(*reached("rate_exp", 1))
            link(dve.tensor_scalar(rate_rows, rate_rows, rate_col, -1.0, ALU.mult, ALU.mult))
            for c in range(TB):
                at = slice(c * P, (c + 1) * P)
                dve.tensor_tensor_scan(gc_rows[:, at], const("ones", GH), rate_rows[:, at], 0.0, ALU.mult, ALU.add)
            dve.wait_ge(*reached("qk_row_sums", 1))
            dve.tensor_scalar(norm_rows[0:16, :], bank[0][0:16, 0:S], 1e-6, None, ALU.add).then_inc(sig("qk_var"), 1)
            dve.wait_ge(*reached("qk_root", 1))
            link(dve.reciprocal(norm_rows[0:16, :], norm_rows[0:16, :]))
            link(dve.tensor_scalar(norm_rows[0:8, :], norm_rows[0:8, :], float(P) ** -0.5, None, ALU.mult))
            st.end()
            def pair_of_heads(src):
                return src.rearrange("p (h c t) -> p h c t", h=2, c=TB)
            tiles = lambda base, i: proj[:, base + 2 * i:base + 2 * i + 2, :].rearrange("p h (c t) -> p h c t", c=TB)
            for i in range(4):
                dve.wait_ge(*reached("spread", 3 * i + 1))
                for hh in range(2):
                    dve.tensor_tensor(kq[:, 2 * i + hh, :, 1, :], tiles(T_GQ, i)[:, hh], pair_of_heads(bank[1])[:, hh], ALU.mult) \
                       .then_inc(sig("spread_used"), 1)
                dve.wait_ge(*reached("spread", 3 * i + 2))
                link(dve.tensor_tensor(tiles(T_GK, i), tiles(T_GK, i), pair_of_heads(bank[2]), ALU.mult))
                dve.wait_ge(*reached("spread", 3 * i + 3))
                for hh in range(2):
                    dve.tensor_tensor(kq[:, 2 * i + hh, :, 0, :], tiles(T_GK, i)[:, hh], pair_of_heads(bank[3])[:, hh], ALU.mult) \
                       .then_inc(sig("spread_used"), 1)
            dve.wait_ge(*reached("spread_used", 16))
            dve.drain().then_inc(sig("keys_ready"), 1)
            dve.wait_ge(*reached("cols_copied", 2))
            for c in range(TB):
                dve.wait_ge(*reached("gv_turned", c + 1))
                src = psum[:, 4 + 2 * c:6 + 2 * c, :].rearrange("p b (h n) -> p (b h) n", n=P)
                dve.tensor_tensor(vb_tok[:, c], src, beta_col[:, c, :].rearrange("p (h o) -> p h o", o=1).to_broadcast([P, GH, P]), ALU.mult) \
                   .then_inc(sig("vb_ready"), 1)
            dve.wait_ge(*reached("rows_turned", 1))
            dve.tensor_tensor(kd_col, bank[0][:, 64:72], gc_col[:, 0, :], ALU.subtract).then_inc(sig("kd_log"), 1)
            dve.wait_ge(*reached("kd_ready", 1))
            dve.wait_ge(*reached("gk_turned", 1))
            dve.tensor_tensor(kd_tok, psum[:, 4:6, :].rearrange("p b (h n) -> p (b h) n", n=P),
                              kd_col.rearrange("p (h o) -> p h o", o=1).to_broadcast([P, GH, P]), ALU.mult)
            st.end()
            for b in range(4):
                ch, h0 = b // 2, 4 * (b % 2)
                dve.wait_ge(*reached("gc_spread", b + 1))
                if b:
                    dve.wait_ge(*reached("g_solved", b))
                for i in range(4):
                    ins = dve.tensor_scalar(heads4(g_xs)[:, i, :], bank[7][:, i * P:(i + 1) * P], gc_col[:, ch, h0 + i:h0 + i + 1], 0.0,
                                            ALU.subtract, ALU.min)
                ins.then_inc(sig("decay_log"), 1)
                dve.wait_ge(*reached("decay_masked", b + 1))
                dve.wait_ge(*reached("g_prods_made", b + 1))
                if b:
                    dve.wait_ge(*reached("g_out_made", b))
                dve.tensor_tensor(g_prods, psum[:, 0:2, :].rearrange("p b (h s t) -> p (b h) s t", h=2, s=2), decays, ALU.mult) \
                   .then_inc(sig("g_prods_ready"), 1)
                dve.wait_ge(*reached("g_prods_ready", b + 1))
                if ch:
                    dve.wait_ge(*reached("eg_ready", b - 1))
                    eg = heads4(egrow)
                    for sd in range(2):
                        ins = dve.tensor_tensor(kq[:, h0:h0 + 4, 1, sd, :], kq[:, h0:h0 + 4, 1, sd, :], eg, ALU.mult)
                    ins.then_inc(sig("kq_decayed"), 1)
                g_solver.dve(dve, link, 4 + b)
                if ch:
                    dve.wait_ge(*reached("g_carried", b - 1))
                    dve.tensor_tensor(heads4(g_xs), vb_tok[:, 1, h0:h0 + 4, :], heads4(bank[7]), ALU.subtract).then_inc(sig("g_right"), 1)
                else:
                    dve.wait_ge(*reached("g_state_made", b + 1))
                    dve.tensor_copy(g_state[:, h0:h0 + 4, :], heads4(bank[6])).then_inc(sig("g_state_ready"), 1)
            st.end()
            dve.wait_ge(*reached("o_row_sums", 1))
            dve.tensor_scalar(norm_rows[0:8, :], bank[0][0:8, 0:S], 1.0 / P, 1e-6, ALU.mult, ALU.add).then_inc(sig("o_var"), 1)
            dve.wait_ge(*reached("o_root", 1))
            dve.reciprocal(norm_rows[0:8, :], norm_rows[0:8, :]).then_inc(sig("o_inverse"), 1)
            for i in range(4):
                dve.wait_ge(*reached("o_spread", i + 1))
                tl = slice(2 * i, 2 * i + 2)
                link(dve.tensor_tensor(o_gdn[:, tl, :], o_gdn[:, tl, :], bank[1 + i].rearrange("p (m t) -> p m t", t=S), ALU.mult))
                dve.scalar_tensor_tensor(out=y_gdn[:, tl, :], in0=o_gdn[:, tl, :], scalar=v("gdn_norm_g_2"), in1=y_gdn[:, tl, :],
                                         op0=ALU.mult, op1=ALU.mult)
            st.end()
            if stages < 9:
                return
            dve.wait_ge(*reached("d_row_sums", 1))
            dve.tensor_scalar(norm_rows[0:24, :], bank[0][0:24, 0:S], 1.0 / P, 1e-6, ALU.mult, ALU.add).then_inc(sig("d_var"), 1)
            dve.wait_ge(*reached("d_root", 1))
            dve.reciprocal(norm_rows[0:24, :], norm_rows[0:24, :]).then_inc(sig("d_inverse"), 1)
            for i in range(12):
                dve.wait_ge(*reached("d_spread", i + 1))
                tl = proj[:, T_DQ + 2 * i:T_DQ + 2 * i + 2, :]
                gain = v("dil_q_norm_g_2" if i < 6 else "dil_k_norm_g_2")
                dve.scalar_tensor_tensor(out=tl, in0=tl, scalar=gain, in1=bank[i % 2].rearrange("p (m t) -> p m t", t=S), op0=ALU.mult, op1=ALU.mult) \
                   .then_inc(sig("d_normed"), 1)
            st.end()
            for i, (b, slot_) in enumerate(dil_items):
                n = (b + 1) * P
                at = slot_ + 4 * b
                mask = dil_masks[:, :, P * (1 - b):2 * P]
                dve.wait_ge(*reached("d_scored", i + 1))
                if i >= 2:
                    dve.wait_ge(*reached("d_probs_made", i - 1))
                src = psum[:, 2 * (i % 2):2 * (i % 2) + 2, :].rearrange("p b n -> p (b n)")[:, 0:768].rearrange("p (g n) -> p g n", g=3)[:, :, 0:n]
                dve.scalar_tensor_tensor(out=d_logits[i % 2][:, :, 0:n], in0=src, scalar=float(P) ** -0.5, in1=mask, op0=ALU.mult, op1=ALU.add) \
                   .then_inc(sig("d_logits_ready"), 1)
                dve.wait_ge(*reached("d_logits_ready", i + 1))
                link(dve.tensor_reduce(d_max[:, at:at + 1], d_logits[i % 2][:, :, 0:n], AX.XY, ALU.max))
                dve.tensor_scalar(d_max[:, at:at + 1], d_max[:, at:at + 1], -1.0, None, ALU.mult).then_inc(sig("d_max_ready"), 1)
                if slot_ == 3:
                    dve.wait_ge(*reached("d_probs_made", i + 1))
                    link(dve.reciprocal(d_sum[:, 4 * b:4 * b + 4], d_sum[:, 4 * b:4 * b + 4]))
                    dve.wait_ge(*reached("d_mixed", i + 1))
                    if b:
                        dve.wait_ge(*reached("d_turned", b))
                    dve.tensor_tensor(heads4(d_tok), heads4(bank[6]), d_sum[:, 4 * b:4 * b + 4].rearrange("p (h o) -> p h o", o=1).to_broadcast([P, 4, P]),
                                      ALU.mult).then_inc(sig("d_scaled"), 1)
            st.end()
            if stages < 10:
                return
            place.skip(0)
            evacuate(dve, place, 4, lambda c, src: dve.tensor_tensor(merged[:, 2 * c:2 * c + 2, :], src, proj[:, T_GATE2 + 2 * c:T_GATE2 + 2 * c + 2, :], ALU.mult))
            dve.wait_ge(evacuated, place.linear + 2)
            add_gated(dve, place, T_GATE2 + KD)
            for c in range(4):
                lin = place.linear + c
                dve.wait_ge(multiplied, place.n + c + 1)
                for m in range(2):
                    k = 2 * c + m
                    ins = dve.scalar_tensor_tensor(out=h[:, k, :], in0=bank[lin % 2][:, m * S:(m + 1) * S], scalar=mods[:, 2 * KD + k:2 * KD + k + 1],
                                                   in1=h[:, k, :], op0=ALU.mult, op1=ALU.add)
                ins.then_inc(evacuated, 1)
            place.skip(4)
            st.end()
            if stages < 11:
                return
            dve_norm(dve, link, 4, lambda k: gain2[:, k:k + 1], lambda k: mods[:, 3 * KD + k:3 * KD + k + 1])
            dve.drain().then_inc(sig("u_ready"), 1)
            dve.wait_ge(*reached("router_loaded", 32))
            dve.wait_ge(*reached("scores_ready", 1))
            link(dve.tensor_tensor(sel_e, sc_e, spread(router_b, TB), ALU.add))
            for b in range(TB):
                for g in range(GROUPS):
                    ins = dve.max(best_e[:, b, g, :], sel_e[:, b, g * 8:(g + 1) * 8])
            link(ins)
            link(dve.tensor_tensor(gs_e, best_e[:, :, :, 0], best_e[:, :, :, 1], ALU.add))
            for b in range(TB):
                other = gs_e[:, b, :].rearrange("p (o j) -> p o j", o=1).to_broadcast([P, GROUPS, GROUPS])
                mine = gs_e[:, b, :].rearrange("p (g o) -> p g o", o=1).to_broadcast([P, GROUPS, GROUPS])
                dve.tensor_tensor(more_e, other, mine, ALU.is_gt)
                link(dve.tensor_tensor(same_e, other, mine, ALU.is_equal))
                link(dve.tensor_tensor(same_e, same_e, const("before").rearrange("p (g j) -> p g j", g=GROUPS), ALU.mult))
                link(dve.tensor_tensor(more_e, more_e, same_e, ALU.add))
                link(dve.tensor_reduce(rank_e, more_e, AX.X, ALU.add))
                link(dve.tensor_scalar(rank_e, rank_e, float(TOP_G), None, ALU.is_lt))
                keep = rank_e.rearrange("p (g o) -> p g o", o=1).to_broadcast([P, GROUPS, 8])
                eight = lambda ap: ap.rearrange("p (g n) -> p g n", g=GROUPS)
                link(dve.tensor_tensor(eight(sel_e[:, b, :]), eight(sel_e[:, b, :]), keep, ALU.mult))
                link(dve.tensor_scalar(rank_e, rank_e, -1.0, -NEG, ALU.add, ALU.mult))
                link(dve.tensor_tensor(eight(sel_e[:, b, :]), eight(sel_e[:, b, :]), keep, ALU.add))
                link(dve.max(top_e, sel_e[:, b, :]))
                link(dve.match_replace(out=left_e[:, b, :], in_to_replace=top_e, in_values=sel_e[:, b, :], imm_value=-3.0e38))
                link(dve.tensor_tensor(comb_e[:, b, :], left_e[:, b, :], sel_e[:, b, :], ALU.not_equal))
                link(dve.tensor_tensor(comb_e[:, b, :], comb_e[:, b, :], sc_e[:, b, :], ALU.mult))
                link(dve.tensor_reduce(sum_e, comb_e[:, b, :], AX.X, ALU.add))
                link(dve.reciprocal(sum_e, sum_e))
                dve.tensor_scalar(comb_e[:, b, :], comb_e[:, b, :], sum_e, ROUTE_SCALE, ALU.mult, ALU.mult).then_inc(sig("combine_ready"), 1)
                dve.wait_ge(*reached("combine_ready", b + 1))
            dve.drain().then_inc(sig("au_free"), 2)
            dve.drain().then_inc(sig("hid_ready"), 1)

            dve_experts(dve, place)
            st.end()
            for k in range(KD):
                ins = dve.scalar_tensor_tensor(out=h[:, k, :], in0=bank[k // 2][:, k % 2 * S:(k % 2 + 1) * S], scalar=mods[:, 5 * KD + k:5 * KD + k + 1],
                                               in1=h[:, k, :], op0=ALU.mult, op1=ALU.add)
            ins.then_inc(sig("h_final"), 1)
            dve.wait_ge(*reached("out_turned", 2))
            dve.tensor_copy(out_tok[:, 1, :], psum[:, 6:8, :].rearrange("p b n -> p (b n)")).then_inc(sig("out_ready_1"), 1)
            st.end()

        @block.tensor
        def _(pe):
            st = Stages(pe)
            place = Stream()
            pe.wait_ge(*reached("x_loaded", 16))
            pe.wait_ge(*reached("consts_loaded", 16))
            x_tok = work[:, 0:2, :]
            for b in range(TB):
                for k in range(KD):
                    last = pe.transpose(bank[2 * b + k // 4][:, k % 4 * P:(k % 4 + 1) * P], x_tok[:, b, k * P:(k + 1) * P], ident)
                last.then_inc(sig("x_turned"), 1)
            pe.wait_ge(*reached("vectors_loaded", 16 * (len(VROWS) + 2)))
            stage = work[:, 2, :]
            for n, at, o in ((VA, 0, 0), (VB, P, VA), (VC, 2 * P, VA + VB)):
                last = pe.transpose(bank[4][:, o:o + n], stage[0:n, at:at + P], ident[0:n, 0:n])
            last.then_inc(sig("vectors_turned"), 1)
            st.end()
            pe_norm(pe, 0)
            pe.wait_ge(*reached("u_ready", 1))
            pe.wait_ge(*reached("idxw_loaded", 16))
            for half in range(2):
                for k in range(KD):
                    last = pe.matmul(bank[4][64 * half:64 * half + 64, 0:S], idxw[:, k, 0:HD], u[:, k, :], start=(k == 0), stop=(k == KD - 1))
            last.then_inc(sig("idx_multiplied"), 1)
            for b in range(TB):
                for k in range(KD):
                    last = pe.matmul(bank[5][:, b * HEADS:(b + 1) * HEADS], u[:, k, b * P:(b + 1) * P], idxw[:, k, HD:HD + HEADS],
                                     start=(k == 0), stop=(k == KD - 1))
            last.then_inc(sig("idx_multiplied"), 1)
            pe_linear(pe, place, 23, u)
            st.end()
            pe.wait_ge(*reached("lora_loaded", 48))
            pe.wait_ge(*reached("token_shifted", 1))
            pe.wait_ge(*reached("lora_in", 2))
            for m in range(RT):
                at = slice(m % 2 * S, (m % 2 + 1) * S)
                pe.matmul(bank[m // 2][:, at], lora[0:64, 0, m * P:(m + 1) * P], tanh_wd[0:64, :], start=True, stop=True)
                pe.matmul(bank[2 + m // 2][:, at], lora[64:128, 0, m * P:(m + 1) * P], proj[64:128, T_WA, :], start=True, stop=True)
                last = pe.matmul(bank[4 + m // 2][:, at], lora[:, 1, m * P:(m + 1) * P], sig_gd, start=True, stop=True)
            last.then_inc(sig("lora_out"), 1)
            pe.wait_ge(*reached("kk_squared", 1))
            for m in range(RT):
                last = pe.matmul(bank[6 + m // 2][:, m % 2 * S:(m % 2 + 1) * S], const("head_ones"), sq[:, m, :], start=True, stop=True)
            last.then_inc(sig("kk_summed"), 1)
            pe.wait_ge(*reached("bonus_terms", 4))
            pe.wait_ge(*reached("g_copied", 1))
            for m in range(RT):
                last = pe.matmul(bank[4 + m // 2][:, m % 2 * S:(m % 2 + 1) * S], const("head_ones"), bonus[:, m, :], start=True, stop=True)
            last.then_inc(sig("bonus_summed"), 1)
            pe.wait_ge(*reached("decay_sig", 4))
            for c in range(TB):
                for m in range(RT):
                    last = pe.transpose(bank[c][:, m * P:(m + 1) * P], proj[:, T_V + m, c * P:(c + 1) * P], ident)
                last.then_inc(sig("v_turned"), 1)
            pe.wait_ge(*reached("a_gate_ready", 4))
            for i, til in enumerate((b_til, k_til)):
                pe.wait_ge(*reached("bk_ready", i + 1))
                for m in range(RT):
                    last = pe.transpose(bank[2 + i][:, m * P:(m + 1) * P], til[:, m, 0:P], ident)
                last.then_inc(sig("bk_turned"), 1)
            st.end()
            if stages < 2:
                return
            for b in range(4):
                ch, m0 = batch(b)
                for i in range(4):
                    m, half = m0 + i // 2, slice(64 * (i % 2), 64 * (i % 2) + 64)
                    if b:
                        pe.wait_ge(*reached("prods_masked", 4 * (b - 1) + i + 1))
                    rhs = ar[half, m, ch, :, :]
                    pe.matmul(bank[i][:, 0:256], b_til[half, m, ch * P:(ch + 1) * P], rhs, start=True, stop=True)
                    pe.matmul(bank[i][:, 256:512], k_til[half, m, ch * P:(ch + 1) * P], rhs, start=True, stop=True) \
                      .then_inc(sig("prods_made"), 1)
                rwkv_solver.pe(pe, b)
                if ch:
                    pe.wait_ge(*reached("state_ready", 4))
                    for i in range(2):
                        pe.matmul(bank[7][:, i * P:(i + 1) * P], ar[:, m0 + i, ch, 0, :], state[:, m0 + i, :],
                                  start=(i == 0), stop=False, skip_group_check=True)
                for i in range(4):
                    last = pe.matmul(bank[7][:, i * HD:(i + 1) * HD], prods[:, i, 256:384], v_tok[:, ch, m0 * P + i * HD:m0 * P + (i + 1) * HD],
                                     start=(ch == 0 and i == 0), stop=(i == 3), skip_group_check=True)
                last.then_inc(sig("x_made"), 1)
                pe.wait_ge(*reached("x_copied", b + 1))
                pe.wait_ge(*reached("inv_updated", 11 * (b + 1)))
                for i in range(4):
                    last = pe.matmul(bank[4][:, i * HD:(i + 1) * HD], inv_t[:, i * P:(i + 1) * P], xs[:, i * HD:(i + 1) * HD], start=True, stop=True)
                last.then_inc(sig("sa_made"), 1)
                pe.wait_ge(*reached("sa_copied", b + 1))
                first = True
                if ch:
                    for i in range(2):
                        pe.matmul(bank[5][:, i * P:(i + 1) * P], ar[:, m0 + i, ch, 1, :], state[:, m0 + i, :],
                                  start=(i == 0), stop=False, skip_group_check=True)
                    first = False
                for i in range(4):
                    pe.matmul(bank[5][:, i * HD:(i + 1) * HD], prods[:, i, 384:512], v_tok[:, ch, m0 * P + i * HD:m0 * P + (i + 1) * HD],
                              start=(first and i == 0), stop=False, skip_group_check=True)
                    last = pe.matmul(bank[5][:, i * HD:(i + 1) * HD], prods[:, i, 128:256], sa[:, i * HD:(i + 1) * HD],
                                     start=False, stop=(i == 3), skip_group_check=True)
                last.then_inc(sig("y_made"), 1)
                if ch == 0:
                    for i in range(2):
                        pe.matmul(bank[6][:, i * P:(i + 1) * P], bk_tok[:, 0, (m0 + i) * P:(m0 + i + 1) * P], sa[:, i * P:(i + 1) * P],
                                  start=True, stop=False)
                        last = pe.matmul(bank[6][:, i * P:(i + 1) * P], bk_tok[:, 1, (m0 + i) * P:(m0 + i + 1) * P],
                                         v_tok[:, ch, (m0 + i) * P:(m0 + i + 1) * P], start=False, stop=True)
                    last.then_inc(sig("state_made"), 1)
                    pe.wait_ge(*reached("state_ready", 2 * (b + 1)))
                pe.wait_ge(*reached("y_copied", b + 1))
            pe.wait_ge(*reached("y_normed", 1))
            for c in range(TB):
                for m in range(RT):
                    last = pe.transpose(bank[c][:, m * P:(m + 1) * P], w4(0).rearrange("p m t -> p (m t)")[:, c * RW + m * P:c * RW + (m + 1) * P], ident)
                last.then_inc(sig("y_turned"), 1)
            st.end()
            if stages < 3:
                return
            for i, t in enumerate(rope_tiles):
                n = t.shape[1] * S
                pe.matmul(bank[i][:, 0:n], const("rot"), t, start=True, stop=True).then_inc(sig("rotated"), 1)
            for c in range(TB):
                if c:
                    pe.wait_ge(*reached("att_v_copied", c))
                for m in range(RT):
                    last = pe.transpose(bank[7][:, m * P:(m + 1) * P], proj[:, T_AV + m, c * P:(c + 1) * P], ident)
                last.then_inc(sig("att_v_turned"), 1)
            st.end()
            for b in range(TB):
                n = (b + 1) * P
                if b:
                    pe.wait_ge(*reached("probs_t_ready", 1))
                pe_scores(pe, 0, T_QI, lambda hd: kidx, b, n).then_inc(sig("idx_scored"), 1)
                if b:
                    pe.wait_ge(*reached("att_normed", b))
                    pe.wait_ge(*reached("y_att_copied", b))
                pe_scores(pe, 4, T_Q, lambda hd: proj[:, T_AK + hd // 2, :], b, n).then_inc(sig("att_scored"), 1)
                pe.wait_ge(*reached("probs_made", HEADS * (b + 1)))
                for kb in range(b + 1):
                    for i in range(HEADS):
                        last = pe.transpose(bank[2 * kb + i // 4][:, i % 4 * P:(i % 4 + 1) * P],
                                            pair_view(probs[:, i // 2, :], n)[:, i % 2, kb * P:(kb + 1) * P], ident)
                last.then_inc(sig("probs_turned"), 1)
                pe.wait_ge(*reached("probs_t_ready", b * (b + 1) // 2 + b + 1))
                for i in range(HEADS):
                    hd = head_at(i)
                    for kb in range(b + 1):
                        last = pe.matmul(bank[4][:, hd * HD:(hd + 1) * HD], probs_t[:, kb, i, :], att_v[:, kb, hd * HD:(hd + 1) * HD],
                                         start=(kb == 0), stop=(kb == b))
                last.then_inc(sig("att_made"), 1)
                pe.wait_ge(*reached("att_normed", b + 1))
                for m in range(RT):
                    last = pe.transpose(bank[5][:, m * P:(m + 1) * P], att_tok[:, m * P:(m + 1) * P], ident)
                last.then_inc(sig("att_turned"), 1)
            st.end()
            pe_linear(pe, place, 2, y_rwkv, 4, RT)
            pe_linear(pe, place, 2, y_att, 4, RT)
            pe.wait_ge(*reached("merged_ready", 2))
            pe_linear(pe, place, 4, merged)
            st.end()
            pe_norm(pe, 1)
            pe.wait_ge(*reached("u_ready", 2))

            def gate_up(at):
                pe.wait_ge(fill[at.slot], at.filled)
                pe.wait_ge(*reached("pair_evacuated", at.pair + 1))
                dst = bank[at.j // 2 % 3 * 2 + at.j % 2]
                for m in range(2):
                    for k in range(KD):
                        last = pe.matmul(dst[:, m * S:(m + 1) * S], ring[:, at.slot, k * CH + m * P:k * CH + (m + 1) * P], u[:, k, :],
                                         start=(k == 0), stop=(k == KD - 1))
                last.then_inc(multiplied, 1)
            sweep(pe, place, 2 * (DFF // CH), gate_up, linear=False)
            pe.wait_ge(*reached("pair_evacuated", 3 + DFF // CH))

            def down(at):
                pe.wait_ge(fill[at.slot], at.filled)
                for kt in range(2):
                    for m in range(KD):
                        last = pe.matmul(bank[m // 2][:, m % 2 * S:(m % 2 + 1) * S], ring[:, at.slot, kt * D + m * P:kt * D + (m + 1) * P],
                                         hidden[:, 2 * at.c + kt, :], start=(at.c == 0 and kt == 0 and m % 2 == 0),
                                         stop=(at.c == DFF // (2 * P) - 1 and kt == 1), skip_group_check=True)
                last.then_inc(multiplied, 1)
            sweep(pe, place, DFF // (2 * P), down, linear=False)
            pe.wait_ge(*reached("h_ready", 1))
            pe_norm(pe, 2)
            st.end()
            pe.wait_ge(*reached("c_ready", 1))

            def modulate(at):
                pe.wait_ge(fill[at.slot], at.filled)
                if at.j == 0:
                    pe.wait_ge(*reached("ada_free", at.turn + 1))
                for m in range(2):
                    for k in range(KD):
                        last = pe.matmul(bank[0][:, 2 * at.j + m:2 * at.j + m + 1], ring[:, at.slot, k * CH + m * P:k * CH + (m + 1) * P],
                                         c_act[:, k:k + 1], start=(k == 0), stop=(k == KD - 1))
                last.then_inc(multiplied, 1)
            sweep(pe, place, 24, modulate, linear=False)
            st.end()
            if stages < 7:
                return
            pe_norm(pe, 3)
            pe.wait_ge(*reached("u_ready", 3))
            pe.wait_ge(*reached("ba_loaded", 16))
            for half in range(2):
                for k in range(KD):
                    last = pe.matmul(bank[4][0:8, half * S:(half + 1) * S], baw[:, k, half * 8:half * 8 + 8], u[:, k, :], start=(k == 0), stop=(k == KD - 1))
            last.then_inc(sig("ba_multiplied"), 1)
            pe_linear(pe, place, 42, u)
            st.end()
            if stages < 8:
                return
            pe.wait_ge(*reached("qk_squared", 4))
            for i in range(2 * GH):
                last = sum_to_row(pe, bank[0][0:32, 0:S], w4((0, 1, 2, 5)[i // 4])[:, i % 4, :], i, 2 * GH)
            last.then_inc(sig("qk_row_sums"), 1)
            st.end()
            for c in range(TB):
                pe.transpose(bank[0][:, c * GH:(c + 1) * GH], gc_rows[:, c * P:(c + 1) * P], ident[0:GH, 0:GH])
                pe.transpose(bank[0][:, 16 + c * GH:16 + (c + 1) * GH], beta_rows[:, c * P:(c + 1) * P], ident[0:GH, 0:GH])
            last = pe.matmul(bank[0][:, 64:72], gc_rows[:, P - 1:P].to_broadcast([GH, P]), ident[0:GH, 0:GH], start=True, stop=True)
            last.then_inc(sig("rows_turned"), 1)
            for c in range(TB):
                for hd in range(GH):
                    last = pe.transpose(bank[4 + 2 * c + hd // 4][:, hd % 4 * P:(hd % 4 + 1) * P], proj[:, T_GV + hd, c * P:(c + 1) * P], ident)
                last.then_inc(sig("gv_turned"), 1)
            for i in range(4):
                for kind in range(3):
                    if i:
                        pe.wait_ge(*reached("spread_used", 4 * (i - 1) + (2 if kind == 0 else 4)))
                    for hh in range(2):
                        hd = 2 * i + hh
                        dst = bank[1 + kind][:, hh * S:(hh + 1) * S]
                        if kind < 2:
                            last = row_to_all(pe, dst, norm_rows[0:16, :], kind * GH + hd, 16)
                        else:
                            last = row_to_all(pe, dst, beta_rows, hd, GH)
                    last.then_inc(sig("spread"), 1)
            pe.wait_ge(*reached("keys_ready", 1))
            pe.wait_ge(*reached("vb_ready", 1))
            for hd in range(GH):
                last = pe.transpose(bank[4 + hd // 4][:, hd % 4 * P:(hd % 4 + 1) * P], proj[:, T_GK + hd, 0:P], ident)
            last.then_inc(sig("gk_turned"), 1)
            st.end()
            for b in range(4):
                ch, h0 = b // 2, 4 * (b % 2)
                tok = slice(ch * P, (ch + 1) * P)
                if b:
                    pe.wait_ge(*reached("g_prods_ready", b))
                    pe.wait_ge(*reached("g_out_copied", b))
                    pe.wait_ge(*reached("g_state_ready", min(b, 2)))
                for i in range(4):
                    last = row_to_all(pe, bank[7][:, i * P:(i + 1) * P], gc_rows[:, tok], h0 + i, GH)
                last.then_inc(sig("gc_spread"), 1)
                for i in range(4):
                    last = pe.matmul(bank[i // 2][:, i % 2 * S:(i % 2 + 1) * S], proj[:, T_GK + h0 + i, tok], kq[:, h0 + i, ch, :, :], start=True, stop=True)
                last.then_inc(sig("g_prods_made"), 1)
                g_solver.pe(pe, 4 + b)
                pe.wait_ge(*reached("inv_updated", 11 * (5 + b)))
                if ch:
                    pe.wait_ge(*reached("eg_ready", b - 1))
                    pe.wait_ge(*reached("kq_decayed", b - 1))
                    for i in range(4):
                        last = pe.matmul(bank[7][:, i * P:(i + 1) * P], kq[:, h0 + i, ch, 0, :], g_state[:, h0 + i, :], start=True, stop=True)
                    last.then_inc(sig("g_carried"), 1)
                    pe.wait_ge(*reached("g_right", b - 1))
                for i in range(4):
                    rhs = heads4(g_xs)[:, i, :] if ch else vb_tok[:, ch, h0 + i, :]
                    last = pe.matmul(bank[4][:, i * P:(i + 1) * P], heads4(g_inv_t)[:, i, :], rhs, start=True, stop=True)
                last.then_inc(sig("g_solved"), 1)
                pe.wait_ge(*reached("g_new_copied", b + 1))
                new = heads4(g_upd)
                for i in range(4):
                    last = pe.matmul(bank[5][:, i * P:(i + 1) * P], new[:, i, :], g_prods[:, i, 1, :], start=True, stop=(ch == 0))
                    if ch:
                        last = pe.matmul(bank[5][:, i * P:(i + 1) * P], g_state[:, h0 + i, :], kq[:, h0 + i, ch, 1, :], start=False, stop=True)
                last.then_inc(sig("g_out_made"), 1)
                if ch == 0:
                    for i in range(4):
                        last = pe.matmul(bank[6][:, i * P:(i + 1) * P], kd_tok[:, h0 + i, :], new[:, i, :], start=True, stop=True)
                    last.then_inc(sig("g_state_made"), 1)
            st.end()
            pe.wait_ge(*reached("o_squared", 2))
            for i in range(GH):
                last = sum_to_row(pe, bank[0][0:32, 0:S], w4(i // 4)[:, i % 4, :], i, GH)
            last.then_inc(sig("o_row_sums"), 1)
            pe.wait_ge(*reached("o_inverse", 1))
            for i in range(4):
                for hh in range(2):
                    last = row_to_all(pe, bank[1 + i][:, hh * S:(hh + 1) * S], norm_rows[0:8, :], 2 * i + hh, 8)
                last.then_inc(sig("o_spread"), 1)
            st.end()
            if stages < 9:
                return
            for c in range(TB):
                for hd in range(DH):
                    n = c * DH + hd
                    last = pe.transpose(bank[2 + n // 4][:, n % 4 * P:(n % 4 + 1) * P], proj[:, T_DV + hd, c * P:(c + 1) * P], ident)
            last.then_inc(sig("d_v_turned"), 1)
            pe.wait_ge(*reached("d_squared", 6))
            for i in range(2 * DH):
                last = sum_to_row(pe, bank[0][0:32, 0:S], w4(i // 4)[:, i % 4, :], i, 2 * DH)
            last.then_inc(sig("d_row_sums"), 1)
            pe.wait_ge(*reached("d_inverse", 1))
            for i in range(DH):
                if i >= 2:
                    pe.wait_ge(*reached("d_normed", i - 1))
                for hh in range(2):
                    last = row_to_all(pe, bank[i % 2][:, hh * S:(hh + 1) * S], norm_rows[0:24, :], 2 * i + hh, 24)
                last.then_inc(sig("d_spread"), 1)
            st.end()

            def dil_scores(i):
                b, slot_ = dil_items[i]
                if i >= 2:
                    pe.wait_ge(*reached("d_logits_ready", i - 1))
                for g in range(3):
                    hd = 4 * g + slot_
                    last = pe.matmul(bank[2 * (i % 2) + g // 2][:, g % 2 * S:g % 2 * S + (b + 1) * P], proj[:, T_DQ + hd, b * P:(b + 1) * P],
                                     proj[:, T_DK + hd, 0:(b + 1) * P], start=True, stop=True)
                last.then_inc(sig("d_scored"), 1)
            dil_scores(0)
            for i, (b, slot_) in enumerate(dil_items):
                if i + 1 < len(dil_items):
                    dil_scores(i + 1)
                pe.wait_ge(*reached("d_probs_made", i + 1))
                if i:
                    pe.wait_ge(*reached("d_probs_t_ready", i))
                for g in range(3):
                    for kb in range(b + 1):
                        last = pe.transpose(bank[4 + g // 2][:, g % 2 * S + kb * P:g % 2 * S + (kb + 1) * P], d_probs[i % 2][:, g, kb * P:(kb + 1) * P], ident)
                last.then_inc(sig("d_probs_turned"), 1)
                pe.wait_ge(*reached("d_probs_t_ready", i + 1))
                if b and slot_ == 0:
                    pe.wait_ge(*reached("d_scaled", b))
                for g in range(3):
                    for kb in range(b + 1):
                        last = pe.matmul(bank[6][:, slot_ * P:(slot_ + 1) * P], d_probs_t[:, g, kb * P:(kb + 1) * P], dv_tok[:, kb, 4 * g + slot_, :],
                                         start=(g == 0 and kb == 0), stop=(g == 2 and kb == b))
                last.then_inc(sig("d_mixed"), 1)
                if slot_ == 3:
                    pe.wait_ge(*reached("d_scaled", b + 1))
                    if b:
                        pe.wait_ge(*reached("y_dil_ready", b))
                    for m in range(4):
                        last = pe.transpose(bank[7][:, m * P:(m + 1) * P], d_tok[:, m * P:(m + 1) * P], ident)
                    last.then_inc(sig("d_turned"), 1)
            st.end()
            if stages < 10:
                return
            pe_linear(pe, place, 4, y_gdn)
            pe_linear(pe, place, 2, y_dil, 4, 4)
            pe.wait_ge(*reached("merged_ready", 4))
            pe_linear(pe, place, 4, merged)
            st.end()
            if stages < 11:
                return
            pe_norm(pe, 4)
            pe.wait_ge(*reached("u_ready", 4))
            pe.wait_ge(*reached("router_loaded", 32))
            for b in range(TB):
                for k in range(KD):
                    last = pe.matmul(bank[0][:, b * EXPERTS:(b + 1) * EXPERTS], u[:, k, b * P:(b + 1) * P], router[:, k, :], start=(k == 0), stop=(k == KD - 1))
            last.then_inc(sig("routed"), 1)

            def into_hidden(at, e, par, kind):
                pe.wait_ge(fill[at.slot], at.filled)
                if kind == 0:
                    pe.wait_ge(*reached("au_free", e + 1))
                for m in range(2):
                    for k in range(KD):
                        last = pe.matmul(bank[4 + 2 * par + kind][:, m * S:(m + 1) * S], ring[:, at.slot, k * CH + m * P:k * CH + (m + 1) * P],
                                         u[:, k, :], start=(k == 0), stop=(k == KD - 1))
                last.then_inc(multiplied, 1)

            def from_hidden(at, e, par, first=False, end=False):
                pe.wait_ge(fill[at.slot], at.filled)
                pe.wait_ge(*reached("hid_ready", e + 2))
                for kt in range(2):
                    for m in range(KD):
                        last = pe.matmul(bank[m // 2][:, m % 2 * S:(m % 2 + 1) * S], ring[:, at.slot, kt * D + m * P:kt * D + (m + 1) * P],
                                         hid_e[par][:, kt * S:(kt + 1) * S], start=(first and kt == 0 and m % 2 == 0), stop=(end and kt == 1),
                                         skip_group_check=True)
                last.then_inc(multiplied, 1)

            sweep(pe, place, 2, lambda at: into_hidden(at, 0, 0, at.c), linear=False)
            pe.wait_ge(*reached("combine_ready", 2))
            for b in range(TB):
                last = pe.transpose(bank[0][0:EXPERTS, b * P:(b + 1) * P], comb_e[:, b, :], ident)
            last.then_inc(sig("combine_turned"), 1)
            pe.wait_ge(*reached("combine_copied", 1))

            def expert_chunk(at):
                x, par = at.third, at.j // 3 % 2
                if at.j % 3 < 2:
                    into_hidden(at, x + 1, 1 - par, at.j % 3)
                else:
                    from_hidden(at, x, par, first=isinstance(x, int) and x == 0)
            sweep(pe, place, SLOTS, expert_chunk, linear=False)
            sweep(pe, place, 3 * EXPERTS - SLOTS, lambda at: expert_chunk(later(at)), linear=False)
            sweep(pe, place, 1, lambda at: from_hidden(at, EXPERTS, EXPERTS % 2, end=True), linear=False)
            st.end()
            pe.wait_ge(*reached("h_final", 1))
            for b in range(TB):
                for k in range(KD):
                    last = pe.transpose(bank[4 + 2 * b + k // 4][:, k % 4 * P:(k % 4 + 1) * P], h[:, k, b * P:(b + 1) * P], ident)
                last.then_inc(sig("out_turned"), 1)
            st.end()


def kernel(**inputs):
    import concourse.bacc as _bacc
    from concourse.bass_utils import run_bass_kernel_spmd as _run

    nc = _bacc.Bacc("TRN2", target_bir_lowering=False, num_devices=1)
    arrays = {f"in_{name}": np.ascontiguousarray(a) for name, a in inputs.items()}
    arrays["in_consts"] = constants()
    args = {name[3:]: nc.dram_tensor(name, a.shape, F32, kind="ExternalInput").ap() for name, a in arrays.items()}
    out = nc.dram_tensor("out", (1, S, D), F32, kind="ExternalOutput").ap()
    build(nc, args, out)
    r = _run(nc, [arrays], core_ids=[0])
    return r.results[0]["out"]
```

```python
from contextlib import ExitStack

import numpy as np

import concourse.bass as bass
from concourse import mybir

F32 = mybir.dt.float32
F32R = mybir.dt.float32r
ACT = mybir.ActivationFunctionType
ALU = mybir.AluOpType
AX = mybir.AxisListType

P = 128
D = 1024
S = 256
KD = D // P
TB = S // P
HEADS = 8
HD = 64
RW = HEADS * HD
RT = RW // P
DFF = 2816
TOPK = 64
NEG = -1.0e30

RWKV_COLS = 3 * RW + 64 + 64 + 128
ATT0 = RWKV_COLS
IDXQ0 = ATT0 + 3 * RW
IDXK0 = IDXQ0 + HEADS * HD
GATE0 = IDXK0 + HD + HEADS

T_R, T_K, T_V, T_WA, T_G = 0, 4, 8, 12, 13
T_Q, T_AK, T_AV, T_QI, T_GATE = 14, 18, 22, 26, 30

SLOTS = 6
SLOT = 2048
CH = 256

GH = 8
DH = 12
GDN_COLS = 4 * GH * P
DIL0 = GDN_COLS + 2 * GH
GATE0_2 = DIL0 + 3 * DH * P
T_GQ, T_GK, T_GV, T_GZ, T_DQ, T_DK, T_DV, T_GATE2 = 0, 8, 16, 24, 32, 44, 56, 68
EXPERTS = 64
DE = 256
TOP_E = 8
GROUPS = 8
TOP_G = 4
ROUTE_SCALE = 2.5

VROWS = {}
for _name, _rows in (("norm1_g", 8), ("tshift_mu", 14), ("w0", 4), ("a0", 4), ("k_k", 4), ("k_a", 4),
                     ("r_k", 4), ("lnx_g", 4), ("lnx_b", 4), ("norm2_g", 8), ("normf_g", 8),
                     ("g_mix_2", 8), ("g_ffn_2", 8), ("c_2", 8), ("gdn_norm_g_2", 1),
                     ("dil_q_norm_g_2", 1), ("dil_k_norm_g_2", 1)):
    VROWS[_name] = (sum(r for _, r in VROWS.values()), _rows)
VA = sum(r for _, r in VROWS.values())
VB = 6 * KD
VC = 4 * 3 * GH

CONST = {}


def constants():
    i = np.arange(P)
    s, t = i[:, None], i[None, :]
    parts = [("ident", s == t), ("ones", np.ones((P, P))),
             ("upper", np.concatenate([s < t, s <= t], 1))]
    for level in range(7):
        half = 1 << level
        pair = (s // (2 * half) == t // (2 * half)) & (s // half % 2 == 0) & (t // half % 2 == 1)
        parts.append((f"level{level}", pair))
    rot = np.zeros((P, P))
    for o in range(P):
        if o % HD < HD // 2:
            rot[o + HD // 2, o] = -1.0
        else:
            rot[o - HD // 2, o] = 1.0
    parts.append(("rot", rot))
    parts.append(("head_ones", s // HD == t // HD))
    inv = (np.float32(1.0) / (np.float32(10000.0) ** (np.arange(HD // 2, dtype=np.float32) * np.float32(2.0) / np.float32(HD)))).astype(np.float32)
    ang = np.arange(S, dtype=np.float32)[None, :] * inv[i % (HD // 2)][:, None]
    parts += [("cos", np.cos(ang)), ("sin", np.sin(ang))]
    parts.append(("before", np.tile((np.arange(8)[None, :] < np.arange(8)[:, None]).reshape(1, 64), (P, 1))))
    for g, (window, step) in enumerate(((128, 1), (512, 4), (2048, 16))):
        gap = s - np.arange(-P, P)[None, :]
        ok = (gap >= 0) & (gap <= window) & (gap % step == 0)
        parts.append((f"dil{g}", np.where(ok, 0.0, NEG)))
    parts.append(("pick", np.tile(np.arange(63)[None, :] == 31, (P, 1))))
    at = 0
    for name, a in parts:
        CONST[name] = (at, a.shape[1])
        at += a.shape[1]
    return np.concatenate([a.astype(np.float32) for _, a in parts], 1)


GROUPS_OF_SIGNALS = {
    "pe_turned": [("x_turned", 2), ("vectors_turned", 1), ("v_turned", 2), ("bk_turned", 2), ("y_turned", 2),
                  ("att_v_turned", 2), ("rows_turned", 1), ("gv_turned", 2), ("gk_turned", 1), ("d_v_turned", 1),
                  ("combine_turned", 1), ("out_turned", 2)],
    "pe_sums_of_squares": [("square_sum_0", 1), ("kk_summed", 1), ("square_sum_1", 1), ("square_sum_2", 1),
                           ("square_sum_3", 1), ("qk_row_sums", 1), ("head_sums", 1),
                           ("square_sum_4", 1)],
    "act_squares": [("squares_act_0", 1), ("kk_squared", 1), ("y_squared", 1), ("squares_act_1", 1),
                    ("squares_act_2", 1), ("squares_act_3", 1), ("qk_squared", 4), ("head_squared", 8), ("squares_act_4", 1)],
    "act_roots": [("root_0", 1), ("kk_norm", 1), ("y_std", 1), ("root_1", 1), ("root_2", 1), ("root_3", 1),
                  ("qk_root", 1), ("head_root", 1), ("root_4", 1)],
    "dve_variances": [("variance_0", 1), ("y_var", 1), ("variance_1", 1), ("variance_2", 1), ("variance_3", 1),
                      ("qk_var", 1), ("head_var", 1), ("variance_4", 1)],
    "dve_logs": [("soft_abs", 1), ("soft_one", 1), ("kd_log", 1)],
    "act_exps": [("rate_exp", 1), ("soft_exp", 1), ("soft_ln", 1), ("kd_ready", 1)],
    "products_made": [("prods_made", 16), ("g_prods_made", 4)],
    "carried_made": [("x_made", 4), ("g_carried", 2)],
    "solution_made": [("sa_made", 4), ("g_solved", 4)],
    "solution_copied": [("sa_copied", 4), ("g_new_copied", 4)],
    "output_made": [("y_made", 4), ("g_out_made", 4)],
    "output_copied": [("y_copied", 4), ("g_out_copied", 4)],
    "state_multiplied": [("state_made", 2), ("g_state_made", 2)],
    "state_written": [("state_ready", 4), ("g_state_ready", 2)],
    "logits_made": [("att_scored", 2), ("d_scored", 8)],
    "maximum_ready": [("row_max", 2), ("d_max_ready", 8)],
    "exps_made": [("probs_made", 16), ("d_probs_made", 8)],
    "exps_turned": [("probs_turned", 2), ("d_probs_turned", 8)],
    "exps_copied": [("probs_t_ready", 3), ("d_probs_t_ready", 8)],
    "mix_made": [("att_made", 2), ("d_mixed", 8)],
    "mix_normed": [("att_normed", 2), ("d_scaled", 2)],
    "mix_turned": [("att_turned", 2), ("d_turned", 2)],
    "mix_copied": [("y_att_copied", 2), ("y_dil_ready", 2)],
}
IN_GROUP = {name: (group, sum(n for _, n in names[:i]))
            for group, names in GROUPS_OF_SIGNALS.items() for i, (name, _) in enumerate(names)}


class Chain:

    def __init__(self, eng, sem):
        self.eng, self.sem, self.n = eng, sem, 0

    def __call__(self, ins):
        self.n += 1
        ins.then_inc(self.sem, 1)
        self.eng.wait_ge(self.sem, self.n)


def build(nc, fp, out):
    ctx = ExitStack()
    with ctx:
        def sb(name, shape):
            return ctx.enter_context(nc.sbuf_tensor(name, shape, F32))

        def sb_two(name, shape):
            raw = nc.sbuf_tensor(name, shape, F32)
            plain = raw.__enter__()
            raw.__exit__(None, None, None)
            return plain, ctx.enter_context(nc.sbuf_tensor(f"{name}_r", shape, F32R))

        sems = {}

        def sig(name):
            name = IN_GROUP.get(name, (name, 0))[0]
            if name not in sems:
                sems[name] = ctx.enter_context(nc.semaphore(name))
            return sems[name]

        def reached(name, n):
            return sig(name), n + IN_GROUP.get(name, (name, 0))[1]

        ncst = fp["consts"].shape[1]
        cst = sb("cst", [P, ncst])
        ring, ring_r = sb_two("ring", [P, SLOTS, SLOT])
        h = sb("h", [P, KD, S])
        u = sb("u", [P, KD, S])
        proj, proj_r = sb_two("proj", [P, 84, S])
        work = sb("work", [P, 10, 1024])
        vec = sb("vec", [P, VA + VB + VC])
        rs = sb("rs", [P, S])
        small = sb("small", [P, 256])
        delta = sb("delta", [P, KD, S])
        lora = work[:, 9, :].rearrange("p (s n) -> p s n", s=2)
        idxw = work[:, 3, 0:KD * (HD + HEADS)].rearrange("p (k n) -> p k n", k=KD)
        psum = ctx.enter_context(nc.psum_tensor("psum", [P, 8, 512], F32))
        bank = [psum[:, b, :] for b in range(8)]

        def const(name, rows=P):
            at, n = CONST[name]
            return cst[0:rows, at:at + n]

        ident = const("ident")

        def v(name, k=0):
            if name == "b_ada_2":
                at = VA
            elif name == "conv":
                at = VA + VB
            else:
                at = VROWS[name][0]
            return vec[:, at + k:at + k + 1]

        def unit(i):
            return proj[:, 46 + 4 * i:50 + 4 * i, :]

        def w4(i):
            return work[:, i, :].rearrange("p (m t) -> p m t", m=4)

        def halves(ap):
            flat = ap.rearrange("p m t -> p (m t)")
            return flat[:, 0:512], flat[:, 512:1024]

        fill = [sig(f"slot_filled_{j}") for j in range(SLOTS)]
        multiplied = sig("chunks_multiplied")
        evacuated = sig("chunks_evacuated")

        class Stream:

            def __init__(self):
                self.n = self.linear = self.split = 0

            def skip(self, count, linear=True, split=False):
                self.n += count
                self.linear += count * linear
                self.split += count * split

        class Chunk:

            def __init__(self, place, c, j, it):
                self.c, self.j = c, j
                self.pair = c // 2 if it is None else it * (SLOTS // 2) + j // 2
                self.third = c // 3 if it is None else it * (SLOTS // 3) + j // 3
                self.slot = (place.n + j) % SLOTS
                self.filled = ((place.n + j) // SLOTS + 1) * 16 + (0 if it is None else it * 16)
                self.n = c + place.n
                self.linear = c + place.linear
                self.turn_of_two = j // 6 if it is None else it
                self.parity = (place.linear + j) % 2
                self.split = c + place.split
                self.buffer = (place.split + j) % 2
                self.after = lambda: Chunk(place, c + 1, j + 1, it)

        def sweep(eng, place, count, body, linear=True, split=False):
            turns = count // SLOTS
            done = 0
            if turns > 1:
                with eng.Fori(0, turns) as it:
                    for j in range(SLOTS):
                        body(Chunk(place, it * SLOTS + j, j, it))
                done = turns * SLOTS
            for j in range(done, count):
                body(Chunk(place, j, j, None))
            place.skip(count, linear, split)

        hi_made, lo_ready = sig("heads_made"), sig("rests_made")
        INPUTS_BEFORE = {"u0": 0, "out": 2, "u1": 6, "u2": 8, "out_2": 10, "u3": 15}

        class Split:

            def __init__(self, heads, xh, xl):
                self.heads, self.xh, self.xl = heads, xh, xl

            def head(self, act, at):
                act.wait_ge(fill[at.slot], at.filled)
                if not isinstance(at.n, int) or at.n >= 2:
                    act.wait_ge(multiplied, at.n - 1)
                act.activation(self.heads[at.buffer], ring[:, at.slot, :], ACT.Copy).then_inc(hi_made, 1)

            def rest(self, dve, at):
                dve.wait_ge(hi_made, at.split + 1)
                dve.tensor_tensor(ring_r[:, at.slot, :], ring[:, at.slot, :], self.heads[at.buffer].bitcast(F32), ALU.subtract) \
                   .then_inc(lo_ready, 1)

            def act_input(self, act, q):
                for i in range(2):
                    act.wait_ge(*reached("u_ready", 2 * q + i + 1))
                    act.activation(self.xh[i], u[:, 4 * i:4 * i + 4, :], ACT.Copy).then_inc(sig("input_heads"), 1)

            def dve_input(self, dve, q):
                for i in range(2):
                    self.input_rest(dve, i, INPUTS_BEFORE[f"u{q}"] + i, u[:, 4 * i:4 * i + 4, :])

            def input_rest(self, dve, i, before, src):
                dve.wait_ge(*reached("input_heads", before + 1))
                dve.tensor_tensor(self.xl[i], src, self.xh[i].bitcast(F32), ALU.subtract).then_inc(sig("input_rests"), 1)

            def tiles(self, k):
                return self.xh[k // 4][:, k % 4, :], self.xl[k // 4][:, k % 4, :]

        def multiply_split(pe, sp_, at, products, halves=None):
            pe.wait_ge(hi_made, at.split + 1)
            for i, (o, (xh, xl), dst, start, stop) in enumerate(products):
                if halves and i in (0, len(products) // 2):
                    pe.wait_ge(*reached("input_rests", halves[i > 0]))
                w = sp_.heads[at.buffer][:, o:o + P]
                pe.matmul(dst, w, xh, start=start, stop=False, skip_group_check=True)
                pe.matmul(dst, w, xl, start=False, stop=False, skip_group_check=True)
            pe.wait_ge(lo_ready, at.split + 1)
            for o, (xh, xl), dst, start, stop in products:
                last = pe.matmul(dst, ring_r[:, at.slot, o:o + P], xh, start=False, stop=stop, skip_group_check=True)
            last.then_inc(multiplied, 1)

        def columns_by(sp_, dst):
            return [(k * CH + m * P, sp_.tiles(k), dst[:, m * S:(m + 1) * S], m == 0 and k == 0, k == KD - 1)
                    for k in range(KD) for m in range(2)]

        def halves_of(q):
            return INPUTS_BEFORE[f"u{q}"] + 1, INPUTS_BEFORE[f"u{q}"] + 2

        def rows_by(hid, first, end):
            return [(kt * D + m * P, hid[kt], bank[m // 2][:, m % 2 * S:(m % 2 + 1) * S], first and kt == 0 and m % 2 == 0, end and kt == 1)
                    for kt in range(2) for m in range(KD)]

        def columns(w, width, base=0):
            return lambda at: w[:, bass.ds(at.c * width + base, width)].rearrange("(k p) n -> p k n", p=P)

        def rows(w, tiles):
            return lambda at: w[bass.ds(at.c * (tiles * P), tiles * P), :].rearrange("(k p) n -> p k n", p=P)

        def columns_of_pair(w, base):
            return lambda at: w[:, bass.ds(at.pair * CH + base, CH)].rearrange("(k p) n -> p k n", p=P)

        def load(sp, place, count, source, linear=True):
            def body(at):
                if not isinstance(at.n, int) or at.n >= SLOTS:
                    sp.wait_ge(multiplied, at.n - (SLOTS - 1))
                src = source(at)
                sp.dma_start(ring[:, at.slot, :].rearrange("p (k n) -> p k n", k=src.shape[1]), src) \
                    .then_inc(fill[at.slot], 16)
            sweep(sp, place, count, body, linear)

        def pe_linear_split(pe, place, count, sp_, q):
            def body(at):
                pe.wait_ge(evacuated, at.linear + 1)
                multiply_split(pe, sp_, at, columns_by(sp_, bank[at.parity]), halves_of(q))
            sweep(pe, place, count, body, split=True)

        def evacuate(eng, place, count, write, split, end=True):
            def body(at):
                if not (end and isinstance(at.c, int) and at.c == count - 1):
                    split.head(eng, at.after())
                eng.wait_ge(multiplied, at.n + 1)
                write(at.c, bank[at.parity].rearrange("p (m t) -> p m t", t=S)).then_inc(evacuated, 1)
            sweep(eng, place, count, body, split=True)

        class Aside:

            def __init__(self, place, first_bank):
                self.place, self.first_bank = place, first_bank
                self.done = 0

            def modulate(self, pe, count):
                for _ in range(count):
                    self.modulate_half(pe)

            def modulate_half(self, pe):
                c, i = divmod(self.done, 2)
                at = Chunk(self.place, c, c, None)
                if i == 0:
                    pe.wait_ge(fill[at.slot], at.filled)
                    if c:
                        pe.wait_ge(*reached("mod_copied", c))
                for k in range(4 * i, 4 * i + 4):
                    last = pe.matmul(mod_place(bank[7], c)[:, CH:2 * CH], c_act[:, k:k + 1], ring[:, at.slot, k * CH:(k + 1) * CH],
                                     start=(k == 0), stop=(k == KD - 1))
                if i:
                    last.then_inc(multiplied, 1)
                self.done += 1

            def copy_modulation(self, act, until):
                while self.done < until:
                    c = self.done
                    act.wait_ge(multiplied, self.place.n + c + 1)
                    act.activation(mod_place(delta, c)[:, c // 3, :], mod_place(bank[7], c)[:, CH:2 * CH], ACT.Copy).then_inc(sig("mod_copied"), 1)
                    self.done += 1

            def multiply(self, pe, count):
                for _ in range(count):
                    c, i = divmod(self.done, 2 * KD)
                    at = Chunk(self.place, c, c, None)
                    m, k = divmod(i, KD)
                    if i == 0:
                        pe.wait_ge(fill[at.slot], at.filled)
                        pe.wait_ge(evacuated, at.linear + 1)
                    last = pe.matmul(bank[self.first_bank + at.parity][:, m * S:(m + 1) * S], ring[:, at.slot, k * CH + m * P:k * CH + (m + 1) * P],
                                     u[:, k, :], start=(k == 0), stop=(k == KD - 1))
                    if i == 2 * KD - 1:
                        last.then_inc(multiplied, 1)
                    self.done += 1

            def evacuate(self, act, until, write):
                while self.done < until:
                    at = Chunk(self.place, self.done, self.done, None)
                    act.wait_ge(multiplied, at.n + 1)
                    write(at.c, bank[self.first_bank + at.parity].rearrange("p (m t) -> p m t", t=S)).then_inc(evacuated, 1)
                    self.done += 1

        over = sig("stage_over")

        class Stages:
            def __init__(self, eng):
                self.eng, self.n = eng, 0

            def end(self):
                self.n += 1
                self.eng.drain().then_inc(over, 1)
                self.eng.wait_ge(over, 4 * self.n)

        class Norm:
            def __init__(self):
                self.n = 0
        squares = work[:, 0:2, :].rearrange("p a (k t) -> p (a k) t", t=S)

        def act_norm(act, r):
            act.activation(squares[:, 0:4, :], h[:, 0:4, :], ACT.Square).then_inc(sig(f"squares_act_{r}"), 1)
            act.activation(small[:, 250:251], const("ones")[:, 0:1], ACT.Sqrt)
            act.wait_ge(*reached(f"variance_{r}", 1))
            act.activation(rs[:, :], rs[:, :], ACT.Sqrt).then_inc(sig(f"root_{r}"), 1)

        def pe_norm(pe, r):
            pe.wait_ge(*reached(f"squares_act_{r}", 1))
            pe.wait_ge(*reached("squares_dve", r + 1))
            for k in range(KD):
                last = pe.matmul(bank[7][:, 0:S], const("ones"), squares[:, k, :], start=(k == 0), stop=(k == KD - 1))
            last.then_inc(sig(f"square_sum_{r}"), 1)

        def dve_norm(dve, link, r, gain, shift=None, dst=u):
            dve.tensor_tensor(squares[:, 4:8, :], h[:, 4:8, :], h[:, 4:8, :], ALU.mult).then_inc(sig("squares_dve"), 1)
            dve.wait_ge(*reached(f"square_sum_{r}", 1))
            dve.tensor_scalar(rs[:, :], bank[7][:, 0:S], 1.0 / D, 1e-6, ALU.mult, ALU.add).then_inc(sig(f"variance_{r}"), 1)
            dve.wait_ge(*reached(f"root_{r}", 1))
            link(dve.reciprocal(rs[:, :], rs[:, :]))
            for half in (range(4), range(4, KD)):
                for k in half:
                    ins = dve.scalar_tensor_tensor(out=dst[:, k, :], in0=h[:, k, :], scalar=gain(k), in1=rs[:, :],
                                                   op0=ALU.mult, op1=ALU.mult)
                if shift is not None:
                    link(ins)
                    for k in half:
                        ins = dve.tensor_scalar(dst[:, k, :], dst[:, k, :], shift(k), None, ALU.add)
                if dst is u:
                    ins.then_inc(sig("u_ready"), 1)

        comb_dram = nc.dram_tensor("combine", (EXPERTS, S), F32, kind="Internal").ap()
        block = ctx.enter_context(nc.Block())

        decay_log, a_gate, g_gate, kk, k2, bonus, sq, cum = (unit(i) for i in range(8))
        tanh_wd, sig_gd, kidx = proj[:, 78, :], proj[:, 79, :], proj[:, 82, :]
        shifted = work[:, 0:4, :].rearrange("p a n -> p (a n)")[:, 0:14 * S].rearrange("p (m t) -> p m t", t=S)
        ar = work[:, 0:2, :].rearrange("p a (x c s t) -> p (a x) c s t", x=2, c=TB, s=2)
        b_til, k_til, e1, e2, e3, cum_prev = w4(2), w4(3), w4(4), w4(5), w4(6), w4(7)
        v_tok = work[:, 8, :].rearrange("p (c n) -> p c n", c=TB)
        bk_tok = work[:, 9, :].rearrange("p (s n) -> p s n", s=2)
        prods = work[:, 4:6, :].rearrange("p a (h n) -> p (a h) n", n=512)
        levels = [work[:, 6, 0:512], work[:, 6, 512:1024]]
        inv, inv_t = halves(cum)
        upd, xs_sa = halves(kk)
        xs, sa = xs_sa[:, 0:256], xs_sa[:, 256:512]
        state = halves(k2)[0].rearrange("p (m n) -> p m n", m=RT)
        y_tok = decay_log.rearrange("p m t -> p (m t)").rearrange("p (c n) -> p c n", c=TB)
        y_rwkv = unit(1)
        cend = small[:, 0:8].rearrange("p (m c) -> p m c", c=TB)
        mid = small[:, 8:16].rearrange("p (m c) -> p m c", c=TB)
        carry = small[:, 16:20]
        one_less_ka = small[:, 20:24]
        w_idx = small[:, 24:40].rearrange("p (b n) -> p b n", b=TB)
        stat = small[:, 48:64]
        stat2 = small[:, 64:80]

        def heads4(ap):
            return ap.rearrange("p (h t) -> p h t", t=P)

        def spread(ap, n):
            return ap.rearrange("p (o t) -> p o t", o=1).to_broadcast([P, n, ap.shape[1]])

        class Solver:

            def __init__(self, inv, inv_t, upd, levels, m_t):
                self.inv, self.inv_t, self.upd, self.levels, self.m_t = inv, inv_t, upd, levels, m_t

            def pe(self, pe, b, meanwhile=lambda lv, wait: None):
                inv, inv_t, upd = self.inv, self.inv_t, self.upd
                pe.wait_ge(*reached("solve_start", b + 1))
                for i in range(4):
                    last = pe.transpose(bank[5][:, i * P:(i + 1) * P], inv_t[:, i * P:(i + 1) * P], ident)
                last.then_inc(sig("solve_turned"), 1)
                for lv in range(6):
                    n = 6 * b + lv
                    pe.wait_ge(*reached("level_masked", n + 1))
                    if lv == 0:
                        pe.wait_ge(*reached("solve_copied", b + 1))
                    else:
                        pe.wait_ge(*reached("inv_updated", 11 * b + 2 * lv))
                    for i in range(4):
                        last = pe.matmul(bank[4][:, i * P:(i + 1) * P], self.levels[n % 2][:, i * P:(i + 1) * P],
                                         inv[:, i * P:(i + 1) * P], start=True, stop=True)
                    last.then_inc(sig("upd_made"), 1)
                    meanwhile(lv, 0)
                    pe.wait_ge(*reached("upd_copied", n + 1))
                    if lv < 5:
                        for i in range(4):
                            last = pe.matmul(bank[5][:, i * P:(i + 1) * P], inv_t[:, i * P:(i + 1) * P],
                                             upd[:, i * P:(i + 1) * P], start=True, stop=True)
                        last.then_inc(sig("inv_step"), 1)
                    for i in range(4):
                        last = pe.matmul(bank[6][:, i * P:(i + 1) * P], upd[:, i * P:(i + 1) * P],
                                         inv_t[:, i * P:(i + 1) * P], start=True, stop=True)
                    last.then_inc(sig("inv_step"), 1)
                    meanwhile(lv, 1)

            def act(self, act, b, meanwhile=lambda lv: None):
                act.wait_ge(*reached("solve_turned", b + 1))
                act.activation(self.inv, bank[5], ACT.Copy).then_inc(sig("solve_copied"), 1)
                for lv in range(6):
                    act.wait_ge(*reached("upd_made", 6 * b + lv + 1))
                    act.activation(self.upd, bank[4], ACT.Copy).then_inc(sig("upd_copied"), 1)
                    meanwhile(lv)

            def dve(self, dve, link, b):
                inv, inv_t = self.inv, self.inv_t
                link(dve.tensor_tensor(heads4(inv_t), self.m_t, spread(const("level0"), 4), ALU.mult))
                dve.tensor_tensor(heads4(inv_t), spread(ident, 4), heads4(inv_t), ALU.subtract) \
                   .then_inc(sig("solve_start"), 1)
                dve.wait_ge(*reached("solve_start", b + 1))
                dve.wait_ge(*reached("solve_copied", b + 1))
                for lv in range(6):
                    done = 11 * b + 2 * lv
                    if lv < 5:
                        dve.wait_ge(*reached("inv_step", done + 1))
                        dve.tensor_tensor(inv, inv, bank[5], ALU.subtract).then_inc(sig("inv_updated"), 1)
                        done += 1
                    dve.wait_ge(*reached("inv_step", done + 1))
                    dve.tensor_tensor(inv_t, inv_t, bank[6], ALU.subtract).then_inc(sig("inv_updated"), 1)
                    dve.wait_ge(*reached("inv_updated", done + 1))

            def pool(self, pool, b):
                for lv in range(6):
                    n = 6 * b + lv
                    if n >= 2:
                        pool.wait_ge(*reached("upd_made", n - 1))
                    pool.tensor_tensor(heads4(self.levels[n % 2]), self.m_t, spread(const(f"level{lv + 1}"), 4), ALU.mult) \
                        .then_inc(sig("level_masked"), 1)

        GATES_FIRST = 2
        GATES_ASIDE = (8 - GATES_FIRST) // TB

        DIL_CHUNKS = 3 * DH * P // CH
        CONV_ASIDE = 10

        def aside_chunks(b, n):
            return CONV_ASIDE + (64 * b + n) // (2 * KD)

        def batch(b):
            return b // 2, 2 * (b % 2)

        rwkv_solver = Solver(inv, inv_t, upd, levels, prods[:, :, 0:P])

        conv_units = (0, 1, 2, 5, 6, 7)
        beta_rows, rate_rows, soft_rows, gc_rows = (work[0:GH, 4, i * S:(i + 1) * S] for i in range(4))
        norm_rows = rs[0:32, :]
        kq = work[:, 0:4, :].rearrange("p a (h c s t) -> p (a h) c s t", h=2, c=TB, s=2)
        vb_tok = work[:, 5:7, :].rearrange("p c (h n) -> p c h n", h=GH)
        kd_tok = work[:, 7, :].rearrange("p (h n) -> p h n", h=GH)
        egrow = work[:, 7, 0:512]
        g_prods = work[:, 8, :].rearrange("p (h s t) -> p h s t", h=4, s=2)
        g_levels = [work[:, 9, 0:512], work[:, 9, 512:1024]]
        late = proj[:, T_GV:T_GV + 8, :].rearrange("p (a m) t -> p a (m t)", a=4)
        g_inv, g_inv_t, g_upd, g_xs = (late[:, i, :] for i in range(4))
        g_solver = Solver(g_inv, g_inv_t, g_upd, g_levels, g_prods[:, :, 0, :])
        o_gdn = proj[:, T_GQ:T_GQ + GH, :]
        decays = delta[:, 0:4, :].rearrange("p (h) (s t) -> p h s t", s=2)
        g_state = delta[:, 4:8, :].rearrange("p a (h n) -> p (a h) n", h=2)
        y_gdn = proj[:, T_GZ:T_GZ + GH, :]
        gc_col = small[:, 200:216].rearrange("p (c n) -> p c n", c=TB)
        beta_col = small[:, 216:232].rearrange("p (c n) -> p c n", c=TB)
        kd_col = small[:, 232:240]
        rate_col, dt_col = small[0:GH, 240:241], small[0:GH, 241:242]
        d_logits = [work[:, i, 0:768].rearrange("p (g n) -> p g n", g=3) for i in range(2)]
        d_probs = [work[:, 2 + i, 0:768].rearrange("p (g n) -> p g n", g=3) for i in range(2)]
        d_probs_t = work[:, 4, 0:768].rearrange("p (g n) -> p g n", g=3)
        dv_tok = work[:, 5:8, :].rearrange("p a n -> p (a n)").rearrange("p (c h n) -> p c h n", c=TB, h=DH)
        d_tok = work[:, 8, 0:512]
        y_dil = w4(9)
        NORMED = GH + 2 * DH
        head_quads = [o_gdn[:, 4 * i:4 * i + 4, :] for i in range(GH // 4)] + [proj[:, T_DQ + 4 * i:T_DQ + 4 * i + 4, :] for i in range(2 * DH // 4)]
        head_pairs = [quad[:, 2 * i:2 * i + 2, :] for quad in head_quads for i in range(2)]
        d_max, d_sum = small[:, 80:88], small[:, 96:104]
        router = proj[:, 32:34, :].rearrange("p a n -> p (a n)").rearrange("p (k n) -> p k n", k=KD)
        router_b = proj[:, 34, 0:EXPERTS]
        sc_e, sel_e, left_e, comb_e = (work[:, 3, (2 + 2 * i) * EXPERTS:(4 + 2 * i) * EXPERTS].rearrange("p (b n) -> p b n", b=TB) for i in range(4))
        best_e = work[:, 4, 0:128].rearrange("p (b g n) -> p b g n", b=TB, g=GROUPS)
        gs_e = work[:, 4, 128:144].rearrange("p (b g) -> p b g", b=TB)
        more_e, same_e = (work[:, 4, 256 + i * 128:384 + i * 128].rearrange("p (b g j) -> p b g j", b=TB, g=GROUPS) for i in range(2))
        rank_e, top_e = (work[:, 4, i:i + TB * GROUPS].rearrange("p (b g) -> p b g", b=TB) for i in (768, 784))
        sum_e = work[:, 4, 800:802]
        comb_t = work[0:EXPERTS, 4, 512:768]
        silu_e = [work[:, 5, i * 512:(i + 1) * 512] for i in range(2)]
        hid_e = [work[:, 6, i * 512:(i + 1) * 512] for i in range(2)]
        comb_row = [work[:, 7, i * S:(i + 1) * S] for i in range(2)]
        out_tok = work[:, 8:10, :]

        dil_items = [(b, i) for b in range(TB) for i in range(4)]
        dil_masks = cst[:, CONST["dil0"][0]:CONST["dil0"][0] + 6 * P].rearrange("p (g n) -> p g n", g=3)

        class Out:

            def __init__(self, name, heads, first, second, sources, gate, merged_before):
                self.before = INPUTS_BEFORE[name]
                self.pieces = sources
                self.n = len(sources)
                self.first = Split(heads, *first)
                self.second = Split(heads, *second)
                self.mix = Split(heads, [proj_r[:, 62 + 4 * i:66 + 4 * i, :] for i in range(2)], mix_rests)
                self.gate, self.merged_before = gate, merged_before

            def split_of(self, i):
                return (self.first, i) if i < self.n - 1 else (self.second, 0)

        def act_out(act, place, o, chunks, early=0):
            at = lambda c: Chunk(place, c, c, None)
            if early:
                o.mix.head(act, at(0))
            for i, src in list(enumerate(o.pieces))[early:]:
                sp_, k = o.split_of(i)
                act.activation(sp_.xh[k], src, ACT.Copy).then_inc(sig("input_heads"), 1)
                if i == 0:
                    sp_.head(act, at(0))
            for c in range(1, chunks):
                o.mix.head(act, at(c))
                if c == chunks - 4:
                    for i in range(2):
                        act.wait_ge(*reached("merged_ready", o.merged_before + i + 1))
                        act.activation(o.mix.xh[i], merged[:, 4 * i:4 * i + 4, :], ACT.Copy).then_inc(sig("input_heads"), 1)
            place.skip(chunks, split=True)

        def dve_out(dve, place, o, chunks, first_gated, write, early=0):
            at = lambda c: Chunk(place, c, c, None)
            if early:
                o.mix.rest(dve, at(0))
            for i, src in list(enumerate(o.pieces))[early:]:
                sp_, k = o.split_of(i)
                sp_.input_rest(dve, k, o.before + i, src)
                if i == 0:
                    sp_.rest(dve, at(0))
            for c in range(chunks):
                if c + 1 < chunks:
                    o.mix.rest(dve, at(c + 1))
                i = c - (chunks - 6)
                dve.wait_ge(multiplied, at(c).n + 1)
                if i < 0:
                    first_gated(c, at(c)).then_inc(evacuated, 1)
                elif i < 2:
                    par = at(c).parity
                    src = psum[:, 2 * par:2 * par + 2, :].rearrange("p b (m t) -> p (b m) t", t=S)
                    part = merged[:, 4 * i:4 * i + 4, :]
                    dve.tensor_tensor(merge_tmp, src, proj[:, o.gate + 4 * i:o.gate + 4 * i + 4, :], ALU.mult).then_inc(evacuated, 1)
                    dve.wait_ge(evacuated, at(c).linear + 3)
                    dve.tensor_tensor(part, part, merge_tmp, ALU.add).then_inc(sig("merged_ready"), 1)
                    dve.wait_ge(*reached("merged_ready", o.merged_before + i + 1))
                    o.mix.input_rest(dve, i, o.before + o.n + i, part)
                else:
                    write(c - (chunks - 4), at(c)).then_inc(evacuated, 1)
            place.skip(chunks, split=True)

        def pe_out(pe, place, o, first_tiles, chunks):
            for c in range(chunks):
                at = Chunk(place, c, c, None)
                i = c - (chunks - 6)
                sp_ = o.first if i < 0 else o.second if i < 2 else o.mix
                halves = (o.before + 1, o.before + o.n - 1) if i < 0 else (o.before + o.n,) * 2 if i < 2 else (o.before + o.n + 1, o.before + o.n + 2)
                pe.wait_ge(evacuated, at.linear + 1)
                if first_tiles == 4 and i < 0 or 0 <= i < 2:
                    dst = lambda m: bank[2 * at.parity + m // 2][:, m % 2 * S:(m % 2 + 1) * S]
                    products = [(k * 4 * P + m * P, sp_.tiles(k), dst(m), m % 2 == 0 and k == 0, k == RT - 1)
                                for m in range(4) for k in range(RT)]
                else:
                    products = columns_by(sp_, bank[2 * at.parity])
                multiply_split(pe, sp_, at, products, halves)
            place.skip(chunks, split=True)

        def of_tiles(*starts):
            return [proj_r[:, t:t + 4, :] for t in starts]

        def step_of(at):
            return at.third + 1, 1 - at.j // 3 % 2, at.j % 3

        def weights_row(act, buffer, x):
            act.dma_start(comb_row[buffer], comb_dram[bass.ds(x, 1), :].to_broadcast([P, S])).then_inc(sig(f"comb_filled_{buffer}"), 16)

        def act_expert_chunk(act, at, e, par, kind):
            split_free.head(act, at.after())
            if kind == 0:
                if not isinstance(e, int) or e > 0:
                    act.wait_ge(*reached("hid_ready", e))
                    if not isinstance(e, int) or e > 1:
                        weights_row(act, 1 - par, e - 1)
                act.wait_ge(multiplied, at.n + 1)
                act.activation(silu_e[par], bank[4 + 2 * par], ACT.Silu).then_inc(sig("silu_done"), 1)

        def dve_expert_chunk(dve, at, e, par, kind):
            split_free.rest(dve, at.after())
            if kind == 1:
                by_tile = lambda ap: ap.rearrange("p (f t) -> p f t", f=2)
                dve.wait_ge(multiplied, at.n + 1)
                dve.wait_ge(*reached("silu_done", e + 1))
                if isinstance(e, int) and e == 0:
                    dve.tensor_tensor(hid_e[par], silu_e[par], bank[5 + 2 * par], ALU.mult).then_inc(sig("au_free"), 1)
                    dve.drain().then_inc(sig("hid_ready"), 1)
                    return
                dve.tensor_tensor(silu_e[par], silu_e[par], bank[5 + 2 * par], ALU.mult).then_inc(sig("au_free"), 1)
                dve.wait_ge(*reached("au_free", e + 3))
                turn = at.turn_of_two
                dve.wait_ge(*reached(f"comb_filled_{1 - par}", turn * 16 + 16))
                dve.tensor_tensor(by_tile(hid_e[par]), by_tile(silu_e[par]), spread(comb_row[1 - par], 2), ALU.mult).then_inc(sig("hid_ready"), 1)

        def later(at):
            at.third = at.third + SLOTS // 3
            at.turn_of_two = at.turn_of_two + 1
            return at

        def row_to_all(pe, dst, rows_, i, k, first=True):
            return pe.matmul(dst, ident[0:k, i:i + 1].to_broadcast([k, P]), rows_, start=True, stop=True)

        def sum_to_row(pe, dst, src, i, n):
            return pe.matmul(dst, const("pick")[:, 31 - i:63 - i], src, start=(i == 0), stop=(i == n - 1))

        relu_s = work[:, 0:2, :].rearrange("p a (b n) -> p (a b) n", n=512)
        score, rest, sel_bias = (work[:, 2, i * S:(i + 1) * S] for i in range(3))
        logits = work[:, 3:5, :].rearrange("p a (b n) -> p (a b) n", n=512)
        probs = work[:, 5:7, :].rearrange("p a (b n) -> p (a b) n", n=512)
        probs_t = work[:, 7:9, :].rearrange("p a (i t) -> p a i t", t=P)
        att_v = unit(3).rearrange("p m t -> p (m t)").rearrange("p (c n) -> p c n", c=TB)
        att_tok = halves(unit(4))[0]
        y_att = unit(6)
        top8, row_max, row_sum = small[:, 80:88], small[:, 88:96], small[:, 96:104]
        rope_tmp = work[:, 0:4, :].rearrange("p a (b n) -> p (a b) n", n=512)
        rope_tiles = [proj[:, t:t + 2, :] for t in (T_Q, T_Q + 2, T_AK, T_AK + 2, T_QI, T_QI + 2)] + [proj[:, 82:83, :]]
        own_causal = const("dil0")[:, P:2 * P]
        merged = work[:, 0:2, :].rearrange("p a (k t) -> p (a k) t", t=S)
        merge_tmp = w4(2)
        mods = small[:, 128:176]
        mod_rows = delta[0:65, :, :]
        def mod_place(t, c):
            part = 32 * (c % 3)
            return t[part:part + 1]
        gain1, gain2, c_act = small[:, 176:184], small[:, 184:192], small[:, 192:200]

        baw = work[:, 3, 0:KD * 16].rearrange("p (k n) -> p k n", k=KD)
        ba_rows = work[0:8, 4, 0:2 * S].rearrange("p (s t) -> p s t", s=2)

        def place_of(hd):
            return 2 * (hd // 4) + hd % 2, hd // 2 % 2

        def head_at(i):
            return i // 4 * 4 + i // 2 % 2 + 2 * (i % 2)

        def pe_scores(pe, base, q_tile, key, b, n):
            for hd in range(HEADS):
                bk, half = place_of(hd)
                part = slice(HD * (hd % 2), HD * (hd % 2) + HD)
                last = pe.matmul(bank[base + bk][:, half * S:half * S + n], proj[part, q_tile + hd // 2, b * P:(b + 1) * P],
                                 key(hd)[part, 0:n], start=True, stop=True)
            return last

        def pair_view(ap, n):
            return ap.rearrange("p (i n) -> p i n", i=2)[:, :, 0:n]

        def tiles_of(t, at, n):
            return t.rearrange("p a (k t) -> p (a k) t", t=S)[:, at:at + n, :]
        def flat_of(ap):
            return ap.rearrange("p k t -> p (k t)")
        split_in = Split([flat_of(proj_r[:, 46 + 8 * i:54 + 8 * i, :]) for i in range(2)],
                         [proj_r[:, 62 + 4 * i:66 + 4 * i, :] for i in range(2)], [proj_r[:, 70 + 4 * i:74 + 4 * i, :] for i in range(2)])
        split_free = Split([flat_of(proj_r[:, 8 * i:8 + 8 * i, :]) for i in range(2)],
                           [proj_r[:, 16 + 4 * i:20 + 4 * i, :] for i in range(2)], [proj_r[:, 24 + 4 * i:28 + 4 * i, :] for i in range(2)])
        split_in_2 = Split([flat_of(proj_r[:, 52 + 8 * i:60 + 8 * i, :]) for i in range(2)],
                           [proj_r[:, 68 + 4 * i:72 + 4 * i, :] for i in range(2)], [proj_r[:, 76 + 4 * i:80 + 4 * i, :] for i in range(2)])
        ffn_tmp = [tiles_of(work, 16 + 2 * i, 2) for i in range(3)]
        ffn_h, ffn_l = proj_r[:, 32:32 + DFF // P, :], proj_r[:, 54:54 + DFF // P, :]
        exp_h, exp_l = ([flat_of(proj_r[:, b + 2 * i:b + 2 * i + 2, :]) for i in range(2)] for b in (36, 40))
        mix_rests = of_tiles(74, 78)
        out_1 = Out("out", split_free.heads, (of_tiles(16), of_tiles(20)), (of_tiles(54), of_tiles(58)), [y_rwkv, y_att], T_GATE + KD, 0)
        heads_2 = [flat_of(proj_r[:, t:t + 8, :]) for t in (0, 36)]
        out_2 = Out("out_2", heads_2, (of_tiles(8, 12), of_tiles(16, 20)), (of_tiles(44), of_tiles(64)),
                    [y_gdn[:, 0:4, :], y_gdn[:, 4:8, :], y_dil], T_GATE2 + KD, 2)
        out_2.mix = Split(heads_2, of_tiles(48, 52), of_tiles(56, 60))
        HID0 = 3 + DFF // CH

        def pool_split(pool, src, head, rest):
            by_128 = lambda ap: ap.rearrange("p (a t) -> p a t", t=P)
            pool.tensor_tensor(by_128(head), by_128(src), spread(const("ones"), 2 * S // P), ALU.mult)
            pool.drain()
            pool.tensor_tensor(rest, src, head.bitcast(F32), ALU.subtract).then_inc(sig("hid_split"), 1)

        @block.sync
        def _(sp):
            place = Stream()
            sp.dma_start(work[:, 0:2, :], fp["x"].rearrange("o (b p) d -> p (o b) d", p=P)).then_inc(sig("x_loaded"), 16)
            sp.dma_start(cst[:, :], fp["consts"]).then_inc(sig("consts_loaded"), 16)
            stage = work[:, 2, :]
            for name, (at, n) in VROWS.items():
                src = fp[name]
                if len(src.shape) == 2:
                    src = src.rearrange("a b -> (a b)")
                sp.dma_start(stage[at:at + n, 0:P], src.rearrange("(a p) -> a p", p=P)).then_inc(sig("vectors_loaded"), 16)
            sp.dma_start(stage[0:VB, P:2 * P], fp["b_ada_2"].rearrange("o (a p) -> (o a) p", p=P)).then_inc(sig("vectors_loaded"), 16)
            sp.dma_start(stage[0:VC, 2 * P:3 * P], fp["gdn_conv_w_2"].rearrange("o j (a p) -> (o j a) p", p=P)).then_inc(sig("vectors_loaded"), 16)
            sp.dma_start(lora[0:64, 0, :], fp["w_decay_up"]).then_inc(sig("lora_loaded"), 16)
            sp.dma_start(lora[64:128, 0, :], fp["a_up"]).then_inc(sig("lora_loaded"), 16)
            sp.dma_start(lora[:, 1, :], fp["g_up"]).then_inc(sig("lora_loaded"), 16)
            sp.dma_start(idxw[:, :, :], fp["w_in"][:, IDXK0:GATE0].rearrange("(k p) n -> p k n", p=P)).then_inc(sig("idxw_loaded"), 16)
            first = columns(fp["w_in"], CH)
            load(sp, place, SLOTS, first)
            load(sp, place, 15 - SLOTS, columns(fp["w_in"], CH, SLOTS * CH))
            load(sp, place, GATES_FIRST, columns(fp["w_in"], CH, GATE0))
            load(sp, place, 24, columns(fp["w_ada_2"][0], CH), linear=False)
            load(sp, place, 8 - GATES_FIRST, columns(fp["w_in"], CH, GATE0 + GATES_FIRST * CH))
            load(sp, place, 2, columns(fp["w_o_rwkv"], 512))
            load(sp, place, 2, columns(fp["w_o_att"], 512))
            load(sp, place, 4, columns(fp["w_out"], CH))
            pair_source = [columns_of_pair(fp["w_ffn_in"], 0), columns_of_pair(fp["w_ffn_in"], DFF)]
            load(sp, place, 2 * (DFF // CH), lambda at: pair_source[at.j % 2](at), linear=False)
            load(sp, place, DFF // (2 * P), rows(fp["w_ffn_out"], 2), linear=False)
            sp.wait_ge(over, 4 * 6)
            sp.dma_start(baw, fp["w_in_2"][0][:, GDN_COLS:DIL0].rearrange("(k p) n -> p k n", p=P)).then_inc(sig("ba_loaded"), 16)
            sp.dma_start(rate_col, fp["gdn_a_log_2"].rearrange("o h -> h o")).then_inc(sig("rates_loaded"), 16)
            sp.dma_start(dt_col, fp["gdn_dt_bias_2"].rearrange("o h -> h o")).then_inc(sig("rates_loaded"), 16)
            for first, count in ((0, 12), (12, 4)):
                load(sp, place, count, columns(fp["w_in_2"][0], CH, first * CH))
            for first, count in ((0, 18), (18, 8)):
                load(sp, place, count, columns(fp["w_in_2"][0], CH, DIL0 + first * CH))
            load(sp, place, 4, columns(fp["w_up_gdn_2"][0], CH))
            load(sp, place, 2, columns(fp["w_up_dil_2"][0], 512))
            load(sp, place, 4, columns(fp["w_out_2"][0], CH))
            tall = lambda w: w.rearrange("(k p) n -> p k n", p=P)
            load(sp, place, 2, lambda at: tall(fp[("w_sh_gate_2", "w_sh_up_2")[at.c]][0]), linear=False)
            sp.wait_ge(over, 4 * 14)
            sp.dma_start(router, fp["w_router_2"][0].rearrange("(k p) n -> p k n", p=P)).then_inc(sig("router_loaded"), 16)
            sp.dma_start(router_b, fp["router_bias_2"].to_broadcast([P, EXPERTS])).then_inc(sig("router_loaded"), 16)

            def expert_source(at):
                kind = at.j % 3
                if kind < 2:
                    w = fp[("w_exp_gate_2", "w_exp_up_2")[kind]][0]
                    return w[bass.ds(at.third, 1), :, :].rearrange("e (k p) n -> p (e k) n", p=P)
                w = fp["w_exp_down_2"][0]
                return w[bass.ds(at.third - 1, 1), :, :].rearrange("e (k p) n -> p (e k) n", p=P)
            first_sources = lambda at: tall(fp["w_sh_down_2"][0]) if at.c == 2 else expert_source(at)
            load(sp, place, SLOTS, first_sources, linear=False)
            load(sp, place, 3 * EXPERTS - SLOTS, lambda at: expert_source(later(at)), linear=False)
            load(sp, place, 1, lambda at: tall(fp["w_exp_down_2"][0][EXPERTS - 1]), linear=False)
            for b in range(TB):
                sp.wait_ge(*reached(f"out_ready_{b}", 1))
                sp.dma_start(out[0, b * P:(b + 1) * P, :], out_tok[:, b, :]).then_inc(sig("out_written"), 16)
            sp.wait_ge(*reached("out_written", 32))

        @block.gpsimd
        def _(pool):
            st = Stages(pool)
            pool.memset(mod_rows, 0.0)
            st.end()
            st.end()
            link = Chain(pool, sig("pool_chain"))
            pool.wait_ge(*reached("token_shifted", 1))
            pool.wait_ge(*reached("a_gate_ready", 4))
            pool.wait_ge(*reached("one_less_ka_ready", 1))
            for m in range(RT):
                pool.tensor_scalar(k2[:, m, :], a_gate[:, m, :], v("k_a", m), one_less_ka[:, m:m + 1], ALU.mult, ALU.add) \
                    .then_inc(sig("pool_scaled"), 1)
            pool.wait_ge(*reached("pool_scaled", 4))
            pool.tensor_tensor(k2, k2, proj[:, T_K:T_K + RT, :], ALU.mult).then_inc(sig("k2_ready"), 1)
            pool.wait_ge(*reached("k2_ready", 1))
            link(pool.tensor_tensor(bonus, k2, proj[:, T_R:T_R + RT, :], ALU.mult))
            for m in range(RT):
                pool.tensor_scalar(bonus[:, m, :], bonus[:, m, :], v("r_k", m), None, ALU.mult).then_inc(sig("bonus_terms"), 1)
            st.end()
            for b in range(4):
                pool.wait_ge(*reached("prods_masked", 4 * (b + 1)))
                rwkv_solver.pool(pool, b)
            st.end()
            for i, t in enumerate(rope_tiles):
                n = t.shape[1]
                pool.tensor_tensor(rope_tmp[:, i, 0:n * S].rearrange("p (m t) -> p m t", t=S), t, spread(const("cos"), n), ALU.mult) \
                    .then_inc(sig("rope_cos"), 1)
            st.end()
            st.end()
            st.end()
            pool.drain().then_inc(sig("hid_split"), 3)
            for i in range(DFF // CH):
                pool.wait_ge(*reached("pair_evacuated", i + 4))
                pool_split(pool, *(flat_of(ap) for ap in (ffn_tmp[i % 3], ffn_h[:, 2 * i:2 * i + 2, :], ffn_l[:, 2 * i:2 * i + 2, :])))
            st.end()
            st.end()
            place = Stream()
            place.skip(15 + GATES_FIRST, split=True)
            place.skip(24, False)
            place.skip(8 - GATES_FIRST)
            place.skip(8, split=True)
            place.skip(3 * (DFF // CH), False, True)
            place.skip(16, split=True)
            for c in range(CONV_ASIDE):
                split_in_2.rest(pool, Chunk(place, c, c, None))
            st.end()
            st.end()
            for b in range(4):
                pool.wait_ge(*reached("decay_exp", b + 1))
                if b:
                    pool.wait_ge(*reached("g_prods_ready", b))
                pool.tensor_tensor(decays, heads4(g_xs).rearrange("p h (o t) -> p h o t", o=1).to_broadcast([P, 4, 2, P]),
                                   const("upper").rearrange("p (o s t) -> p o s t", o=1, s=2).to_broadcast([P, 4, 2, P]), ALU.mult) \
                    .then_inc(sig("decay_masked"), 1)
                pool.wait_ge(*reached("g_prods_ready", b + 1))
                g_solver.pool(pool, 4 + b)
            st.end()
            st.end()
            st.end()
            st.end()
            with pool.Fori(0, EXPERTS // 2) as it:
                for j in range(2):
                    pool.wait_ge(*reached("hid_ready", it * 2 + (j + 2)))
                    pool_split(pool, hid_e[j], exp_h[j], exp_l[j])
            pool.wait_ge(*reached("hid_ready", EXPERTS + 2))
            pool_split(pool, hid_e[0], exp_h[0], exp_l[0])
            st.end()
            st.end()

        @block.scalar
        def _(act):
            st = Stages(act)
            place = Stream()
            act.drain().then_inc(evacuated, 2)
            act.wait_ge(*reached("x_turned", 2))
            act.activation(h[:, :, P:S], psum[:, 2:4, :].rearrange("p b (k t) -> p (b k) t", t=P), ACT.Copy)
            st.end()
            act_norm(act, 0)
            split_in.act_input(act, 0)
            split_in.head(act, Chunk(place, 0, 0, None))
            act.wait_ge(*reached("idx_multiplied", 2))
            act.activation(kidx, bank[4][:, 0:S], ACT.Copy)
            act.activation(w_idx, bank[5][:, 0:2 * HEADS].rearrange("p (b n) -> p b n", b=TB), ACT.Copy,
                           scale=float(HD) ** -0.5 * float(HEADS) ** -0.5)
            evacuate(act, place, 15, lambda c, src: act.activation(proj[:, bass.ds(c * 2, 2), :], src, ACT.Copy), split=split_in, end=False)
            evacuate(act, place, GATES_FIRST, lambda c, src: act.activation(proj[:, bass.ds(c * 2 + T_GATE, 2), :], src, ACT.Sigmoid), split=split_in)
            st.end()
            act.wait_ge(*reached("token_shifted", 1))
            act.activation(c_act, vec[:, VROWS["c_2"][0]:VROWS["c_2"][0] + KD], ACT.Silu)
            act.activation(tanh_wd[0:64, :], proj[0:64, T_WA, :], ACT.Tanh).then_inc(sig("lora_in"), 1)
            act.activation(sig_gd, proj[:, T_G, :], ACT.Sigmoid).then_inc(sig("lora_in"), 1)
            for m in range(RT):
                act.wait_ge(*reached("lora_out", 1))
                act.activation(a_gate[:, m, :], bank[2 + m // 2][:, m % 2 * S:(m % 2 + 1) * S], ACT.Sigmoid, bias=v("a0", m)) \
                   .then_inc(sig("a_gate_ready"), 1)
            for m in range(RT):
                act.activation(decay_log[:, m, :], bank[m // 2][:, m % 2 * S:(m % 2 + 1) * S], ACT.Sigmoid, bias=v("w0", m)) \
                   .then_inc(sig("decay_sig"), 1)
            act.activation(g_gate, psum[:, 4:6, :].rearrange("p b (m t) -> p (b m) t", t=S), ACT.Copy).then_inc(sig("g_copied"), 1)
            act.wait_ge(*reached("kk_raw", 1))
            act.activation(sq, kk, ACT.Square).then_inc(sig("kk_squared"), 1)
            act.wait_ge(*reached("kk_summed", 1))
            act.activation(sq, psum[:, 6:8, :].rearrange("p b (m t) -> p (b m) t", t=S), ACT.Sqrt).then_inc(sig("kk_norm"), 1)
            act.wait_ge(*reached("cum_ready", 1))
            act.activation(e1, cum, ACT.Exp).then_inc(sig("exps"), 1)
            act.activation(e2, cum, ACT.Exp, scale=-1.0).then_inc(sig("exps"), 1)
            act.wait_ge(*reached("cum_ready", 2))
            act.activation(e3, cum_prev, ACT.Exp).then_inc(sig("exps"), 1)
            act.activation(carry, carry, ACT.Exp).then_inc(sig("exps"), 1)
            act.wait_ge(*reached("v_turned", 2))
            act.activation(v_tok, psum[:, 0:2, :], ACT.Copy)
            act.wait_ge(*reached("bk_turned", 2))
            act.activation(bk_tok, psum[:, 2:4, :], ACT.Copy)
            st.end()
            aside = Aside(place, 7)
            for b in range(4):
                ch, m0 = batch(b)
                rwkv_solver.act(act, b, lambda lv: aside.copy_modulation(act, 6 * b + lv))
                aside.copy_modulation(act, 6 * b + 6)
                act.wait_ge(*reached("x_made", b + 1))
                act.activation(xs, bank[7][:, 0:256], ACT.Copy, scale=-1.0).then_inc(sig("x_copied"), 1)
                act.wait_ge(*reached("sa_made", b + 1))
                act.activation(sa, bank[4][:, 0:256], ACT.Copy).then_inc(sig("sa_copied"), 1)
                act.wait_ge(*reached("y_made", b + 1))
                act.activation(y_tok[:, ch, m0 * P:m0 * P + 256], bank[5][:, 0:256], ACT.Copy).then_inc(sig("y_copied"), 1)
            place.skip(24, False)
            yc = w4(0).rearrange("p m t -> p (m t)").rearrange("p (g n) -> p g n", n=HD)
            act.wait_ge(*reached("y_centred", 1))
            act.activation(w4(1).rearrange("p m t -> p (m t)").rearrange("p (g n) -> p g n", n=HD), yc, ACT.Square).then_inc(sig("y_squared"), 1)
            act.wait_ge(*reached("y_var", 1))
            act.activation(stat2, stat2, ACT.Sqrt).then_inc(sig("y_std"), 1)
            act.wait_ge(*reached("y_turned", 2))
            for m in range(RT):
                act.activation(w4(2)[:, m, :].rearrange("p (c t) -> p c t", c=TB),
                               psum[:, 0:2, m * P:(m + 1) * P], ACT.Identity, scale=v("lnx_g", m), bias=v("lnx_b", m)) \
                   .then_inc(sig("y_affine"), 1)
            st.end()
            for c in range(TB):
                act.wait_ge(*reached("att_v_turned", c + 1))
                act.activation(att_v[:, c, :], bank[7], ACT.Copy).then_inc(sig("att_v_copied"), 1)
            st.end()
            aside = Aside(place, 2)
            for b in range(TB):
                n = (b + 1) * P
                act.wait_ge(*reached("idx_scored", b + 1))
                if b:
                    act.wait_ge(*reached("idx_summed", b))
                for bk in range(4):
                    act.activation(pair_view(relu_s[:, bk, :], n), pair_view(bank[bk], n), ACT.Relu).then_inc(sig("idx_relu"), 1)
                aside.evacuate(act, GATES_ASIDE * (b + 1), lambda c, src: act.activation(
                    proj[:, T_GATE + 2 * (c + GATES_FIRST):T_GATE + 2 * (c + GATES_FIRST) + 2, :], src, ACT.Sigmoid))
                act.wait_ge(*reached("row_max", b + 1))
                for i in range(HEADS):
                    hd = head_at(i)
                    act.activation(pair_view(probs[:, i // 2, :], n)[:, i % 2, :], pair_view(logits[:, i // 2, :], n)[:, i % 2, :], ACT.Exp,
                                   bias=row_max[:, i:i + 1], accum_out=row_sum[:, hd:hd + 1]).then_inc(sig("probs_made"), 1)
                act.wait_ge(*reached("probs_turned", b + 1))
                if b:
                    act.wait_ge(*reached("att_made", b))
                for kb in range(b + 1):
                    act.activation(probs_t[:, kb, :, :], psum[:, 2 * kb:2 * kb + 2, :].rearrange("p a (i t) -> p (a i) t", t=P), ACT.Copy) \
                       .then_inc(sig("probs_t_ready"), 1)
                act.wait_ge(*reached("att_turned", b + 1))
                act.activation(y_att[:, :, b * P:(b + 1) * P], bank[5].rearrange("p (m t) -> p m t", t=P), ACT.Copy).then_inc(sig("y_att_copied"), 1)
            st.end()
            place.skip(8 - GATES_FIRST)
            act_out(act, place, out_1, 8)
            st.end()
            act_norm(act, 1)
            split_free.act_input(act, 1)
            split_free.head(act, Chunk(place, 0, 0, None))

            def silu_gate(at):
                split_free.head(act, at.after())
                if at.j % 2 == 0:
                    act.wait_ge(multiplied, at.n + 1)
                    act.wait_ge(*reached("hid_split", at.pair + 1))
                    src = bank[at.j // 2 % 3 * 2].rearrange("p (m t) -> p m t", t=S)
                    act.activation(ffn_tmp[at.j // 2 % 3], src, ACT.Silu).then_inc(sig("gate_silu"), 1)
            sweep(act, place, 2 * (DFF // CH), silu_gate, linear=False, split=True)
            sweep(act, place, DFF // (2 * P) - 1, lambda at: split_free.head(act, at.after()), linear=False, split=True)
            place.skip(1, False, True)
            act.wait_ge(*reached("h_ready", 1))
            act_norm(act, 2)
            st.end()
            act_norm(act, 3)
            split_in_2.act_input(act, 2)
            split_in_2.head(act, Chunk(place, 0, 0, None))
            act.wait_ge(*reached("ba_multiplied", 1))
            act.activation(ba_rows, bank[4][0:8, :].rearrange("p (s t) -> p s t", s=2), ACT.Copy)
            copy_to = lambda base, func: lambda c, src: act.activation(proj[:, bass.ds(c * 2 + base, 2), :], src, func)
            evacuate(act, place, 12, copy_to(0, ACT.Copy), split=split_in_2, end=False)
            evacuate(act, place, 4, copy_to(T_GZ, ACT.Silu), split=split_in_2, end=False)
            st.end()
            aside = Aside(place, 2)
            dilated_or_gate = lambda c, src: copy_to(T_DQ, ACT.Copy)(c, src) if c < DIL_CHUNKS else copy_to(T_GATE2, ACT.Sigmoid)(c - DIL_CHUNKS, src)
            summed = 0
            for c in range(CONV_ASIDE):
                if c + 1 < CONV_ASIDE:
                    split_in_2.head(act, Chunk(place, c + 1, c + 1, None))
                aside.evacuate(act, c + 1, dilated_or_gate)
                if c == 0:
                    act.wait_ge(*reached("rates_loaded", 32))
                    act.activation(rate_col, rate_col, ACT.Exp).then_inc(sig("rate_exp"), 1)
                    act.activation(beta_rows, beta_rows, ACT.Sigmoid)
                    act.wait_ge(*reached("soft_abs", 1))
                    act.activation(soft_rows, soft_rows, ACT.Exp, scale=-1.0).then_inc(sig("soft_exp"), 1)
                    act.wait_ge(*reached("soft_exp", 1))
                    act.wait_ge(*reached("soft_one", 1))
                    act.activation(soft_rows, soft_rows, ACT.Ln).then_inc(sig("soft_ln"), 1)
                if c in (1, 2, 4, 5, 6, 7):
                    act.wait_ge(*reached("conv_summed", summed + 1))
                    act.activation(proj[:, 4 * summed:4 * summed + 4, :], w4(conv_units[summed]), ACT.Silu).then_inc(sig("conv_done"), 1)
                    summed += 1
                    if summed <= 4:
                        act.wait_ge(*reached("conv_done", summed))
                        act.activation(w4(conv_units[summed - 1]), proj[:, 4 * summed - 4:4 * summed, :], ACT.Square).then_inc(sig("qk_squared"), 1)
            act.wait_ge(*reached("qk_var", 1))
            act.activation(norm_rows[0:16, :], norm_rows[0:16, :], ACT.Sqrt).then_inc(sig("qk_root"), 1)
            st.end()
            act.wait_ge(*reached("rows_turned", 1))
            act.activation(gc_col, bank[0][:, 0:16].rearrange("p (c n) -> p c n", c=TB), ACT.Copy).then_inc(sig("cols_copied"), 1)
            act.activation(beta_col, bank[0][:, 16:32].rearrange("p (c n) -> p c n", c=TB), ACT.Copy).then_inc(sig("cols_copied"), 1)
            act.wait_ge(*reached("kd_log", 1))
            act.activation(kd_col, kd_col, ACT.Exp).then_inc(sig("kd_ready"), 1)
            st.end()
            for b in range(4):
                ch, h0 = b // 2, 4 * (b % 2)
                act.wait_ge(*reached("decay_log", b + 1))
                act.activation(g_xs, g_xs, ACT.Exp).then_inc(sig("decay_exp"), 1)
                if ch:
                    act.wait_ge(*reached("gc_spread", b + 1))
                    if b == 2:
                        act.wait_ge(*reached("g_state_made", 2))
                    act.activation(egrow, bank[7], ACT.Exp).then_inc(sig("eg_ready"), 1)
                g_solver.act(act, 4 + b, lambda lv: aside.evacuate(act, aside_chunks(b, 16 + 8 * lv), dilated_or_gate))
                act.wait_ge(*reached("g_solved", b + 1))
                act.activation(g_upd, bank[4], ACT.Copy).then_inc(sig("g_new_copied"), 1)
                aside.evacuate(act, aside_chunks(b, 64), dilated_or_gate)
                act.wait_ge(*reached("g_out_made", b + 1))
                act.activation(o_gdn[:, h0:h0 + 4, ch * P:(ch + 1) * P], heads4(bank[5]), ACT.Copy).then_inc(sig("g_out_copied"), 1)
            place.skip(CONV_ASIDE, split=True)
            place.skip(26 - CONV_ASIDE)
            st.end()
            for i, quad in enumerate(head_quads):
                act.activation(w4(i), quad, ACT.Square).then_inc(sig("head_squared"), 1)
            act.wait_ge(*reached("head_var", 1))
            act.activation(norm_rows, norm_rows, ACT.Sqrt).then_inc(sig("head_root"), 1)
            act.wait_ge(*reached("d_v_turned", 1))
            act.wait_ge(*reached("head_sums", 1))
            act.activation(dv_tok.rearrange("p c h n -> p (c h n)"), psum[:, 2:8, :].rearrange("p b n -> p (b n)"), ACT.Copy)
            st.end()
            for i in range(2):
                act.activation(out_2.first.xh[i], out_2.pieces[i], ACT.Copy).then_inc(sig("input_heads"), 1)
            for i, (b, slot_) in enumerate(dil_items):
                n = (b + 1) * P
                at = slot_ + 4 * b
                act.wait_ge(*reached("d_max_ready", i + 1))
                if i >= 2:
                    act.wait_ge(*reached("d_probs_turned", i - 1))
                act.activation(d_probs[i % 2][:, :, 0:n], d_logits[i % 2][:, :, 0:n], ACT.Exp, bias=d_max[:, at:at + 1],
                               accum_out=d_sum[:, at:at + 1]).then_inc(sig("d_probs_made"), 1)
                act.wait_ge(*reached("d_probs_turned", i + 1))
                if i:
                    act.wait_ge(*reached("d_mixed", i))
                act.activation(d_probs_t[:, :, 0:n], psum[:, 4:6, :].rearrange("p b n -> p (b n)")[:, 0:768].rearrange("p (g n) -> p g n", g=3)[:, :, 0:n],
                               ACT.Copy).then_inc(sig("d_probs_t_ready"), 1)
                if slot_ == 3:
                    act.wait_ge(*reached("d_turned", b + 1))
                    act.activation(y_dil[:, :, b * P:(b + 1) * P], heads4(bank[7]), ACT.Copy).then_inc(sig("y_dil_ready"), 1)
            st.end()
            act_out(act, place, out_2, 10, early=2)
            st.end()
            act_norm(act, 4)
            split_free.act_input(act, 3)
            split_free.head(act, Chunk(place, 0, 0, None))
            act.wait_ge(*reached("routed", 1))
            act.activation(sc_e, bank[0][:, 0:2 * EXPERTS].rearrange("p (b n) -> p b n", b=TB), ACT.Sigmoid).then_inc(sig("scores_ready"), 1)
            sweep(act, place, 2, lambda at: act_expert_chunk(act, at, 0, 0, at.c), linear=False, split=True)
            for c in range(SLOTS):
                at = Chunk(place, c, c, None)
                if c == 2:
                    act.wait_ge(*reached("combine_turned", 1))
                    act.activation(comb_t, bank[0][0:EXPERTS, 0:S], ACT.Copy).then_inc(sig("combine_copied"), 1)
                    act.wait_ge(*reached("combine_copied", 1))
                    act.dma_start(comb_dram, comb_t).then_inc(sig("combine_written"), 16)
                    act.wait_ge(*reached("combine_written", 16))
                    weights_row(act, 0, 0)
                act_expert_chunk(act, at, *step_of(at))
            place.skip(SLOTS, False, True)
            sweep(act, place, 3 * EXPERTS - SLOTS, lambda at: act_expert_chunk(act, at, *step_of(later(at))), linear=False, split=True)
            st.end()
            act.wait_ge(*reached("out_turned", 1))
            act.activation(out_tok[:, 0, :], psum[:, 4:6, :].rearrange("p b n -> p (b n)"), ACT.Copy).then_inc(sig("out_ready_0"), 1)
            st.end()

        @block.vector
        def _(dve):
            st = Stages(dve)
            link = Chain(dve, sig("dve_chain"))
            dve.wait_ge(*reached("x_turned", 2))
            dve.tensor_copy(h[:, :, 0:P], psum[:, 0:2, :].rearrange("p b (k t) -> p (b k) t", t=P))
            dve.wait_ge(*reached("vectors_turned", 1))
            link(dve.tensor_copy(vec[:, :], bank[4][:, 0:VA + VB + VC]))
            dve.tensor_scalar(one_less_ka, vec[:, VROWS["k_a"][0]:VROWS["k_a"][0] + RT], -1.0, 1.0, ALU.mult, ALU.add) \
               .then_inc(sig("one_less_ka_ready"), 1)
            st.end()
            dve_norm(dve, link, 0, lambda k: v("norm1_g", k))
            place = Stream()
            split_in.dve_input(dve, 0)
            sweep(dve, place, 2 * SLOTS, lambda at: split_in.rest(dve, at), split=True)
            mix = proj[:, 0:14, :]
            dve.wait_ge(*reached("idx_multiplied", 2))
            dve.wait_ge(evacuated, 2 + 7)
            last_chunks = 15 + GATES_FIRST - 2 * SLOTS
            for c in range(last_chunks):
                split_in.rest(dve, Chunk(place, c, c, None))
                if c < 2:
                    tl = slice(7 * c, 7 * c + 7)
                    dve.tensor_scalar(shifted[:, tl, 0:1], mix[:, tl, 0:1], -1.0, None, ALU.mult)
                    ins = dve.tensor_tensor(shifted[:, tl, 1:S], mix[:, tl, 0:S - 1], mix[:, tl, 1:S], ALU.subtract)
                    if c == 1:
                        link(ins)
                else:
                    for m in range(5 * (c - 2), min(5 * (c - 1), 14)):
                        ins = dve.scalar_tensor_tensor(out=mix[:, m, :], in0=shifted[:, m, :], scalar=v("tshift_mu", m), in1=mix[:, m, :],
                                                       op0=ALU.mult, op1=ALU.add)
            ins.then_inc(sig("token_shifted"), 1)
            place.skip(last_chunks, split=True)
            st.end()
            dve.wait_ge(*reached("token_shifted", 1))
            for m in range(RT):
                ins = dve.tensor_scalar(kk[:, m, :], proj[:, T_K + m, :], v("k_k", m), None, ALU.mult)
            ins.then_inc(sig("kk_raw"), 1)
            dve.wait_ge(*reached("decay_sig", 4))
            link(dve.tensor_scalar(decay_log, decay_log, -float(np.exp(-0.5)), None, ALU.mult))
            for m in range(RT):
                for c in range(TB):
                    ins = dve.tensor_tensor_scan(cum[:, m, c * P:(c + 1) * P], const("ones"), decay_log[:, m, c * P:(c + 1) * P],
                                                 0.0, ALU.mult, ALU.add)
            link(ins)
            cums = cum.rearrange("p m (c t) -> p m c t", c=TB)
            link(dve.tensor_copy(cend, cums[:, :, :, P - 1]))
            link(dve.tensor_scalar(mid, cend, 0.5, None, ALU.mult))
            dve.tensor_tensor(carry, mid[:, :, 0], mid[:, :, 1], ALU.add)
            flat = cum.rearrange("p m (c t) -> p (m c) t", c=TB)
            dve.tensor_tensor(flat, flat, small[:, 8:16].rearrange("p (n o) -> p n o", o=1).to_broadcast([P, 8, P]), ALU.subtract) \
               .then_inc(sig("cum_ready"), 1)
            dve.wait_ge(*reached("cum_ready", 1))
            dve.tensor_tensor(cum_prev, cum, decay_log, ALU.subtract).then_inc(sig("cum_ready"), 1)
            dve.wait_ge(*reached("kk_norm", 1))
            link(dve.tensor_scalar(sq, sq, 1e-12, None, ALU.max))
            link(dve.reciprocal(sq, sq))
            link(dve.tensor_tensor(kk, kk, sq, ALU.mult))
            dve.wait_ge(*reached("exps", 3))
            tiles = lambda ap: ap.rearrange("p m (c t) -> p m c t", c=TB)
            for m in range(RT):
                dve.tensor_tensor(ar[:, m, :, 0, :], tiles(kk)[:, m], tiles(e3)[:, m], ALU.mult)
                dve.tensor_tensor(ar[:, m, :, 1, :], proj[:, T_R + m, :].rearrange("p (c t) -> p c t", c=TB), tiles(e1)[:, m], ALU.mult)
            link(dve.tensor_tensor(b_til, kk, a_gate, ALU.mult))
            dve.tensor_tensor(b_til, b_til, e2, ALU.mult).then_inc(sig("bk_ready"), 1)
            dve.wait_ge(*reached("k2_ready", 1))
            dve.tensor_tensor(k_til, k2, e2, ALU.mult).then_inc(sig("bk_ready"), 1)
            dve.wait_ge(*reached("bonus_summed", 1))
            dve.tensor_tensor(bonus, psum[:, 4:6, :].rearrange("p b (m t) -> p (b m) t", t=S), proj[:, T_V:T_V + RT, :], ALU.mult)
            st.end()
            for b in range(4):
                ch, m0 = batch(b)
                if b:
                    dve.wait_ge(*reached("y_made", b))
                for i in range(4):
                    dve.wait_ge(*reached("prods_made", 4 * b + i + 1))
                    dve.tensor_tensor(prods[:, i, :].rearrange("p (s n) -> p s n", s=2), bank[i].rearrange("p (s n) -> p s n", s=2),
                                      spread(const("upper"), 2), ALU.mult).then_inc(sig("prods_masked"), 1)
                dve.wait_ge(*reached("prods_masked", 4 * (b + 1)))
                rwkv_solver.dve(dve, link, b)
                if ch == 0:
                    dve.wait_ge(*reached("state_made", b + 1))
                    for i in range(2):
                        dve.scalar_tensor_tensor(out=state[:, m0 + i, :], in0=bank[6][:, i * P:(i + 1) * P], scalar=carry[:, m0 + i:m0 + i + 1],
                                                 in1=const("head_ones"), op0=ALU.mult, op1=ALU.mult).then_inc(sig("state_ready"), 1)
            y3 = y_tok.rearrange("p c n -> p (c n)").rearrange("p (g n) -> p g n", n=HD)
            yc = w4(0).rearrange("p m t -> p (m t)").rearrange("p (g n) -> p g n", n=HD)
            y2 = w4(1).rearrange("p m t -> p (m t)").rearrange("p (g n) -> p g n", n=HD)
            wide = lambda ap: ap.rearrange("p (g o) -> p g o", o=1).to_broadcast([P, 16, HD])
            dve.wait_ge(*reached("y_copied", 4))
            link(dve.tensor_reduce(stat, y3, AX.X, ALU.add))
            link(dve.tensor_scalar(stat, stat, 1.0 / HD, None, ALU.mult))
            dve.tensor_tensor(yc, y3, wide(stat), ALU.subtract).then_inc(sig("y_centred"), 1)
            dve.wait_ge(*reached("y_squared", 1))
            link(dve.tensor_reduce(stat2, y2, AX.X, ALU.add))
            dve.tensor_scalar(stat2, stat2, 1.0 / HD, 64e-5, ALU.mult, ALU.add).then_inc(sig("y_var"), 1)
            dve.wait_ge(*reached("y_std", 1))
            link(dve.reciprocal(stat2, stat2))
            dve.tensor_tensor(yc, yc, wide(stat2), ALU.mult).then_inc(sig("y_normed"), 1)
            dve.wait_ge(*reached("y_affine", 4))
            link(dve.tensor_tensor(y_rwkv, w4(2), bonus, ALU.add))
            dve.tensor_tensor(y_rwkv, y_rwkv, g_gate, ALU.mult)
            st.end()
            for i, t in enumerate(rope_tiles):
                n = t.shape[1]
                dve.wait_ge(*reached("rotated", i + 1))
                dve.wait_ge(*reached("rope_cos", i + 1))
                link(dve.tensor_tensor(t, bank[i][:, 0:n * S].rearrange("p (m t) -> p m t", t=S), spread(const("sin"), n), ALU.mult))
                dve.tensor_tensor(t, t, rope_tmp[:, i, 0:n * S].rearrange("p (m t) -> p m t", t=S), ALU.add)
            st.end()
            for b in range(TB):
                n = (b + 1) * P
                dve.wait_ge(*reached("idx_relu", 4 * (b + 1)))
                for hd in range(HEADS):
                    bk, half = place_of(hd)
                    src, w = pair_view(relu_s[:, bk, :], n)[:, half, :], w_idx[:, b, hd:hd + 1]
                    if hd == 0:
                        link(dve.tensor_scalar(score[:, 0:n], src, w, None, ALU.mult))
                    else:
                        link(dve.scalar_tensor_tensor(out=score[:, 0:n], in0=src, scalar=w, in1=score[:, 0:n], op0=ALU.mult, op1=ALU.add))
                dve.tensor_tensor(score[:, n - P:n], score[:, n - P:n], own_causal, ALU.add).then_inc(sig("idx_summed"), 1)
                dve.wait_ge(*reached("idx_summed", b + 1))
                left = score
                for _ in range(TOPK // 8):
                    link(dve.max(top8, left[:, 0:n]))
                    link(dve.match_replace(out=rest[:, 0:n], in_to_replace=top8, in_values=left[:, 0:n], imm_value=-3.0e38))
                    left = rest
                link(dve.tensor_tensor(sel_bias[:, 0:n], rest[:, 0:n], score[:, 0:n], ALU.not_equal))
                link(dve.tensor_scalar(sel_bias[:, 0:n], sel_bias[:, 0:n], -1.0, -NEG, ALU.add, ALU.mult))
                link(dve.tensor_tensor(sel_bias[:, n - P:n], sel_bias[:, n - P:n], own_causal, ALU.add))
                dve.wait_ge(*reached("att_scored", b + 1))
                for bk in range(4):
                    ins = dve.scalar_tensor_tensor(out=pair_view(logits[:, bk, :], n), in0=pair_view(bank[4 + bk], n), scalar=float(HD) ** -0.5,
                                                   in1=spread(sel_bias[:, 0:n], 2), op0=ALU.mult, op1=ALU.add)
                link(ins)
                link(dve.tensor_reduce(row_max, logits.rearrange("p b (i n) -> p (b i) n", i=2)[:, :, 0:n], AX.X, ALU.max))
                dve.tensor_scalar(row_max, row_max, -1.0, None, ALU.mult).then_inc(sig("row_max"), 1)
                dve.wait_ge(*reached("probs_made", HEADS * (b + 1)))
                link(dve.reciprocal(row_sum, row_sum))
                dve.wait_ge(*reached("att_made", b + 1))
                dve.tensor_tensor(att_tok.rearrange("p (i d) -> p i d", d=HD), bank[4].rearrange("p (i d) -> p i d", d=HD),
                                  row_sum.rearrange("p (i o) -> p i o", o=1).to_broadcast([P, HEADS, HD]), ALU.mult).then_inc(sig("att_normed"), 1)
            st.end()
            place.skip(24, False)
            place.skip(8 - GATES_FIRST)
            wide_tiles = lambda at: psum[:, 2 * at.parity:2 * at.parity + 2, :].rearrange("p b (m t) -> p (b m) t", t=S)
            two_tiles = lambda at: bank[2 * at.parity].rearrange("p (m t) -> p m t", t=S)
            dve_out(dve, place, out_1, 8,
                    lambda c, at: dve.tensor_tensor(merged[:, 4 * c:4 * c + 4, :], wide_tiles(at), proj[:, T_GATE + 4 * c:T_GATE + 4 * c + 4, :], ALU.mult),
                    lambda c, at: dve.tensor_tensor(h[:, 2 * c:2 * c + 2, :], two_tiles(at), h[:, 2 * c:2 * c + 2, :], ALU.add))
            st.end()
            dve.drain().then_inc(sig("pair_evacuated"), 3)
            dve_norm(dve, link, 1, lambda k: v("norm2_g", k))
            split_free.dve_input(dve, 1)
            split_free.rest(dve, Chunk(place, 0, 0, None))
            dve.wait_ge(*reached("mods_turned", 1))
            by_chunk = lambda ap: ap.rearrange("p (t q m) -> p t q m", q=3, m=2)
            link(dve.tensor_tensor(by_chunk(mods), bank[6][:, 0:48].rearrange("p (t m q) -> p t q m", m=2, q=3), by_chunk(vec[:, VA:VA + VB]), ALU.add))
            for gain, name, at in ((gain1, "g_mix_2", KD), (gain2, "g_ffn_2", 4 * KD)):
                link(dve.tensor_scalar(gain, mods[:, at:at + KD], 1.0, None, ALU.add))
                link(dve.tensor_tensor(gain, gain, vec[:, VROWS[name][0]:VROWS[name][0] + KD], ALU.mult))

            def up_product(at):
                split_free.rest(dve, at.after())
                if at.j % 2 == 1:
                    dve.wait_ge(multiplied, at.n + 1)
                    dve.wait_ge(*reached("gate_silu", at.pair + 1))
                    dst = ffn_tmp[at.j // 2 % 3]
                    dve.tensor_tensor(dst, dst, bank[at.j // 2 % 3 * 2 + 1].rearrange("p (m t) -> p m t", t=S), ALU.mult) \
                       .then_inc(sig("pair_evacuated"), 1)
            sweep(dve, place, 2 * (DFF // CH), up_product, linear=False, split=True)
            sweep(dve, place, DFF // (2 * P) - 1, lambda at: split_free.rest(dve, at.after()), linear=False, split=True)
            place.skip(1, False, True)
            dve.wait_ge(multiplied, place.n)
            link(dve.tensor_tensor(h[:, :, :], h[:, :, :], psum[:, 0:4, :].rearrange("p b (m t) -> p (b m) t", t=S), ALU.add))
            dve.drain().then_inc(sig("h_ready"), 1)
            dve.wait_ge(*reached("h_ready", 1))
            dve_norm(dve, link, 2, lambda k: v("normf_g", k), dst=h)
            st.end()
            dve_norm(dve, link, 3, lambda k: gain1[:, k:k + 1], lambda k: mods[:, k:k + 1])
            split_in_2.dve_input(dve, 2)
            sweep(dve, place, 16, lambda at: split_in_2.rest(dve, at), split=True)
            place.skip(CONV_ASIDE, split=True)
            place.skip(26 - CONV_ASIDE)
            st.end()
            def tap(j, tile):
                at = VA + VB + j * 3 * GH + tile
                return vec[:, at:at + 1]
            for i, un in enumerate(conv_units):
                acc = w4(un)
                for m in range(4):
                    ins = dve.tensor_scalar(acc[:, m, :], proj[:, 4 * i + m, :], tap(3, 4 * i + m), None, ALU.mult)
                for back in range(1, 4):
                    link(ins)
                    for m in range(4):
                        tile = 4 * i + m
                        ins = dve.scalar_tensor_tensor(out=acc[:, m, back:S], in0=proj[:, tile, 0:S - back], scalar=tap(3 - back, tile),
                                                       in1=acc[:, m, back:S], op0=ALU.mult, op1=ALU.add)
                ins.then_inc(sig("conv_summed"), 1)
                if i == 0:
                    dve.wait_ge(*reached("rates_loaded", 32))
                    link(dve.tensor_scalar(rate_rows, rate_rows, dt_col, None, ALU.add))
                    dve.scalar_tensor_tensor(out=soft_rows, in0=rate_rows, scalar=-1.0, in1=rate_rows, op0=ALU.mult, op1=ALU.max).then_inc(sig("soft_abs"), 1)
                    link(dve.tensor_scalar(rate_rows, rate_rows, 0.0, None, ALU.max))
                    dve.wait_ge(*reached("soft_exp", 1))
                    dve.tensor_scalar(soft_rows, soft_rows, 1.0, None, ALU.add).then_inc(sig("soft_one"), 1)
                    dve.wait_ge(*reached("soft_ln", 1))
                    link(dve.tensor_tensor(rate_rows, rate_rows, soft_rows, ALU.add))
                    dve.wait_ge(*reached("rate_exp", 1))
                    link(dve.tensor_scalar(rate_rows, rate_rows, rate_col, -1.0, ALU.mult, ALU.mult))
                    for c in range(TB):
                        at = slice(c * P, (c + 1) * P)
                        dve.tensor_tensor_scan(gc_rows[:, at], const("ones", GH), rate_rows[:, at], 0.0, ALU.mult, ALU.add)
            dve.wait_ge(*reached("qk_row_sums", 1))
            dve.tensor_scalar(norm_rows[0:16, :], bank[0][0:16, 0:S], 1e-6, None, ALU.add).then_inc(sig("qk_var"), 1)
            dve.wait_ge(*reached("qk_root", 1))
            link(dve.reciprocal(norm_rows[0:16, :], norm_rows[0:16, :]))
            link(dve.tensor_scalar(norm_rows[0:8, :], norm_rows[0:8, :], float(P) ** -0.5, None, ALU.mult))
            st.end()
            def pair_of_heads(src):
                return src.rearrange("p (h c t) -> p h c t", h=2, c=TB)
            tiles = lambda base, i: proj[:, base + 2 * i:base + 2 * i + 2, :].rearrange("p h (c t) -> p h c t", c=TB)
            for i in range(4):
                dve.wait_ge(*reached("spread", 3 * i + 1))
                for hh in range(2):
                    dve.tensor_tensor(kq[:, 2 * i + hh, :, 1, :], tiles(T_GQ, i)[:, hh], pair_of_heads(bank[1])[:, hh], ALU.mult) \
                       .then_inc(sig("spread_used"), 1)
                dve.wait_ge(*reached("spread", 3 * i + 2))
                link(dve.tensor_tensor(tiles(T_GK, i), tiles(T_GK, i), pair_of_heads(bank[2]), ALU.mult))
                dve.wait_ge(*reached("spread", 3 * i + 3))
                for hh in range(2):
                    dve.tensor_tensor(kq[:, 2 * i + hh, :, 0, :], tiles(T_GK, i)[:, hh], pair_of_heads(bank[3])[:, hh], ALU.mult) \
                       .then_inc(sig("spread_used"), 1)
            dve.wait_ge(*reached("spread_used", 16))
            dve.drain().then_inc(sig("keys_ready"), 1)
            dve.wait_ge(*reached("cols_copied", 2))
            for c in range(TB):
                dve.wait_ge(*reached("gv_turned", c + 1))
                src = psum[:, 4 + 2 * c:6 + 2 * c, :].rearrange("p b (h n) -> p (b h) n", n=P)
                dve.tensor_tensor(vb_tok[:, c], src, beta_col[:, c, :].rearrange("p (h o) -> p h o", o=1).to_broadcast([P, GH, P]), ALU.mult) \
                   .then_inc(sig("vb_ready"), 1)
            dve.wait_ge(*reached("rows_turned", 1))
            dve.tensor_tensor(kd_col, bank[0][:, 64:72], gc_col[:, 0, :], ALU.subtract).then_inc(sig("kd_log"), 1)
            dve.wait_ge(*reached("kd_ready", 1))
            dve.wait_ge(*reached("gk_turned", 1))
            dve.tensor_tensor(kd_tok, psum[:, 4:6, :].rearrange("p b (h n) -> p (b h) n", n=P),
                              kd_col.rearrange("p (h o) -> p h o", o=1).to_broadcast([P, GH, P]), ALU.mult)
            st.end()
            for b in range(4):
                ch, h0 = b // 2, 4 * (b % 2)
                dve.wait_ge(*reached("gc_spread", b + 1))
                if b:
                    dve.wait_ge(*reached("g_solved", b))
                for i in range(4):
                    ins = dve.tensor_scalar(heads4(g_xs)[:, i, :], bank[7][:, i * P:(i + 1) * P], gc_col[:, ch, h0 + i:h0 + i + 1], 0.0,
                                            ALU.subtract, ALU.min)
                ins.then_inc(sig("decay_log"), 1)
                dve.wait_ge(*reached("decay_masked", b + 1))
                dve.wait_ge(*reached("g_prods_made", b + 1))
                if b:
                    dve.wait_ge(*reached("g_out_made", b))
                dve.tensor_tensor(g_prods, psum[:, 0:2, :].rearrange("p b (h s t) -> p (b h) s t", h=2, s=2), decays, ALU.mult) \
                   .then_inc(sig("g_prods_ready"), 1)
                dve.wait_ge(*reached("g_prods_ready", b + 1))
                if ch:
                    dve.wait_ge(*reached("eg_ready", b - 1))
                    eg = heads4(egrow)
                    for sd in range(2):
                        ins = dve.tensor_tensor(kq[:, h0:h0 + 4, 1, sd, :], kq[:, h0:h0 + 4, 1, sd, :], eg, ALU.mult)
                    ins.then_inc(sig("kq_decayed"), 1)
                g_solver.dve(dve, link, 4 + b)
                if ch:
                    dve.wait_ge(*reached("g_carried", b - 1))
                    dve.tensor_tensor(heads4(g_xs), vb_tok[:, 1, h0:h0 + 4, :], heads4(bank[7]), ALU.subtract).then_inc(sig("g_right"), 1)
                else:
                    dve.wait_ge(*reached("g_state_made", b + 1))
                    dve.tensor_copy(g_state[:, h0:h0 + 4, :], heads4(bank[6])).then_inc(sig("g_state_ready"), 1)
            st.end()
            dve.wait_ge(*reached("head_sums", 1))
            dve.tensor_scalar(norm_rows, bank[0][0:NORMED, 0:S], 1.0 / P, 1e-6, ALU.mult, ALU.add).then_inc(sig("head_var"), 1)
            dve.wait_ge(*reached("head_root", 1))
            dve.reciprocal(norm_rows, norm_rows).then_inc(sig("head_inverse"), 1)
            for i, pair in enumerate(head_pairs):
                dve.wait_ge(*reached("head_spread", i + 1))
                inverse = bank[i % 2].rearrange("p (m t) -> p m t", t=S)
                gain = v("gdn_norm_g_2" if i < GH // 2 else "dil_q_norm_g_2" if i < (GH + DH) // 2 else "dil_k_norm_g_2")
                dve.scalar_tensor_tensor(out=pair, in0=pair, scalar=gain, in1=inverse, op0=ALU.mult, op1=ALU.mult).then_inc(sig("head_normed"), 1)
                if i < GH // 2:
                    dve.wait_ge(*reached("head_normed", i + 1))
                    gate = y_gdn[:, 2 * i:2 * i + 2, :]
                    dve.tensor_tensor(gate, pair, gate, ALU.mult)
            st.end()
            for i in range(2):
                out_2.first.input_rest(dve, i, out_2.before + i, out_2.pieces[i])
            for i, (b, slot_) in enumerate(dil_items):
                n = (b + 1) * P
                at = slot_ + 4 * b
                mask = dil_masks[:, :, P * (1 - b):2 * P]
                dve.wait_ge(*reached("d_scored", i + 1))
                if i >= 2:
                    dve.wait_ge(*reached("d_probs_made", i - 1))
                src = psum[:, 2 * (i % 2):2 * (i % 2) + 2, :].rearrange("p b n -> p (b n)")[:, 0:768].rearrange("p (g n) -> p g n", g=3)[:, :, 0:n]
                dve.scalar_tensor_tensor(out=d_logits[i % 2][:, :, 0:n], in0=src, scalar=float(P) ** -0.5, in1=mask, op0=ALU.mult, op1=ALU.add) \
                   .then_inc(sig("d_logits_ready"), 1)
                dve.wait_ge(*reached("d_logits_ready", i + 1))
                link(dve.tensor_reduce(d_max[:, at:at + 1], d_logits[i % 2][:, :, 0:n], AX.XY, ALU.max))
                dve.tensor_scalar(d_max[:, at:at + 1], d_max[:, at:at + 1], -1.0, None, ALU.mult).then_inc(sig("d_max_ready"), 1)
                if slot_ == 3:
                    dve.wait_ge(*reached("d_probs_made", i + 1))
                    link(dve.reciprocal(d_sum[:, 4 * b:4 * b + 4], d_sum[:, 4 * b:4 * b + 4]))
                    dve.wait_ge(*reached("d_mixed", i + 1))
                    if b:
                        dve.wait_ge(*reached("d_turned", b))
                    dve.tensor_tensor(heads4(d_tok), heads4(bank[6]), d_sum[:, 4 * b:4 * b + 4].rearrange("p (h o) -> p h o", o=1).to_broadcast([P, 4, P]),
                                      ALU.mult).then_inc(sig("d_scaled"), 1)
            st.end()

            def into_h(c, at):
                for m in range(2):
                    k = 2 * c + m
                    ins = dve.scalar_tensor_tensor(out=h[:, k, :], in0=bank[2 * at.parity][:, m * S:(m + 1) * S], scalar=mods[:, 2 * KD + k:2 * KD + k + 1],
                                                   in1=h[:, k, :], op0=ALU.mult, op1=ALU.add)
                return ins
            dve_out(dve, place, out_2, 10,
                    lambda c, at: dve.tensor_tensor(merged[:, 2 * c:2 * c + 2, :], two_tiles(at), proj[:, T_GATE2 + 2 * c:T_GATE2 + 2 * c + 2, :], ALU.mult),
                    into_h, early=2)
            st.end()
            dve_norm(dve, link, 4, lambda k: gain2[:, k:k + 1], lambda k: mods[:, 3 * KD + k:3 * KD + k + 1])
            split_free.dve_input(dve, 3)
            for c in range(2):
                split_free.rest(dve, Chunk(place, c, c, None))
            dve.drain().then_inc(sig("au_free"), 2)
            dve.drain().then_inc(sig("hid_ready"), 1)
            dve.wait_ge(*reached("router_loaded", 32))
            dve.wait_ge(*reached("scores_ready", 1))
            link(dve.tensor_tensor(sel_e, sc_e, spread(router_b, TB), ALU.add))
            for b in range(TB):
                for g in range(GROUPS):
                    ins = dve.max(best_e[:, b, g, :], sel_e[:, b, g * 8:(g + 1) * 8])
            link(ins)
            link(dve.tensor_tensor(gs_e, best_e[:, :, :, 0], best_e[:, :, :, 1], ALU.add))
            dve_expert_chunk(dve, Chunk(place, 1, 1, None), 0, 0, 1)
            place.skip(2, False, True)
            at = Chunk(place, 0, 0, None)
            dve_expert_chunk(dve, at, *step_of(at))
            other = gs_e.rearrange("p b (o j) -> p b o j", o=1).to_broadcast([P, TB, GROUPS, GROUPS])
            across = lambda ap: ap.rearrange("p b (g o) -> p b g o", o=1).to_broadcast([P, TB, GROUPS, GROUPS])
            eight = lambda ap: ap.rearrange("p b (g n) -> p b g n", g=GROUPS)
            dve.tensor_tensor(more_e, other, across(gs_e), ALU.is_gt)
            link(dve.tensor_tensor(same_e, other, across(gs_e), ALU.is_equal))
            link(dve.tensor_tensor(same_e, same_e, const("before").rearrange("p (o g j) -> p o g j", o=1, g=GROUPS).to_broadcast([P, TB, GROUPS, GROUPS]), ALU.mult))
            link(dve.tensor_tensor(more_e, more_e, same_e, ALU.add))
            link(dve.tensor_reduce(rank_e, more_e, AX.X, ALU.add))
            link(dve.tensor_scalar(rank_e, rank_e, float(TOP_G), None, ALU.is_lt))
            link(dve.tensor_tensor(eight(sel_e), eight(sel_e), across(rank_e), ALU.mult))
            link(dve.tensor_scalar(rank_e, rank_e, -1.0, -NEG, ALU.add, ALU.mult))
            link(dve.tensor_tensor(eight(sel_e), eight(sel_e), across(rank_e), ALU.add))
            for b in range(TB):
                ins = dve.max(top_e[:, b, :], sel_e[:, b, :])
            link(ins)
            for b in range(TB):
                ins = dve.match_replace(out=left_e[:, b, :], in_to_replace=top_e[:, b, :], in_values=sel_e[:, b, :], imm_value=-3.0e38)
            link(ins)
            link(dve.tensor_tensor(comb_e, left_e, sel_e, ALU.not_equal))
            link(dve.tensor_tensor(comb_e, comb_e, sc_e, ALU.mult))
            link(dve.tensor_reduce(sum_e, comb_e, AX.X, ALU.add))
            link(dve.reciprocal(sum_e, sum_e))
            for b in range(TB):
                dve.tensor_scalar(comb_e[:, b, :], comb_e[:, b, :], sum_e[:, b:b + 1], ROUTE_SCALE, ALU.mult, ALU.mult).then_inc(sig("combine_ready"), 1)

            for c in range(1, SLOTS):
                at = Chunk(place, c, c, None)
                dve_expert_chunk(dve, at, *step_of(at))
            place.skip(SLOTS, False, True)
            sweep(dve, place, 3 * EXPERTS - SLOTS, lambda at: dve_expert_chunk(dve, at, *step_of(later(at))), linear=False, split=True)
            st.end()
            for k in range(KD):
                ins = dve.scalar_tensor_tensor(out=h[:, k, :], in0=bank[k // 2][:, k % 2 * S:(k % 2 + 1) * S], scalar=mods[:, 5 * KD + k:5 * KD + k + 1],
                                               in1=h[:, k, :], op0=ALU.mult, op1=ALU.add)
            ins.then_inc(sig("h_final"), 1)
            dve.wait_ge(*reached("out_turned", 2))
            dve.tensor_copy(out_tok[:, 1, :], psum[:, 6:8, :].rearrange("p b n -> p (b n)")).then_inc(sig("out_ready_1"), 1)
            st.end()

        @block.tensor
        def _(pe):
            st = Stages(pe)
            place = Stream()
            pe.wait_ge(*reached("x_loaded", 16))
            pe.wait_ge(*reached("consts_loaded", 16))
            x_tok = work[:, 0:2, :]
            for b in range(TB):
                for k in range(KD):
                    last = pe.transpose(bank[2 * b + k // 4][:, k % 4 * P:(k % 4 + 1) * P], x_tok[:, b, k * P:(k + 1) * P], ident)
                last.then_inc(sig("x_turned"), 1)
            pe.wait_ge(*reached("vectors_loaded", 16 * (len(VROWS) + 2)))
            stage = work[:, 2, :]
            for n, at, o in ((VA, 0, 0), (VB, P, VA), (VC, 2 * P, VA + VB)):
                last = pe.transpose(bank[4][:, o:o + n], stage[0:n, at:at + P], ident[0:n, 0:n])
            last.then_inc(sig("vectors_turned"), 1)
            st.end()
            pe_norm(pe, 0)
            pe.wait_ge(*reached("u_ready", 2 * 1))
            pe.wait_ge(*reached("idxw_loaded", 16))
            for half in range(2):
                for k in range(KD):
                    last = pe.matmul(bank[4][64 * half:64 * half + 64, 0:S], idxw[:, k, 0:HD], u[:, k, :], start=(k == 0), stop=(k == KD - 1))
            last.then_inc(sig("idx_multiplied"), 1)
            for b in range(TB):
                for k in range(KD):
                    last = pe.matmul(bank[5][:, b * HEADS:(b + 1) * HEADS], u[:, k, b * P:(b + 1) * P], idxw[:, k, HD:HD + HEADS],
                                     start=(k == 0), stop=(k == KD - 1))
            last.then_inc(sig("idx_multiplied"), 1)
            pe_linear_split(pe, place, 15 + GATES_FIRST, split_in, 0)
            st.end()
            pe.wait_ge(*reached("lora_loaded", 48))
            pe.wait_ge(*reached("token_shifted", 1))
            pe.wait_ge(*reached("lora_in", 2))
            for m in range(RT):
                at = slice(m % 2 * S, (m % 2 + 1) * S)
                pe.matmul(bank[m // 2][:, at], lora[0:64, 0, m * P:(m + 1) * P], tanh_wd[0:64, :], start=True, stop=True)
                pe.matmul(bank[2 + m // 2][:, at], lora[64:128, 0, m * P:(m + 1) * P], proj[64:128, T_WA, :], start=True, stop=True)
                last = pe.matmul(bank[4 + m // 2][:, at], lora[:, 1, m * P:(m + 1) * P], sig_gd, start=True, stop=True)
            last.then_inc(sig("lora_out"), 1)
            pe.wait_ge(*reached("kk_squared", 1))
            for m in range(RT):
                last = pe.matmul(bank[6 + m // 2][:, m % 2 * S:(m % 2 + 1) * S], const("head_ones"), sq[:, m, :], start=True, stop=True)
            last.then_inc(sig("kk_summed"), 1)
            pe.wait_ge(*reached("bonus_terms", 4))
            pe.wait_ge(*reached("g_copied", 1))
            for m in range(RT):
                last = pe.matmul(bank[4 + m // 2][:, m % 2 * S:(m % 2 + 1) * S], const("head_ones"), bonus[:, m, :], start=True, stop=True)
            last.then_inc(sig("bonus_summed"), 1)
            pe.wait_ge(*reached("decay_sig", 4))
            for c in range(TB):
                for m in range(RT):
                    last = pe.transpose(bank[c][:, m * P:(m + 1) * P], proj[:, T_V + m, c * P:(c + 1) * P], ident)
                last.then_inc(sig("v_turned"), 1)
            pe.wait_ge(*reached("a_gate_ready", 4))
            for i, til in enumerate((b_til, k_til)):
                pe.wait_ge(*reached("bk_ready", i + 1))
                for m in range(RT):
                    last = pe.transpose(bank[2 + i][:, m * P:(m + 1) * P], til[:, m, 0:P], ident)
                last.then_inc(sig("bk_turned"), 1)
            st.end()
            aside = Aside(place, 7)
            for b in range(4):
                ch, m0 = batch(b)
                for i in range(4):
                    m, half = m0 + i // 2, slice(64 * (i % 2), 64 * (i % 2) + 64)
                    if b:
                        pe.wait_ge(*reached("prods_masked", 4 * (b - 1) + i + 1))
                    rhs = ar[half, m, ch, :, :]
                    pe.matmul(bank[i][:, 0:256], b_til[half, m, ch * P:(ch + 1) * P], rhs, start=True, stop=True)
                    pe.matmul(bank[i][:, 256:512], k_til[half, m, ch * P:(ch + 1) * P], rhs, start=True, stop=True) \
                      .then_inc(sig("prods_made"), 1)
                rwkv_solver.pe(pe, b, lambda lv, wait: aside.modulate(pe, (lv + wait > 0) + (lv + wait == 6)))
                pe.wait_ge(*reached("mod_copied", 6 * (b + 1)))
                if ch:
                    pe.wait_ge(*reached("state_ready", 4))
                    for i in range(2):
                        pe.matmul(bank[7][:, i * P:(i + 1) * P], ar[:, m0 + i, ch, 0, :], state[:, m0 + i, :],
                                  start=(i == 0), stop=False, skip_group_check=True)
                for i in range(4):
                    last = pe.matmul(bank[7][:, i * HD:(i + 1) * HD], prods[:, i, 256:384], v_tok[:, ch, m0 * P + i * HD:m0 * P + (i + 1) * HD],
                                     start=(ch == 0 and i == 0), stop=(i == 3), skip_group_check=True)
                last.then_inc(sig("x_made"), 1)
                pe.wait_ge(*reached("x_copied", b + 1))
                pe.wait_ge(*reached("inv_updated", 11 * (b + 1)))
                for i in range(4):
                    last = pe.matmul(bank[4][:, i * HD:(i + 1) * HD], inv_t[:, i * P:(i + 1) * P], xs[:, i * HD:(i + 1) * HD], start=True, stop=True)
                last.then_inc(sig("sa_made"), 1)
                pe.wait_ge(*reached("sa_copied", b + 1))
                first = True
                if ch:
                    for i in range(2):
                        pe.matmul(bank[5][:, i * P:(i + 1) * P], ar[:, m0 + i, ch, 1, :], state[:, m0 + i, :],
                                  start=(i == 0), stop=False, skip_group_check=True)
                    first = False
                for i in range(4):
                    pe.matmul(bank[5][:, i * HD:(i + 1) * HD], prods[:, i, 384:512], v_tok[:, ch, m0 * P + i * HD:m0 * P + (i + 1) * HD],
                              start=(first and i == 0), stop=False, skip_group_check=True)
                    last = pe.matmul(bank[5][:, i * HD:(i + 1) * HD], prods[:, i, 128:256], sa[:, i * HD:(i + 1) * HD],
                                     start=False, stop=(i == 3), skip_group_check=True)
                last.then_inc(sig("y_made"), 1)
                if ch == 0:
                    for i in range(2):
                        pe.matmul(bank[6][:, i * P:(i + 1) * P], bk_tok[:, 0, (m0 + i) * P:(m0 + i + 1) * P], sa[:, i * P:(i + 1) * P],
                                  start=True, stop=False)
                        last = pe.matmul(bank[6][:, i * P:(i + 1) * P], bk_tok[:, 1, (m0 + i) * P:(m0 + i + 1) * P],
                                         v_tok[:, ch, (m0 + i) * P:(m0 + i + 1) * P], start=False, stop=True)
                    last.then_inc(sig("state_made"), 1)
                    pe.wait_ge(*reached("state_ready", 2 * (b + 1)))
                pe.wait_ge(*reached("y_copied", b + 1))
            place.skip(24, False)
            pe.wait_ge(*reached("y_normed", 1))
            for c in range(TB):
                for m in range(RT):
                    last = pe.transpose(bank[c][:, m * P:(m + 1) * P], w4(0).rearrange("p m t -> p (m t)")[:, c * RW + m * P:c * RW + (m + 1) * P], ident)
                last.then_inc(sig("y_turned"), 1)
            st.end()
            for i, t in enumerate(rope_tiles):
                n = t.shape[1] * S
                pe.matmul(bank[i][:, 0:n], const("rot"), t, start=True, stop=True).then_inc(sig("rotated"), 1)
            for c in range(TB):
                if c:
                    pe.wait_ge(*reached("att_v_copied", c))
                for m in range(RT):
                    last = pe.transpose(bank[7][:, m * P:(m + 1) * P], proj[:, T_AV + m, c * P:(c + 1) * P], ident)
                last.then_inc(sig("att_v_turned"), 1)
            st.end()
            aside = Aside(place, 2)
            for b in range(TB):
                n = (b + 1) * P
                if b:
                    pe.wait_ge(*reached("probs_t_ready", 1))
                pe_scores(pe, 0, T_QI, lambda hd: kidx, b, n).then_inc(sig("idx_scored"), 1)
                if b:
                    pe.wait_ge(*reached("att_normed", b))
                    pe.wait_ge(*reached("y_att_copied", b))
                pe_scores(pe, 4, T_Q, lambda hd: proj[:, T_AK + hd // 2, :], b, n).then_inc(sig("att_scored"), 1)
                pe.wait_ge(*reached("idx_relu", 4 * (b + 1)))
                aside.multiply(pe, GATES_ASIDE * 2 * KD)
                pe.wait_ge(evacuated, place.linear + GATES_ASIDE * (b + 1) + 2)
                pe.wait_ge(*reached("probs_made", HEADS * (b + 1)))
                for kb in range(b + 1):
                    for i in range(HEADS):
                        last = pe.transpose(bank[2 * kb + i // 4][:, i % 4 * P:(i % 4 + 1) * P],
                                            pair_view(probs[:, i // 2, :], n)[:, i % 2, kb * P:(kb + 1) * P], ident)
                last.then_inc(sig("probs_turned"), 1)
                pe.wait_ge(*reached("probs_t_ready", b * (b + 1) // 2 + b + 1))
                for i in range(HEADS):
                    hd = head_at(i)
                    for kb in range(b + 1):
                        last = pe.matmul(bank[4][:, hd * HD:(hd + 1) * HD], probs_t[:, kb, i, :], att_v[:, kb, hd * HD:(hd + 1) * HD],
                                         start=(kb == 0), stop=(kb == b))
                last.then_inc(sig("att_made"), 1)
                pe.wait_ge(*reached("att_normed", b + 1))
                for m in range(RT):
                    last = pe.transpose(bank[5][:, m * P:(m + 1) * P], att_tok[:, m * P:(m + 1) * P], ident)
                last.then_inc(sig("att_turned"), 1)
            st.end()
            place.skip(8 - GATES_FIRST)
            pe_out(pe, place, out_1, 4, 8)
            st.end()
            pe_norm(pe, 1)
            pe.wait_ge(*reached("u_ready", 2 * 2))

            def gate_up(at):
                pe.wait_ge(*reached("pair_evacuated", at.pair + 1))
                multiply_split(pe, split_free, at, columns_by(split_free, bank[at.j // 2 % 3 * 2 + at.j % 2]), halves_of(1))
            for i in range(2 * KD):
                last = pe.matmul(bank[6][:, 3 * i:3 * i + 3], mod_rows[:, i // 2, i % 2 * P:(i % 2 + 1) * P],
                                 ident[0:65, :].rearrange("p (q n) -> p q n", n=32)[:, 0:3, 0], start=True, stop=True)
            last.then_inc(sig("mods_turned"), 1)
            sweep(pe, place, 2 * (DFF // CH), gate_up, linear=False, split=True)
            pe.wait_ge(*reached("pair_evacuated", 3 + DFF // CH))
            pe.wait_ge(*reached("hid_split", HID0))

            def down(at):
                hid = [(ffn_h[:, 2 * at.c + kt, :], ffn_l[:, 2 * at.c + kt, :]) for kt in range(2)]
                multiply_split(pe, split_free, at, rows_by(hid, at.c == 0, at.c == DFF // (2 * P) - 1))
            sweep(pe, place, DFF // (2 * P), down, linear=False, split=True)
            pe.wait_ge(*reached("h_ready", 1))
            pe_norm(pe, 2)
            st.end()
            pe_norm(pe, 3)
            pe.wait_ge(*reached("u_ready", 2 * 3))
            pe.wait_ge(*reached("ba_loaded", 16))
            for half in range(2):
                for k in range(KD):
                    last = pe.matmul(bank[4][0:8, half * S:(half + 1) * S], baw[:, k, half * 8:half * 8 + 8], u[:, k, :], start=(k == 0), stop=(k == KD - 1))
            last.then_inc(sig("ba_multiplied"), 1)
            pe_linear_split(pe, place, 16, split_in_2, 2)
            st.end()
            aside = Aside(place, 2)
            for c in range(CONV_ASIDE):
                at = Chunk(place, c, c, None)
                pe.wait_ge(evacuated, at.linear + 1)
                multiply_split(pe, split_in_2, at, columns_by(split_in_2, bank[2 + at.parity]))
                if c == CONV_ASIDE - 2:
                    pe.wait_ge(*reached("qk_squared", 4))
                    for i in range(2 * GH):
                        last = sum_to_row(pe, bank[0][0:32, 0:S], w4(conv_units[i // 4])[:, i % 4, :], i, 2 * GH)
                    last.then_inc(sig("qk_row_sums"), 1)
            aside.done = CONV_ASIDE * 2 * KD
            st.end()
            for c in range(TB):
                pe.transpose(bank[0][:, c * GH:(c + 1) * GH], gc_rows[:, c * P:(c + 1) * P], ident[0:GH, 0:GH])
                pe.transpose(bank[0][:, 16 + c * GH:16 + (c + 1) * GH], beta_rows[:, c * P:(c + 1) * P], ident[0:GH, 0:GH])
            last = pe.matmul(bank[0][:, 64:72], gc_rows[:, P - 1:P].to_broadcast([GH, P]), ident[0:GH, 0:GH], start=True, stop=True)
            last.then_inc(sig("rows_turned"), 1)
            for c in range(TB):
                for hd in range(GH):
                    last = pe.transpose(bank[4 + 2 * c + hd // 4][:, hd % 4 * P:(hd % 4 + 1) * P], proj[:, T_GV + hd, c * P:(c + 1) * P], ident)
                last.then_inc(sig("gv_turned"), 1)
            for i in range(4):
                for kind in range(3):
                    if i:
                        pe.wait_ge(*reached("spread_used", 4 * (i - 1) + (2 if kind == 0 else 4)))
                    for hh in range(2):
                        hd = 2 * i + hh
                        dst = bank[1 + kind][:, hh * S:(hh + 1) * S]
                        if kind < 2:
                            last = row_to_all(pe, dst, norm_rows[0:16, :], kind * GH + hd, 16)
                        else:
                            last = row_to_all(pe, dst, beta_rows, hd, GH)
                    last.then_inc(sig("spread"), 1)
            pe.wait_ge(*reached("keys_ready", 1))
            pe.wait_ge(*reached("vb_ready", 1))
            for hd in range(GH):
                last = pe.transpose(bank[4 + hd // 4][:, hd % 4 * P:(hd % 4 + 1) * P], proj[:, T_GK + hd, 0:P], ident)
            last.then_inc(sig("gk_turned"), 1)
            st.end()
            for b in range(4):
                ch, h0 = b // 2, 4 * (b % 2)
                tok = slice(ch * P, (ch + 1) * P)
                if b:
                    pe.wait_ge(*reached("g_prods_ready", b))
                    pe.wait_ge(*reached("g_out_copied", b))
                    pe.wait_ge(*reached("g_state_ready", min(b, 2)))
                for i in range(4):
                    last = row_to_all(pe, bank[7][:, i * P:(i + 1) * P], gc_rows[:, tok], h0 + i, GH)
                last.then_inc(sig("gc_spread"), 1)
                for i in range(4):
                    last = pe.matmul(bank[i // 2][:, i % 2 * S:(i % 2 + 1) * S], proj[:, T_GK + h0 + i, tok], kq[:, h0 + i, ch, :, :], start=True, stop=True)
                last.then_inc(sig("g_prods_made"), 1)
                aside.multiply(pe, 16)
                g_solver.pe(pe, 4 + b, lambda lv, wait: aside.multiply(pe, 4))
                pe.wait_ge(*reached("inv_updated", 11 * (5 + b)))
                if ch:
                    pe.wait_ge(*reached("eg_ready", b - 1))
                    pe.wait_ge(*reached("kq_decayed", b - 1))
                    for i in range(4):
                        last = pe.matmul(bank[7][:, i * P:(i + 1) * P], kq[:, h0 + i, ch, 0, :], g_state[:, h0 + i, :], start=True, stop=True)
                    last.then_inc(sig("g_carried"), 1)
                    pe.wait_ge(*reached("g_right", b - 1))
                for i in range(4):
                    rhs = heads4(g_xs)[:, i, :] if ch else vb_tok[:, ch, h0 + i, :]
                    last = pe.matmul(bank[4][:, i * P:(i + 1) * P], heads4(g_inv_t)[:, i, :], rhs, start=True, stop=True)
                last.then_inc(sig("g_solved"), 1)
                pe.wait_ge(*reached("g_new_copied", b + 1))
                new = heads4(g_upd)
                for i in range(4):
                    last = pe.matmul(bank[5][:, i * P:(i + 1) * P], new[:, i, :], g_prods[:, i, 1, :], start=True, stop=(ch == 0))
                    if ch:
                        last = pe.matmul(bank[5][:, i * P:(i + 1) * P], g_state[:, h0 + i, :], kq[:, h0 + i, ch, 1, :], start=False, stop=True)
                last.then_inc(sig("g_out_made"), 1)
                if ch == 0:
                    for i in range(4):
                        last = pe.matmul(bank[6][:, i * P:(i + 1) * P], kd_tok[:, h0 + i, :], new[:, i, :], start=True, stop=True)
                    last.then_inc(sig("g_state_made"), 1)
            place.skip(CONV_ASIDE, split=True)
            place.skip(26 - CONV_ASIDE)
            st.end()
            for c in range(TB):
                for hd in range(DH):
                    n = c * DH + hd
                    last = pe.transpose(bank[2 + n // 4][:, n % 4 * P:(n % 4 + 1) * P], proj[:, T_DV + hd, c * P:(c + 1) * P], ident)
            last.then_inc(sig("d_v_turned"), 1)
            for i in range(NORMED):
                if i % 4 == 0:
                    pe.wait_ge(*reached("head_squared", i // 4 + 1))
                last = sum_to_row(pe, bank[0][0:32, 0:S], w4(i // 4)[:, i % 4, :], i, NORMED)
            last.then_inc(sig("head_sums"), 1)
            pe.wait_ge(*reached("head_inverse", 1))
            for i in range(NORMED // 2):
                if i >= 2:
                    pe.wait_ge(*reached("head_normed", i - 1))
                for hh in range(2):
                    last = row_to_all(pe, bank[i % 2][:, hh * S:(hh + 1) * S], norm_rows, 2 * i + hh, NORMED)
                last.then_inc(sig("head_spread"), 1)
            st.end()

            def dil_scores(i):
                b, slot_ = dil_items[i]
                if i >= 2:
                    pe.wait_ge(*reached("d_logits_ready", i - 1))
                for g in range(3):
                    hd = 4 * g + slot_
                    last = pe.matmul(bank[2 * (i % 2) + g // 2][:, g % 2 * S:g % 2 * S + (b + 1) * P], proj[:, T_DQ + hd, b * P:(b + 1) * P],
                                     proj[:, T_DK + hd, 0:(b + 1) * P], start=True, stop=True)
                last.then_inc(sig("d_scored"), 1)
            dil_scores(0)
            for i, (b, slot_) in enumerate(dil_items):
                if i + 1 < len(dil_items):
                    dil_scores(i + 1)
                pe.wait_ge(*reached("d_probs_made", i + 1))
                if i:
                    pe.wait_ge(*reached("d_probs_t_ready", i))
                for g in range(3):
                    for kb in range(b + 1):
                        last = pe.transpose(bank[4 + g // 2][:, g % 2 * S + kb * P:g % 2 * S + (kb + 1) * P], d_probs[i % 2][:, g, kb * P:(kb + 1) * P], ident)
                last.then_inc(sig("d_probs_turned"), 1)
                pe.wait_ge(*reached("d_probs_t_ready", i + 1))
                if b and slot_ == 0:
                    pe.wait_ge(*reached("d_scaled", b))
                for g in range(3):
                    for kb in range(b + 1):
                        last = pe.matmul(bank[6][:, slot_ * P:(slot_ + 1) * P], d_probs_t[:, g, kb * P:(kb + 1) * P], dv_tok[:, kb, 4 * g + slot_, :],
                                         start=(g == 0 and kb == 0), stop=(g == 2 and kb == b))
                last.then_inc(sig("d_mixed"), 1)
                if slot_ == 3:
                    pe.wait_ge(*reached("d_scaled", b + 1))
                    if b:
                        pe.wait_ge(*reached("y_dil_ready", b))
                    for m in range(4):
                        last = pe.transpose(bank[7][:, m * P:(m + 1) * P], d_tok[:, m * P:(m + 1) * P], ident)
                    last.then_inc(sig("d_turned"), 1)
            st.end()
            pe_out(pe, place, out_2, 2, 10)
            st.end()
            pe_norm(pe, 4)
            pe.wait_ge(*reached("u_ready", 2 * 4))
            pe.wait_ge(*reached("router_loaded", 32))
            for b in range(TB):
                for k in range(KD):
                    last = pe.matmul(bank[0][:, b * EXPERTS:(b + 1) * EXPERTS], u[:, k, b * P:(b + 1) * P], router[:, k, :], start=(k == 0), stop=(k == KD - 1))
            last.then_inc(sig("routed"), 1)

            def into_hidden(at, e, par, kind):
                if kind == 0:
                    pe.wait_ge(*reached("au_free", e + 1))
                multiply_split(pe, split_free, at, columns_by(split_free, bank[4 + 2 * par + kind]),
                               halves_of(3) if isinstance(e, int) and e == 0 else None)

            def from_hidden(at, e, par, first=False, end=False):
                pe.wait_ge(*reached("hid_split", e + (HID0 + 1)))
                hid = [(exp_h[par][:, kt * S:(kt + 1) * S], exp_l[par][:, kt * S:(kt + 1) * S]) for kt in range(2)]
                multiply_split(pe, split_free, at, rows_by(hid, first, end))

            sweep(pe, place, 2, lambda at: into_hidden(at, 0, 0, at.c), linear=False, split=True)

            def turn_combine():
                pe.wait_ge(*reached("combine_ready", 2))
                for b in range(TB):
                    last = pe.transpose(bank[0][0:EXPERTS, b * P:(b + 1) * P], comb_e[:, b, :], ident)
                last.then_inc(sig("combine_turned"), 1)
                pe.wait_ge(*reached("combine_copied", 1))

            def expert_chunk(at):
                x, par = at.third, at.j // 3 % 2
                if at.j % 3 < 2:
                    into_hidden(at, x + 1, 1 - par, at.j % 3)
                else:
                    if isinstance(x, int) and x == 0:
                        turn_combine()
                    from_hidden(at, x, par, first=isinstance(x, int) and x == 0)
            sweep(pe, place, SLOTS, expert_chunk, linear=False, split=True)
            sweep(pe, place, 3 * EXPERTS - SLOTS, lambda at: expert_chunk(later(at)), linear=False, split=True)
            sweep(pe, place, 1, lambda at: from_hidden(at, EXPERTS, EXPERTS % 2, end=True), linear=False, split=True)
            st.end()
            pe.wait_ge(*reached("h_final", 1))
            for b in range(TB):
                for k in range(KD):
                    last = pe.transpose(bank[4 + 2 * b + k // 4][:, k % 4 * P:(k % 4 + 1) * P], h[:, k, b * P:(b + 1) * P], ident)
                last.then_inc(sig("out_turned"), 1)
            st.end()


def kernel(**inputs):
    import concourse.bacc as _bacc
    from concourse.bass_utils import run_bass_kernel_spmd as _run

    nc = _bacc.Bacc("TRN2", target_bir_lowering=False, num_devices=1, dynamic_dma_scratch_size=1024)
    arrays = {f"in_{name}": np.ascontiguousarray(a) for name, a in inputs.items()}
    arrays["in_consts"] = constants()
    args = {name[3:]: nc.dram_tensor(name, a.shape, F32, kind="ExternalInput").ap() for name, a in arrays.items()}
    out = nc.dram_tensor("out", (1, S, D), F32, kind="ExternalOutput").ap()
    build(nc, args, out)
    r = _run(nc, [arrays], core_ids=[0])
    return r.results[0]["out"]
```
